# Optimizing a Trainium2 kernel written in Bass

```python
import functools
import jax, jax.numpy as jnp
from jax import lax
import numpy as np

D_MODEL = 1024
BATCH = 1
SEQ = 1024
DEPTH = 1
DEC_BATCH = 8
DEC_SEQ = 16
PAST_LEN = 128

CHUNK = 64
MIX_WIDTH = D_MODEL
RMS_EPS = 1e-6

R_HEAD_DIM = 64
R_WIDTH = MIX_WIDTH // 2
R_HEADS = R_WIDTH // R_HEAD_DIM
R_DECAY_LORA = 64
R_AAA_LORA = 64
R_GATE_LORA = 160
P_RWKV = 3 * R_WIDTH + R_DECAY_LORA + R_AAA_LORA + R_GATE_LORA
R_SPLITS = (R_WIDTH, 2 * R_WIDTH, 3 * R_WIDTH, 3 * R_WIDTH + R_DECAY_LORA,
            3 * R_WIDTH + R_DECAY_LORA + R_AAA_LORA)
LN_X_EPS = 64e-5
L2_EPS = 1e-12

A_HEAD_DIM = 64
A_WIDTH = MIX_WIDTH - R_WIDTH
A_HEADS = A_WIDTH // A_HEAD_DIM
A_KV_HEADS = 2
A_GROUP = A_HEADS // A_KV_HEADS
A_KV_WIDTH = A_KV_HEADS * A_HEAD_DIM
A_SCALE = A_HEAD_DIM ** -0.5
WINDOW = 128
W_CHUNKS = WINDOW // CHUNK
BAND = (W_CHUNKS + 1) * CHUNK
P_TOTAL = P_RWKV + A_WIDTH + 2 * A_KV_WIDTH

PEER_HEADS = 8
PEER_QDIM = 256
PEER_HALF = PEER_QDIM // 2
N_KEYS = 128
N_EXPERTS = N_KEYS * N_KEYS
PEER_TOPK = 16
PEER_BLOCK = 256

kernel_name = "rwkv7_swa_sink_peer_hybrid_step"

def rms_norm(x, g):
    xf = x.astype(jnp.float32)
    return xf * lax.rsqrt(jnp.mean(xf * xf, axis=-1, keepdims=True) + RMS_EPS) * g.astype(jnp.float32)

def wkv_step(S, inp):
    r, w, k, v, a, b = inp
    sa = jnp.einsum('bhvk,bhk->bhv', S, a)
    S = S * w[:, :, None, :] + sa[..., None] * b[:, :, None, :] + v[..., None] * k[:, :, None, :]
    return S, jnp.einsum('bhvk,bhk->bhv', S, r)

def rwkv7_group(p, shift_prev, wkv_prev, mu, w0, w2, a0, a2, g2, k_k, k_a, r_k, ln_w, ln_b):
    B, L, _ = p.shape
    p_prev = jnp.concatenate([shift_prev.astype(p.dtype), p[:, :-1]], axis=1)
    xs = p + (p_prev - p) * mu
    r, k, v, xw, xa, xg = jnp.split(xs, list(R_SPLITS), axis=-1)
    w = -jax.nn.softplus(-(w0 + jnp.tanh(xw) @ w2)) - 0.5
    decay = jnp.exp(-jnp.exp(w.astype(jnp.float32)))
    a = jax.nn.sigmoid(a0 + xa @ a2)
    g = jax.nn.sigmoid(xg) @ g2
    heads = lambda t: t.astype(jnp.float32).reshape(B, L, R_HEADS, R_HEAD_DIM)
    kk = heads(k * k_k)
    kk = kk / jnp.maximum(jnp.sqrt(jnp.sum(kk * kk, axis=-1, keepdims=True)), L2_EPS)
    k = k * (1.0 + (a - 1.0) * k_a)
    r_h, k_h, v_h, a_h = heads(r), heads(k), heads(v), heads(a)
    seq = tuple(jnp.swapaxes(t, 0, 1) for t in (r_h, heads(decay), k_h, v_h, -kk, kk * a_h))
    wkv_last, y = lax.scan(wkv_step, wkv_prev.astype(jnp.float32), seq)
    y = jnp.swapaxes(y, 0, 1)
    mean = jnp.mean(y, axis=-1, keepdims=True)
    var = jnp.mean(jnp.square(y - mean), axis=-1, keepdims=True)
    y = (y - mean) * lax.rsqrt(var + LN_X_EPS) * ln_w.reshape(R_HEADS, R_HEAD_DIM) \
        + ln_b.reshape(R_HEADS, R_HEAD_DIM)
    y = y + jnp.sum(r_h * k_h * r_k, axis=-1, keepdims=True) * v_h
    return y.reshape(B, L, R_WIDTH) * g, p[:, -1:], wkv_last

def sink_attend(s, v, sinks, valid, out_spec):
    s = s.astype(jnp.float32)
    if valid is not None:
        s = jnp.where(valid, s, -jnp.inf)
    sink = sinks.astype(jnp.float32).reshape(A_KV_HEADS, A_GROUP, 1, 1)
    m = jnp.maximum(jnp.max(s, axis=-1, keepdims=True), sink)
    pr = jnp.exp(s - m)
    denom = jnp.sum(pr, axis=-1, keepdims=True) + jnp.exp(sink - m)
    return jnp.einsum(out_spec, pr / denom, v.astype(jnp.float32))

def swa_group(q, k, v, hist_k, hist_v, sinks, out_g):
    B, L = q.shape[:2]
    q = q.reshape(B, L, A_KV_HEADS, A_GROUP, A_HEAD_DIM) * A_SCALE
    k = k.reshape(B, L, A_KV_HEADS, A_HEAD_DIM)
    v = v.reshape(B, L, A_KV_HEADS, A_HEAD_DIM)
    if hist_k is None:
        nc = L // CHUNK
        qb = q.reshape(B, nc, CHUNK, A_KV_HEADS, A_GROUP, A_HEAD_DIM)
        pad = jnp.zeros((B, WINDOW, A_KV_HEADS, A_HEAD_DIM), k.dtype)
        kp = jnp.concatenate([pad, k], axis=1).reshape(B, nc + W_CHUNKS, CHUNK, A_KV_HEADS, A_HEAD_DIM)
        vp = jnp.concatenate([pad, v], axis=1).reshape(B, nc + W_CHUNKS, CHUNK, A_KV_HEADS, A_HEAD_DIM)
        kb = jnp.concatenate([kp[:, i:i + nc] for i in range(W_CHUNKS + 1)], axis=2)
        vb = jnp.concatenate([vp[:, i:i + nc] for i in range(W_CHUNKS + 1)], axis=2)
        s = jnp.einsum('bcqhgd,bckhd->bchgqk', qb, kb)
        key_chunk = jnp.arange(nc)[:, None] - W_CHUNKS + jnp.arange(BAND)[None, :] // CHUNK
        valid = (key_chunk >= 0).reshape(1, nc, 1, 1, 1, BAND)
        o = sink_attend(s, vb, sinks, valid, 'bchgqk,bckhd->bcqhgd')
        o = o.reshape(B, L, A_KV_HEADS, A_GROUP, A_HEAD_DIM)
        new_k, new_v = k[:, -WINDOW:], v[:, -WINDOW:]
    else:
        kc = jnp.concatenate([hist_k.astype(k.dtype), k], axis=1)
        vc = jnp.concatenate([hist_v.astype(v.dtype), v], axis=1)
        s = jnp.einsum('bqhgd,bkhd->bhgqk', q, kc)
        o = sink_attend(s, vc, sinks, None, 'bhgqk,bkhd->bqhgd')
        rows = hist_k.shape[1]
        new_k, new_v = kc[:, -rows:], vc[:, -rows:]
    o = o * lax.rsqrt(jnp.mean(o * o, axis=-1, keepdims=True) + RMS_EPS) \
        * out_g.astype(jnp.float32).reshape(A_KV_HEADS, A_GROUP, A_HEAD_DIM)
    return o.reshape(B, L, A_WIDTH), new_k, new_v

def peer_block(t, w_q, key1, key2, down, up):
    T = t.shape[0]
    q = (t @ w_q).astype(jnp.float32).reshape(T, PEER_HEADS, 2, PEER_HALF)
    s1 = jnp.einsum('thd,nd->thn', q[:, :, 0], key1.astype(jnp.float32))
    s2 = jnp.einsum('thd,nd->thn', q[:, :, 1], key2.astype(jnp.float32))
    v1, i1 = lax.top_k(s1, PEER_TOPK)
    v2, i2 = lax.top_k(s2, PEER_TOPK)
    cand_s = (v1[..., :, None] + v2[..., None, :]).reshape(T, PEER_HEADS, PEER_TOPK * PEER_TOPK)
    cand_i = (i1[..., :, None] * N_KEYS + i2[..., None, :]).reshape(T, PEER_HEADS, PEER_TOPK * PEER_TOPK)
    best_s, pos = lax.top_k(cand_s, PEER_TOPK)
    expert = jnp.take_along_axis(cand_i, pos, axis=-1)
    gate = jax.nn.softmax(best_s, axis=-1)
    u = jnp.take(down, expert, axis=0)
    act = jax.nn.gelu(jnp.einsum('thed,td->the', u, t), approximate=False)
    vv = jnp.take(up, expert, axis=0)
    return jnp.einsum('the,thed->td', gate * act, vv)

def peer_ffn(h, w_q, key1, key2, down, up):
    lead = h.shape[:-1]
    t = h.reshape(-1, D_MODEL)
    n = t.shape[0]
    blk = min(PEER_BLOCK, n)
    nb = -(-n // blk)
    t = jnp.pad(t, ((0, nb * blk - n), (0, 0))).reshape(nb, blk, D_MODEL)
    out = lax.map(lambda tb: peer_block(tb, w_q, key1, key2, down, up), t)
    return out.reshape(nb * blk, D_MODEL)[:n].reshape(*lead, D_MODEL)

def trunk_layer(x, shift_prev, wkv_prev, hist_k, hist_v, norm_mix_g, w_in, rwkv_mu, rwkv_w0, rwkv_w2,
                rwkv_a0, rwkv_a2, rwkv_g2, rwkv_k_k, rwkv_k_a, rwkv_r_k, rwkv_ln_w, rwkv_ln_b,
                attn_sinks, attn_out_g, w_out, norm_ffn_g, peer_w_q, peer_key1, peer_key2,
                peer_down, peer_up):
    h = rms_norm(x, norm_mix_g)
    proj = h @ w_in
    p_r = proj[..., :P_RWKV]
    q = proj[..., P_RWKV:P_RWKV + A_WIDTH]
    k = proj[..., P_RWKV + A_WIDTH:P_RWKV + A_WIDTH + A_KV_WIDTH]
    v = proj[..., P_RWKV + A_WIDTH + A_KV_WIDTH:]
    y_r, new_shift, new_wkv = rwkv7_group(p_r, shift_prev, wkv_prev, rwkv_mu, rwkv_w0, rwkv_w2,
                                          rwkv_a0, rwkv_a2, rwkv_g2, rwkv_k_k, rwkv_k_a, rwkv_r_k,
                                          rwkv_ln_w, rwkv_ln_b)
    y_a, new_k, new_v = swa_group(q, k, v, hist_k, hist_v, attn_sinks, attn_out_g)
    x = x + jnp.concatenate([y_r, y_a], axis=-1) @ w_out
    x = x + peer_ffn(rms_norm(x, norm_ffn_g), peer_w_q, peer_key1, peer_key2, peer_down, peer_up)
    return x, new_shift, new_wkv, new_k, new_v

def setup_inputs(seed: int = 0) -> dict:
    key = jax.random.key(seed)
    ks = jax.random.split(key, 32)
    nrm = lambda k, shape, s=1.0: s * jax.random.normal(k, shape, jnp.float32)
    unif = lambda k, shape, lo, hi: jax.random.uniform(k, shape, jnp.float32, lo, hi)
    win_rows = min(WINDOW, PAST_LEN)
    return {
        "x_prompt": nrm(ks[0], (BATCH, SEQ, D_MODEL)),
        "x_sample": nrm(ks[1], (DEC_BATCH, DEC_SEQ, D_MODEL)),
        "state_rwkv_shift": nrm(ks[2], (DEPTH, DEC_BATCH, 1, P_RWKV)),
        "state_rwkv_wkv": nrm(ks[3], (DEPTH, DEC_BATCH, R_HEADS, R_HEAD_DIM, R_HEAD_DIM), 0.3),
        "cache_swa_k": nrm(ks[4], (DEPTH, DEC_BATCH, win_rows, A_KV_HEADS, A_HEAD_DIM)),
        "cache_swa_v": nrm(ks[5], (DEPTH, DEC_BATCH, win_rows, A_KV_HEADS, A_HEAD_DIM)),
        "norm_mix_g": 1.0 + nrm(ks[6], (DEPTH, D_MODEL), 0.02),
        "w_in": nrm(ks[7], (DEPTH, D_MODEL, P_TOTAL), D_MODEL ** -0.5),
        "rwkv_mu": unif(ks[8], (DEPTH, P_RWKV), 0.0, 1.0),
        "rwkv_w0": unif(ks[9], (DEPTH, R_WIDTH), -6.0, -1.0),
        "rwkv_w2": nrm(ks[10], (DEPTH, R_DECAY_LORA, R_WIDTH), 0.5 * R_DECAY_LORA ** -0.5),
        "rwkv_a0": nrm(ks[11], (DEPTH, R_WIDTH), 0.1),
        "rwkv_a2": nrm(ks[12], (DEPTH, R_AAA_LORA, R_WIDTH), 0.5 * R_AAA_LORA ** -0.5),
        "rwkv_g2": nrm(ks[13], (DEPTH, R_GATE_LORA, R_WIDTH), R_GATE_LORA ** -0.5),
        "rwkv_k_k": 0.85 + nrm(ks[14], (DEPTH, R_WIDTH), 0.05),
        "rwkv_k_a": 1.0 + nrm(ks[15], (DEPTH, R_WIDTH), 0.05),
        "rwkv_r_k": nrm(ks[16], (DEPTH, R_HEADS, R_HEAD_DIM), 0.1),
        "rwkv_ln_w": 1.0 + nrm(ks[17], (DEPTH, R_WIDTH), 0.02),
        "rwkv_ln_b": nrm(ks[18], (DEPTH, R_WIDTH), 0.02),
        "attn_sinks": nrm(ks[19], (DEPTH, A_HEADS), 0.5),
        "attn_out_g": 1.0 + nrm(ks[20], (DEPTH, A_WIDTH), 0.02),
        "w_out": nrm(ks[21], (DEPTH, MIX_WIDTH, D_MODEL), MIX_WIDTH ** -0.5),
        "norm_ffn_g": 1.0 + nrm(ks[22], (DEPTH, D_MODEL), 0.02),
        "peer_w_q": nrm(ks[23], (DEPTH, D_MODEL, PEER_HEADS * PEER_QDIM), D_MODEL ** -0.5),
        "peer_key1": nrm(ks[24], (DEPTH, N_KEYS, PEER_HALF), PEER_HALF ** -0.5),
        "peer_key2": nrm(ks[25], (DEPTH, N_KEYS, PEER_HALF), PEER_HALF ** -0.5),
        "peer_down": nrm(ks[26], (DEPTH, N_EXPERTS, D_MODEL), D_MODEL ** -0.5),
        "peer_up": nrm(ks[27], (DEPTH, N_EXPERTS, D_MODEL), 0.5),
        "norm_final_g": 1.0 + nrm(ks[28], (D_MODEL,), 0.02),
    }

def reference(x_prompt, x_sample, state_rwkv_shift, state_rwkv_wkv, cache_swa_k, cache_swa_v,
              norm_mix_g, w_in, rwkv_mu, rwkv_w0, rwkv_w2, rwkv_a0, rwkv_a2, rwkv_g2, rwkv_k_k,
              rwkv_k_a, rwkv_r_k, rwkv_ln_w, rwkv_ln_b, attn_sinks, attn_out_g, w_out, norm_ffn_g,
              peer_w_q, peer_key1, peer_key2, peer_down, peer_up, norm_final_g):
    hp, hs = x_prompt, x_sample
    b_p = x_prompt.shape[0]
    sp_l, wp_l, kp_l, vp_l = [], [], [], []
    ss_l, ws_l, ks_l, vs_l = [], [], [], []
    for l in range(DEPTH):
        lp = dict(norm_mix_g=norm_mix_g[l], w_in=w_in[l], rwkv_mu=rwkv_mu[l], rwkv_w0=rwkv_w0[l],
                  rwkv_w2=rwkv_w2[l], rwkv_a0=rwkv_a0[l], rwkv_a2=rwkv_a2[l], rwkv_g2=rwkv_g2[l],
                  rwkv_k_k=rwkv_k_k[l], rwkv_k_a=rwkv_k_a[l], rwkv_r_k=rwkv_r_k[l],
                  rwkv_ln_w=rwkv_ln_w[l], rwkv_ln_b=rwkv_ln_b[l], attn_sinks=attn_sinks[l],
                  attn_out_g=attn_out_g[l], w_out=w_out[l], norm_ffn_g=norm_ffn_g[l],
                  peer_w_q=peer_w_q[l], peer_key1=peer_key1[l], peer_key2=peer_key2[l],
                  peer_down=peer_down[l], peer_up=peer_up[l])
        zero_shift = jnp.zeros((b_p, 1, P_RWKV), jnp.float32)
        zero_wkv = jnp.zeros((b_p, R_HEADS, R_HEAD_DIM, R_HEAD_DIM), jnp.float32)
        hp, sp, wp, kp, vp = trunk_layer(hp, zero_shift, zero_wkv, None, None, **lp)
        hs, ss, ws, kss, vss = trunk_layer(hs, state_rwkv_shift[l], state_rwkv_wkv[l],
                                           cache_swa_k[l], cache_swa_v[l], **lp)
        sp_l.append(sp); wp_l.append(wp); kp_l.append(kp); vp_l.append(vp)
        ss_l.append(ss); ws_l.append(ws); ks_l.append(kss); vs_l.append(vss)
    y_prompt = rms_norm(hp, norm_final_g)
    y_sample = rms_norm(hs, norm_final_g)
    new_shift_prompt = jnp.stack(sp_l)
    new_wkv_prompt = jnp.stack(wp_l)
    new_k_prompt = jnp.stack(kp_l)
    new_v_prompt = jnp.stack(vp_l)
    new_shift_sample = jnp.stack(ss_l)
    new_wkv_sample = jnp.stack(ws_l)
    new_k_sample = jnp.stack(ks_l)
    new_v_sample = jnp.stack(vs_l)
    return (y_prompt, y_sample, new_shift_prompt, new_wkv_prompt, new_k_prompt, new_v_prompt,
            new_shift_sample, new_wkv_sample, new_k_sample, new_v_sample)


_drawn_inputs = setup_inputs


def setup_inputs(seed=0):
    import zlib

    import numpy as np

    out = dict(_drawn_inputs(seed))
    spreads = {}
    factors = {'rwkv_ln_w': 3.267, 'rwkv_ln_b': 3.266, 'attn_sinks': 8.0, 'norm_final_g': 2.744}
    for name, (base, spread) in spreads.items():
        noise = np.random.default_rng([zlib.crc32(name.encode()), seed]).standard_normal(out[name].shape)
        drawn = base * np.exp(spread * noise) if base else spread * noise
        out[name] = __import__('jax').numpy.asarray(drawn.astype(out[name].dtype))
    for name, factor in factors.items():
        out[name] = (out[name] * factor).astype(out[name].dtype)
    return out
```

```python
import math
from contextlib import ExitStack

import numpy as np

import concourse.bass as bass
from concourse import mybir

F32 = mybir.dt.float32
U32 = mybir.dt.uint32
ALU = mybir.AluOpType
ACT = mybir.ActivationFunctionType
AX = mybir.AxisListType

P = 128
D = 1024
SEQ = 1024
SAMPLES, STEPS = 8, 16
TOKENS = SEQ + SAMPLES * STEPS
TILES = TOKENS // P
PROMPT_TILES = SEQ // P
HEADS, HD = 8, 64
RW = HEADS * HD
LORA = 64
GLORA = 160
P_RWKV = 3 * RW + 2 * LORA + GLORA
Q0, K0, V0 = P_RWKV, P_RWKV + RW, P_RWKV + RW + 128
P_TOTAL = V0 + 128
KC = D // P
PAIRS = HEADS // 2
RMS_EPS = 1e-6
LN_EPS = 64e-5
L2_EPS = 1e-12
SCALE = HD ** -0.5
PGROUPS = 6
PG = P_TOTAL // PGROUPS
EXPERTS = 128 * 128
TOPK = 16
SLOTS = 8 * TOPK
TRI_I, TRI_X, TRI_S, IND, MASK2, MASKN, RC_COLS = 0, 128, 256, 384, 392, 648, 776
MU, W0A0, KKC, KAC, RKC, LNW, LNB, OUTG, SINK = 0, 1824, 2848, 3360, 3872, 4384, 4896, 5408, 5920
BC_COLS = 5928
NEG = -1e30


DVE_LINKS = 59
ALL_CONSTS = 16 * 19


class Signal:

    def __init__(self, ctx, nc, name, per=1):
        self.sem, self.per = ctx.enter_context(nc.semaphore(name)), per

    def due(self, t, k):
        return t * self.per + k


class Link:

    def __init__(self, eng, ended, t):
        self.eng, self.ended, self.t, self.n = eng, ended, t, 0

    def __call__(self, ins):
        self.n += 1
        ins.then_inc(self.ended.sem, 1)
        self.eng.wait_ge(self.ended.sem, self.ended.due(self.t, self.n))

    def hold(self, ins, passed):
        self.n += 1
        ins.then_inc(self.ended.sem, 1)
        self.eng.wait_ge(self.ended.sem, self.ended.due(self.t, self.n)).then_inc(passed.sem, 1)

    def close(self):
        assert self.n == self.ended.per, (self.ended.sem, self.n, self.ended.per)


def row(vec):
    return vec.rearrange("(a n) -> a n", a=1)


def project(nc, A):
    with ExitStack() as ctx:
        def sb(name, shape, dt=F32):
            return ctx.enter_context(nc.sbuf_tensor("pj_" + name, shape, dt))

        def signal(name, per=1):
            return Signal(ctx, nc, name, per)

        w = sb("w_in_sb", [P, KC, P_TOTAL])
        gain = sb("gain_col", [P, KC])
        ident = sb("ident_a", [P, P])
        x = sb("x_in", [P, 2, D])
        junk = sb("squares", [P, D])
        ssq = sb("ssq_a", [P, 2])
        rstd = sb("rstd_a", [P, 2])
        hT = sb("hT", [P, 2, KC, P])
        pbuf = sb("proj_sb", [P, 2, P_TOTAL])
        psT = ctx.enter_context(nc.psum_tensor("psT", [P, KC, P], F32))
        psP = ctx.enter_context(nc.psum_tensor("psP", [P, PGROUPS, 512], F32))

        w_in_loaded = signal("w_in_loaded")
        const_loaded = signal("const_a_loaded")
        x_loaded = [signal("x_loaded0", 16), signal("x_loaded1", 16)]
        squared = signal("squared")
        transposed = signal("transposed")
        std_ready = signal("std_ready")
        var_ready = signal("var_ready")
        rstd_ready = signal("rstd_ready")
        hT_ready = signal("hT_ready", 2)
        proj_done = signal("proj_done", PGROUPS)
        act_evac = signal("act_evac", 3)
        dve_evac = signal("dve_evac", 3)
        stored = [signal("proj_stored0", 16), signal("proj_stored1", 16)]
        zeroed = signal("zeroed")

        out = A["proj"]

        block = ctx.enter_context(nc.Block())

        @block.sync
        def _(sp):
            sp.dma_start(ident[:, :], A["ident"]).then_inc(const_loaded.sem, 16)
            sp.dma_start(gain[:, :], A["norm_mix_col"]).then_inc(const_loaded.sem, 16)

            def load(t, par, n):
                sp.wait_ge(squared.sem, t + 1)
                sp.wait_ge(transposed.sem, t + 1)
                sp.dma_start(x[:, par, :], A["x"][bass.ds(t * P, P), :]).then_inc(x_loaded[par].sem, 16)

            load(0, 0, 0)
            load(1, 1, 0)
            for k in range(KC):
                sp.dma_start(w[:, k, :], A["w_in"][k * P:(k + 1) * P, :]).then_inc(w_in_loaded.sem, 16)
            with sp.Fori(1, TILES // 2) as u:
                load(2 * u, 0, u)
                load(2 * u + 1, 1, u)
            load(TILES - 1, 0, 0)
            sp.wait_ge(zeroed.sem, 1)
            sp.dma_start(out[0:P, :], pbuf[:, 1, :]).then_inc(zeroed.sem, 16)
            sp.wait_ge(zeroed.sem, 17)
            sp.wait_ge(stored[0].sem, 16 * (1 + 5))
            sp.wait_ge(stored[1].sem, 16 * (1 + 4))

        @block.scalar
        def _(act):
            act.sem_inc(squared.sem, 2)
            act.sem_inc(act_evac.sem, 3)
            act.sem_inc(stored[0].sem, 16)
            act.sem_inc(stored[1].sem, 16)

            def square(t, par, u):
                act.wait_ge(x_loaded[par].sem, 16 * u + 16)
                act.wait_ge(squared.sem, t + 2)
                act.activation(junk[:, :], x[:, par, :], ACT.Square,
                               accum_out=ssq[:, par:par + 1]).then_inc(squared.sem, 1)
                act.wait_ge(var_ready.sem, t + 1)
                act.activation(rstd[:, par:par + 1], ssq[:, par:par + 1], ACT.Sqrt).then_inc(std_ready.sem, 1)

            def evacuate(t, par, u):
                act.wait_ge(rstd_ready.sem, t + 1)
                act.wait_ge(stored[par].sem, 16 * u + 16)
                for g in range(0, PGROUPS, 2):
                    act.wait_ge(proj_done.sem, 12 + 6 * t + g + 1)
                    act.activation(pbuf[:, par, g * PG:(g + 1) * PG], psP[:, g, 0:PG], ACT.Copy,
                                   scale=rstd[:, par:par + 1]).then_inc(act_evac.sem, 1)
                act.wait_ge(act_evac.sem, 3 * t + 6)
                act.wait_ge(dve_evac.sem, 3 * t + 6)
                act.dma_start(out[bass.ds(P + t * P, P), :], pbuf[:, par, :]).then_inc(stored[par].sem, 16)

            square(0, 0, 0)
            with act.Fori(0, TILES // 2) as u:
                square(2 * u + 1, 1, u)
                evacuate(2 * u, 0, u)
                square(2 * u + 2, 0, u + 1)
                evacuate(2 * u + 1, 1, u)
            evacuate(TILES - 1, 0, TILES // 2)

        @block.vector
        def _(dve):
            dve.sem_inc(dve_evac.sem, 3)
            dve.wait_ge(const_loaded.sem, 32)

            def normalise(t, par, u):
                dve.wait_ge(squared.sem, t + 3)
                dve.tensor_scalar(ssq[:, par:par + 1], ssq[:, par:par + 1], 1.0 / D, RMS_EPS,
                                  ALU.mult, ALU.add).then_inc(var_ready.sem, 1)
                dve.wait_ge(transposed.sem, t + 3)
                dve.wait_ge(proj_done.sem, 6 * t + 6)
                for k in range(0, KC, 4):
                    dve.tensor_tensor(hT[:, par, k:k + 4, :], psT[:, k:k + 4, :],
                                      gain[:, k:k + 4].unsqueeze(2).to_broadcast([P, 4, P]),
                                      ALU.mult).then_inc(hT_ready.sem, 1)
                dve.wait_ge(std_ready.sem, t + 1)
                dve.reciprocal(rstd[:, par:par + 1], rstd[:, par:par + 1]).then_inc(rstd_ready.sem, 1)

            def evacuate(t, par, u):
                dve.wait_ge(rstd_ready.sem, t + 1)
                dve.wait_ge(stored[par].sem, 16 * u + 16)
                for g in range(1, PGROUPS, 2):
                    dve.wait_ge(proj_done.sem, 12 + 6 * t + g + 1)
                    dve.tensor_scalar(pbuf[:, par, g * PG:(g + 1) * PG], psP[:, g, 0:PG],
                                      rstd[:, par:par + 1], None, ALU.mult).then_inc(dve_evac.sem, 1)

            normalise(0, 0, 0)
            with dve.Fori(0, TILES // 2) as u:
                normalise(2 * u + 1, 1, u)
                evacuate(2 * u, 0, u)
                normalise(2 * u + 2, 0, u + 1)
                evacuate(2 * u + 1, 1, u)
            evacuate(TILES - 1, 0, TILES // 2)
            dve.wait_ge(stored[1].sem, 16 * 5)
            dve.memset(pbuf[:, 1, :], 0.0).then_inc(zeroed.sem, 1)

        @block.tensor
        def _(pe):
            pe.sem_inc(transposed.sem, 2)
            pe.sem_inc(proj_done.sem, 12)
            pe.wait_ge(const_loaded.sem, 32)

            def transposes(t, par, u, first=False):
                pe.wait_ge(x_loaded[par].sem, 16 * u + 16)
                if not first:
                    pe.wait_ge(hT_ready.sem, 2 * t)
                for k in range(KC):
                    last = pe.transpose(psT[:, k, :], x[:, par, k * P:(k + 1) * P], ident[:, :])
                last.then_inc(transposed.sem, 1)

            def products(t, par, u):
                pe.wait_ge(hT_ready.sem, 2 * t + 2)
                for g in range(PGROUPS):
                    pe.wait_ge((dve_evac if g % 2 else act_evac).sem, 3 * t + g // 2 + 1)
                    for k in range(KC):
                        last = pe.matmul(psP[:, g, 0:PG], hT[:, par, k, :], w[:, k, g * PG:(g + 1) * PG],
                                         start=k == 0, stop=k == KC - 1)
                    last.then_inc(proj_done.sem, 1)

            transposes(0, 0, 0, True)
            pe.wait_ge(w_in_loaded.sem, 16 * KC)
            with pe.Fori(0, TILES // 2) as u:
                transposes(2 * u + 1, 1, u)
                products(2 * u, 0, u)
                transposes(2 * u + 2, 0, u + 1)
                products(2 * u + 1, 1, u)
            products(TILES - 1, 0, TILES // 2)


def mix(nc, A):
    with ExitStack() as ctx:
        def sb(name, shape, dt=F32):
            return ctx.enter_context(nc.sbuf_tensor("mx_" + name, shape, dt))

        def signal(name, per=1):
            return Signal(ctx, nc, name, per)

        NKS = SAMPLES + 1
        ident = sb("ident_m", [P, P])
        ident2 = sb("ident2", [P, HD])
        rc = sb("rc", [P, 2, RC_COLS])
        rowm = sb("row_mask", [P, 2])
        colm = sb("col_mask", [P, 2, P])
        bc = sb("bc", [P, BC_COLS])
        w2a2 = sb("w2a2", [P, 2 * RW])
        g2a = sb("g2a", [P, RW])
        g2b = sb("g2b", [GLORA - P, RW])

        p_cur = sb("p_cur", [P, P_TOTAL])
        xs = sb("xs", [P, P_RWKV])
        kv = sb("kv", [P, NKS, 256])
        amask = sb("amask", [P, NKS * P])
        lora = sb("lora", [P, 2 * LORA + GLORA])
        loraT = sb("loraT", [P, 3 * P])
        sa = sb("sa", [P, 2, RW])
        gate = sb("gate_g", [P, RW])
        ex = sb("ex", [P, 4, RW])
        pc = sb("pc", [P, PAIRS, 8])
        kk = sb("kk", [P, RW])
        k2 = sb("k2", [P, RW])
        work = sb("work", [P, RW])
        work2 = sb("work2", [P, RW])
        small = sb("small", [P, 8, HEADS])
        bonus = sb("bonus", [P, HEADS])
        fac = sb("fac", [P, 4, RW])
        bk = sb("bk", [P, 2, 2, RW])
        arT = sb("arT", [P, PAIRS, 2 * P])
        bT = sb("bT", [P, PAIRS, P])
        kT = sb("kT", [P, PAIRS, P])
        pqb = sb("pqb", [P, 2, PAIRS, 2 * P])
        pqk = sb("pqk", [P, 2, PAIRS, 2 * P])
        pw = sb("powers", [P, 2, HEADS, P])
        pwT = sb("powersT", [P, 2, HEADS, P])
        X = sb("X", [P, HEADS, P])
        rpT = sb("rpT", [P, 2, PAIRS, P])
        y = sb("y", [P, RW])
        pcd = sb("pcd", [P, 2, PAIRS, HD])
        G = sb("G", [P, 4, PAIRS, P])
        H = sb("H", [P, 4, PAIRS, P])
        S = sb("S", [P, PAIRS, P])
        S2 = sb("S2", [P, PAIRS, P])
        cat = sb("cat", [P, D])
        qT = sb("qT", [P, PAIRS, P])
        keyT = sb("keyT", [P, NKS * P])
        sc = sb("sc", [P, NKS * P])
        prT = sb("prT", [P, NKS * P])
        ast = sb("ast", [P, 8, HEADS])
        ps = ctx.enter_context(nc.psum_tensor("ps_m", [P, 8, 512], F32))

        v_of = lambda h: xs[:, 2 * RW + h * HD:2 * RW + (h + 1) * HD]
        heads_oP = lambda ap: ap.rearrange("p (q o c) -> p o q c", o=2, c=HD)

        consts = signal("mix_consts")
        tile_end = signal("mix_tile_end", 5)
        p_in = signal("p_in", 16)
        prev_in = signal("prev_in", 16)
        prev_fix = signal("prev_fix")
        kv_in = signal("kv_in", 16)
        kv_in2 = signal("kv_in2")
        mask_in = signal("mask_in", 16)
        xs_ready = signal("xs_ready")
        lora_in = signal("lora_in")
        loraT_out = signal("loraT_out")
        loraT_ready = signal("loraT_ready")
        lora_out = signal("lora_out", 2)
        pre_ready = signal("pre_ready")
        sig_ready = signal("sig_ready")
        gate_ready = signal("gate_ready")
        cum_done = signal("cum_done")
        exps_ready = signal("exps_ready", 5)
        kk_ss = signal("kk_ss")
        kk_norm = signal("kk_norm")
        factors = signal("factors", 6)
        facT_out = signal("facT_out", 4)
        facT_ready = signal("facT_ready", 4)
        pb_out = signal("pb_out")
        pk_out = signal("pk_out")
        pqb_ready = signal("pqb_ready", 2)
        pqk_ready = signal("pqk_ready", 2)
        n_out = signal("n_out")
        w0_out = signal("w0_out")
        n_ready = signal("n_ready")
        x0_ready = signal("x0_ready")
        sq_out = signal("sq_out", 4)
        sq_ready = signal("sq_ready", 4)
        ap_out = signal("ap_out", 5)
        x_ready = signal("x_ready", 5)
        rp_out = signal("rp_out")
        y0_out = signal("y0_out")
        rp_ready = signal("rp_ready")
        y0_ready = signal("y0_ready")
        gh_out = signal("gh_out", 4)
        pcd_ready = signal("pcd_ready", 4)
        g_ready = signal("g_ready", 4)
        h_ready = signal("h_ready", 4)
        st_out = signal("st_out", 4)
        s_ready = signal("s_ready", 4)
        s_loaded = signal("s_loaded")
        s_stored = signal("s_stored")
        gn_var = signal("gn_var")
        gn_std = signal("gn_std")
        y_done = signal("y_done")
        qkT_out = signal("qkT_out")
        qkT_ready = signal("qkT_ready")
        sc_out = signal("sc_out", 8)
        max_ready = signal("max_ready", 8)
        pr_ready = signal("pr_ready", 8)
        prT_out = signal("prT_out", 8)
        prT_ready = signal("prT_ready", 8)
        o_out = signal("o_out", 8)
        sink_in = signal("sink_in")
        sink_exp = signal("sink_exp")
        o_var = signal("o_var")
        o_std = signal("o_std")
        cat_ready = signal("cat_ready")
        cat_stored = signal("cat_stored", 16)
        dve_link = signal("mix_dve_link", DVE_LINKS)
        dve_start = signal("mix_dve_start")

        proj = A["proj"]
        T8 = PROMPT_TILES

        def sync_tile(sp, t, sample):
            sp.wait_ge(tile_end.sem, tile_end.due(t, 5))
            sp.dma_start(p_cur[:, :], proj[bass.ds(P + t * P, P), :]).then_inc(p_in.sem, 16)
            sp.dma_start(xs[:, :], proj[bass.ds(P - 1 + t * P, P), 0:P_RWKV]).then_inc(prev_in.sem, 16)
            if sample:
                sp.wait_ge(prev_in.sem, prev_in.due(t, 16))
                sp.dma_start(xs[0:P:STEPS, :], A["state_shift"]).then_inc(prev_fix.sem, 16)
                for b in range(SAMPLES):
                    sp.dma_start(kv[:, b, 0:P], A["cache_k"][b]).then_inc(kv_in2.sem, 16)
                    sp.dma_start(kv[:, b, P:2 * P], A["cache_v"][b]).then_inc(kv_in2.sem, 16)
                sp.dma_start(kv[:, SAMPLES, :], proj[bass.ds(P + t * P, P), K0:P_TOTAL]).then_inc(kv_in.sem, 16)
                sp.dma_start(amask[:, :], A["mask_sample"]).then_inc(mask_in.sem, 16)
            else:
                sp.dma_start(kv[:, 0:2, :], proj[bass.ds(t * P, 2 * P), K0:P_TOTAL]
                             .rearrange("(n p) c -> p n c", p=P)).then_inc(kv_in.sem, 16)
                sp.dma_start(amask[:, 0:2 * P], A["mask_prompt"][bass.ds(t * P, P), :]).then_inc(mask_in.sem, 16)
            if sample:
                for n in range(SAMPLES):
                    b = 2 * (n % 4) + n // 4
                    sp.wait_ge(s_stored.sem, 32 * n + 32)
                    for o in range(2):
                        sp.dma_start(S[o * HD:(o + 1) * HD, :, o * HD:(o + 1) * HD],
                                     A["state_wkvT"][b, o]).then_inc(s_loaded.sem, 16)
                    sp.wait_ge(s_ready.sem, s_ready.due(t, n + 1))
                    for o in range(2):
                        sp.dma_start(A["wkvT_sample"][b, o],
                                     S2[o * HD:(o + 1) * HD, :, o * HD:(o + 1) * HD]).then_inc(s_stored.sem, 16)
            sp.wait_ge(cat_ready.sem, cat_ready.due(t, 1))
            sp.dma_start(A["mixed"][bass.ds(t * P, P), :], cat[:, :]).then_inc(cat_stored.sem, 16)
            sp.wait_ge(cat_stored.sem, cat_stored.due(t, 16))
            sp.sem_inc(tile_end.sem, 1)

        def scalar_tile(act, t, sample):
            act.wait_ge(tile_end.sem, tile_end.due(t, 5))
            act.wait_ge(xs_ready.sem, xs_ready.due(t, 1))
            act.activation(lora[:, 0:LORA], xs[:, 3 * RW:3 * RW + LORA], ACT.Tanh)
            act.activation(lora[:, LORA:2 * LORA], xs[:, 3 * RW + LORA:3 * RW + 2 * LORA], ACT.Copy)
            act.activation(lora[:, 2 * LORA:], xs[:, 3 * RW + 2 * LORA:P_RWKV], ACT.Sigmoid)\
               .then_inc(lora_in.sem, 1)
            act.wait_ge(loraT_out.sem, loraT_out.due(t, 1))
            act.activation(loraT[:, 0:2 * P], ps[:, 0, 0:2 * P], ACT.Copy)
            act.activation(loraT[0:GLORA - P, 2 * P:3 * P], ps[0:GLORA - P, 0, 2 * P:3 * P], ACT.Copy)\
               .then_inc(loraT_ready.sem, 1)
            act.wait_ge(pre_ready.sem, pre_ready.due(t, 1))
            act.activation(sa[:, :, :], sa[:, :, :], ACT.Sigmoid).then_inc(sig_ready.sem, 1)
            act.wait_ge(lora_out.sem, lora_out.due(t, 2))
            act.activation(gate[:, :], ps[:, 3, :], ACT.Copy).then_inc(gate_ready.sem, 1)
            act.wait_ge(kk_ss.sem, kk_ss.due(t, 1))
            act.activation(small[:, 1, :], small[:, 0, :], ACT.Sqrt).then_inc(kk_norm.sem, 1)
            act.wait_ge(cum_done.sem, cum_done.due(t, 1))
            act.activation(ex[:, 1, :], ps[:, 5, :], ACT.Exp).then_inc(exps_ready.sem, 1)
            act.activation(ex[:, 2, :], ps[:, 4, :], ACT.Exp, scale=-1.0).then_inc(exps_ready.sem, 1)
            act.activation(ex[:, 0, :], ps[:, 4, :], ACT.Exp).then_inc(exps_ready.sem, 1)
            act.activation(ex[:, 3, :], ps[:, 6, :], ACT.Exp).then_inc(exps_ready.sem, 1)
            act.activation(pc[:, :, :], ps[:, 7, 0:32].rearrange("p (a n) -> p a n", n=8), ACT.Exp)\
               .then_inc(exps_ready.sem, 1)
            for n, dst in enumerate((arT[:, :, 0:P], arT[:, :, P:2 * P], bT[:, :, :], kT[:, :, :])):
                act.wait_ge(facT_out.sem, facT_out.due(t, n + 1))
                act.activation(dst, ps[:, n, :].rearrange("p (a n) -> p a n", n=P), ACT.Copy)\
                   .then_inc(facT_ready.sem, 1)
            act.wait_ge(factors.sem, factors.due(t, 1))
            for o in range(2):
                act.activation(X[:, 4 * o:4 * o + 4, 0:HD],
                               fac[:, 0, :].rearrange("p (q o c) -> p o q c", o=2, c=HD)[:, o], ACT.Copy)
            act.wait_ge(w0_out.sem, w0_out.due(t, 1))
            act.activation(X[:, :, HD:P], ps[:, 6, :].rearrange("p (h c) -> p h c", c=HD), ACT.Copy)\
               .then_inc(x0_ready.sem, 1)
            for i in range(4):
                act.wait_ge(sq_out.sem, sq_out.due(t, i + 1))
                if i:
                    act.wait_ge(ap_out.sem, ap_out.due(t, i))
                act.activation(pwT[:, i % 2, :, :], ps[:, 2:4, :].rearrange("p b (h c) -> p (b h) c", c=P), ACT.Copy)
                act.activation(pw[:, (i + 1) % 2, :, :], ps[:, 4:6, :].rearrange("p b (h c) -> p (b h) c", c=P),
                               ACT.Copy).then_inc(sq_ready.sem, 1)
            act.wait_ge(y0_out.sem, y0_out.due(t, 1))
            act.activation(y[:, :], ps[:, 7, :], ACT.Copy).then_inc(y0_ready.sem, 1)
            for n in range(8 if sample else 4):
                if sample and n >= 4:
                    act.wait_ge(st_out.sem, st_out.due(t, n - 3))
                    act.wait_ge(s_ready.sem, s_ready.due(t, n - 3))
                act.wait_ge(g_ready.sem, g_ready.due(t, n + 1))
                for o in range(2):
                    ins = act.activation(H[o * HD:(o + 1) * HD, n % 4, :, o * HD:(o + 1) * HD],
                                         ps[o * HD:(o + 1) * HD, n % 4, 256:512].rearrange("p (a c) -> p a c", c=HD),
                                         ACT.Copy)
                ins.then_inc(h_ready.sem, 1)
            act.wait_ge(gn_var.sem, gn_var.due(t, 1))
            act.activation(small[:, 5, :], small[:, 4, :], ACT.Sqrt).then_inc(gn_std.sem, 1)
            nk = SAMPLES + 1 if sample else 2
            act.wait_ge(qkT_out.sem, qkT_out.due(t, 1))
            act.activation(qT[:, :, :], ps[:, 0, :].rearrange("p (a n) -> p a n", n=P), ACT.Copy)
            act.activation(keyT[:, 0:nk * P], ps[:, 1:4, :].rearrange("p b n -> p (b n)")[:, 0:nk * P], ACT.Copy)\
               .then_inc(qkT_ready.sem, 1)
            for h in range(HEADS):
                act.wait_ge(max_ready.sem, max_ready.due(t, h + 1))
                act.activation(sc[:, 0:nk * P], sc[:, 0:nk * P], ACT.Exp, bias=ast[:, 2, h:h + 1],
                               scale=SCALE, accum_out=ast[:, 3, h:h + 1]).then_inc(pr_ready.sem, 1)
                act.wait_ge(prT_out.sem, prT_out.due(t, h + 1))
                act.activation(prT[:, 0:nk * P], ps[:, 0:3, :].rearrange("p b n -> p (b n)")[:, 0:nk * P],
                               ACT.Copy).then_inc(prT_ready.sem, 1)
            act.wait_ge(sink_in.sem, sink_in.due(t, 1))
            act.activation(ast[:, 4, :], ast[:, 4, :], ACT.Exp).then_inc(sink_exp.sem, 1)
            act.wait_ge(o_var.sem, o_var.due(t, 1))
            act.activation(ast[:, 6, :], ast[:, 6, :], ACT.Sqrt).then_inc(o_std.sem, 1)
            act.wait_ge(o_std.sem, o_std.due(t, 1))
            act.sem_inc(tile_end.sem, 1)

        def vector_tile(dve, t, sample, links):
            link = Link(dve, links, t)
            v = 1 if sample else 0
            B = lambda c, n: bc[:, c:c + n]
            h3 = lambda ap: ap.rearrange("p (h c) -> p h c", c=HD)
            per_head = lambda ap: ap.unsqueeze(2).to_broadcast([P, HEADS, HD])
            r, k, vv = (xs[:, n * RW:(n + 1) * RW] for n in range(3))
            dve.wait_ge(tile_end.sem, tile_end.due(t, 5))
            dve.wait_ge(p_in.sem, p_in.due(t, 16))
            dve.wait_ge(prev_in.sem, prev_in.due(t, 16))
            if sample:
                dve.wait_ge(prev_fix.sem, 16)
            link(dve.tensor_tensor(xs[:, :], xs[:, :], p_cur[:, 0:P_RWKV], ALU.subtract))
            link(dve.tensor_tensor(xs[:, :], xs[:, :], B(MU, P_RWKV), ALU.mult))
            link(dve.tensor_tensor(xs[:, :], xs[:, :], p_cur[:, 0:P_RWKV], ALU.add))
            dve.sem_inc(xs_ready.sem, 1)
            link(dve.tensor_tensor(kk[:, :], k, B(KKC, RW), ALU.mult))
            link(dve.tensor_tensor(work[:, :], kk[:, :], kk[:, :], ALU.mult))
            dve.tensor_reduce(small[:, 0, :], h3(work[:, :]), AX.X, ALU.add).then_inc(kk_ss.sem, 1)
            dve.wait_ge(lora_out.sem, lora_out.due(t, 1))
            dve.tensor_tensor(sa[:, :, :], ps[:, 1:3, :], B(W0A0, 2 * RW).rearrange("p (a n) -> p a n", a=2),
                              ALU.add).then_inc(pre_ready.sem, 1)
            dve.wait_ge(kk_norm.sem, kk_norm.due(t, 1))
            link(dve.tensor_scalar(small[:, 1, :], small[:, 1, :], L2_EPS, None, ALU.max))
            link(dve.reciprocal(small[:, 1, :], small[:, 1, :]))
            link(dve.tensor_tensor(h3(kk[:, :]), h3(kk[:, :]), per_head(small[:, 1, :]), ALU.mult))
            dve.wait_ge(sig_ready.sem, sig_ready.due(t, 1))
            a = sa[:, 1, :]
            link(dve.scalar_tensor_tensor(out=work[:, :], in0=a, scalar=-1.0, in1=B(KAC, RW), op0=ALU.add, op1=ALU.mult))
            link(dve.scalar_tensor_tensor(out=k2[:, :], in0=work[:, :], scalar=1.0, in1=k, op0=ALU.add, op1=ALU.mult))
            link(dve.tensor_tensor(work2[:, :], kk[:, :], a, ALU.mult))
            dve.wait_ge(exps_ready.sem, exps_ready.due(t, 1))
            dve.scalar_tensor_tensor(out=fac[:, 0, :], in0=kk[:, :], scalar=-1.0, in1=ex[:, 1, :],
                                     op0=ALU.mult, op1=ALU.mult).then_inc(factors.sem, 1)
            dve.wait_ge(exps_ready.sem, exps_ready.due(t, 2))
            dve.tensor_tensor(fac[:, 2, :], work2[:, :], ex[:, 2, :], ALU.mult).then_inc(factors.sem, 1)
            dve.tensor_tensor(fac[:, 3, :], k2[:, :], ex[:, 2, :], ALU.mult).then_inc(factors.sem, 1)
            dve.wait_ge(exps_ready.sem, exps_ready.due(t, 4))
            dve.tensor_tensor(fac[:, 1, :], r, ex[:, 0, :], ALU.mult).then_inc(factors.sem, 1)
            link(dve.tensor_tensor(bk[:, 0, 0, :], work2[:, :], ex[:, 3, :], ALU.mult))
            link(dve.tensor_tensor(bk[:, 1, 0, :], k2[:, :], ex[:, 3, :], ALU.mult))
            if sample:
                for n in range(2):
                    dve.tensor_scalar(bk[:, n, 1, :], bk[:, n, 0, :], rowm[:, 1:2], None, ALU.mult)
                    link(dve.tensor_scalar(bk[:, n, 0, :], bk[:, n, 0, :], rowm[:, 0:1], None, ALU.mult))
            dve.sem_inc(factors.sem, 2)
            link(dve.tensor_tensor(work[:, :], r, k2[:, :], ALU.mult))
            link(dve.tensor_tensor(work[:, :], work[:, :], B(RKC, RW), ALU.mult))
            dve.tensor_reduce(bonus[:, :], h3(work[:, :]), AX.X, ALU.add)
            m2 = rc[:, v, MASK2:MASK2 + 2 * P].unsqueeze(1).to_broadcast([P, PAIRS, 2 * P])
            for dst, out, ready, bank in ((pqb, pb_out, pqb_ready, 4), (pqk, pk_out, pqk_ready, 0)):
                dve.wait_ge(out.sem, out.due(t, 1))
                for o in range(2):
                    dve.tensor_tensor(dst[:, o, :, :], ps[:, bank + 2 * o:bank + 2 * o + 2, :]
                                      .rearrange("p b (a n) -> p (b a) n", n=2 * P), m2, ALU.mult)\
                       .then_inc(ready.sem, 1)
            dve.wait_ge(n_out.sem, n_out.due(t, 1))
            dve.tensor_tensor(pw[:, 0, :, :], ps[:, 4:6, :].rearrange("p b (a n) -> p (b a) n", n=P),
                              rc[:, v, MASKN:MASKN + P].unsqueeze(1).to_broadcast([P, HEADS, P]), ALU.mult)\
               .then_inc(n_ready.sem, 1)
            dve.wait_ge(x0_ready.sem, x0_ready.due(t, 1))
            for i in range(5):
                dve.wait_ge(ap_out.sem, ap_out.due(t, i + 1))
                dve.tensor_tensor(X[:, :, :], X[:, :, :], ps[:, 0:2, :].rearrange("p b (a n) -> p (b a) n", n=P),
                                  ALU.add).then_inc(x_ready.sem, 1)
            dve.wait_ge(rp_out.sem, rp_out.due(t, 1))
            if sample:
                link(dve.tensor_tensor(rpT[:, 1, :, :], ps[:, 6, :].rearrange("p (a n) -> p a n", n=P),
                                       arT[:, :, P:2 * P], ALU.add))
                cm = lambda e: colm[:, e, :].unsqueeze(1).to_broadcast([P, PAIRS, P])
                link(dve.tensor_tensor(rpT[:, 0, :, :], rpT[:, 1, :, :], cm(0), ALU.mult))
                dve.tensor_tensor(rpT[:, 1, :, :], rpT[:, 1, :, :], cm(1), ALU.mult).then_inc(rp_ready.sem, 1)
            else:
                dve.tensor_tensor(rpT[:, 0, :, :], ps[:, 6, :].rearrange("p (a n) -> p a n", n=P),
                                  arT[:, :, P:2 * P], ALU.add).then_inc(rp_ready.sem, 1)

            def g_blocks(n):
                dve.wait_ge(gh_out.sem, gh_out.due(t, n + 1))
                dve.wait_ge(pcd_ready.sem, pcd_ready.due(t, n + 1))
                for o in range(2):
                    q = slice(o * HD, (o + 1) * HD)
                    ins = dve.tensor_tensor(G[q, n % 4, :, q], ps[q, n % 4, 0:256].rearrange("p (a c) -> p a c", c=HD),
                                            pcd[q, n % 2, :, :], ALU.add)
                ins.then_inc(g_ready.sem, 1)

            def next_state(n):
                dve.wait_ge(st_out.sem, st_out.due(t, n + 1))
                dve.wait_ge(h_ready.sem, h_ready.due(t, n + 1))
                if sample:
                    dve.wait_ge(s_stored.sem, 32 * n + 32)
                dve.tensor_tensor((S2 if sample else S)[:, :, :], ps[:, 4 if n % 2 == 0 else 6, :]
                                  .rearrange("p (a c) -> p a c", c=P), H[:, n % 4, :, :], ALU.add)\
                   .then_inc(s_ready.sem, 1)

            if sample:
                for n in range(4):
                    g_blocks(n)
                for n in range(8):
                    next_state(n)
                    if n < 4:
                        g_blocks(n + 4)
            else:
                for n in range(4):
                    g_blocks(n)
                for n in range(4):
                    next_state(n)
            dve.wait_ge(y0_ready.sem, y0_ready.due(t, 1))
            link(dve.tensor_tensor(y[:, :], y[:, :], ps[:, 5, :], ALU.add))
            link(dve.tensor_reduce(small[:, 2, :], h3(y[:, :]), AX.X, ALU.add))
            link(dve.tensor_scalar(small[:, 2, :], small[:, 2, :], 1.0 / HD, None, ALU.mult))
            link(dve.tensor_tensor(h3(y[:, :]), h3(y[:, :]), per_head(small[:, 2, :]), ALU.subtract))
            link(dve.tensor_tensor(work[:, :], y[:, :], y[:, :], ALU.mult))
            link(dve.tensor_reduce(small[:, 3, :], h3(work[:, :]), AX.X, ALU.add))
            dve.tensor_scalar(small[:, 4, :], small[:, 3, :], 1.0 / HD, LN_EPS, ALU.mult, ALU.add)\
               .then_inc(gn_var.sem, 1)
            dve.wait_ge(gn_std.sem, gn_std.due(t, 1))
            link(dve.reciprocal(small[:, 5, :], small[:, 5, :]))
            link(dve.tensor_tensor(h3(y[:, :]), h3(y[:, :]), per_head(small[:, 5, :]), ALU.mult))
            link(dve.tensor_tensor(y[:, :], y[:, :], B(LNW, RW), ALU.mult))
            link(dve.tensor_tensor(y[:, :], y[:, :], B(LNB, RW), ALU.add))
            link(dve.tensor_tensor(h3(work[:, :]), per_head(bonus[:, :]), h3(vv), ALU.mult))
            link(dve.tensor_tensor(y[:, :], y[:, :], work[:, :], ALU.add))
            dve.wait_ge(gate_ready.sem, gate_ready.due(t, 1))
            dve.tensor_tensor(cat[:, 0:RW], y[:, :], gate[:, :], ALU.mult).then_inc(y_done.sem, 1)
            nk = SAMPLES + 1 if sample else 2
            dve.wait_ge(mask_in.sem, mask_in.due(t, 16))
            for h in range(HEADS):
                dve.wait_ge(sc_out.sem, sc_out.due(t, h + 1))
                if h:
                    dve.wait_ge(prT_out.sem, prT_out.due(t, h))
                link(dve.tensor_tensor(sc[:, 0:nk * P], ps[:, 4:7, :].rearrange("p b n -> p (b n)")[:, 0:nk * P],
                                       amask[:, 0:nk * P], ALU.add))
                link(dve.tensor_reduce(ast[:, 0, h:h + 1], sc[:, 0:nk * P], AX.X, ALU.max))
                link(dve.tensor_scalar(ast[:, 1, h:h + 1], ast[:, 0, h:h + 1], SCALE, bc[:, SINK + h:SINK + h + 1],
                                       ALU.mult, ALU.max))
                dve.tensor_scalar(ast[:, 2, h:h + 1], ast[:, 1, h:h + 1], -1.0, None, ALU.mult)\
                   .then_inc(max_ready.sem, 1)
            dve.tensor_tensor(ast[:, 4, :], B(SINK, HEADS), ast[:, 1, :], ALU.subtract).then_inc(sink_in.sem, 1)
            dve.wait_ge(sink_exp.sem, sink_exp.due(t, 1))
            link(dve.tensor_tensor(ast[:, 5, :], ast[:, 3, :], ast[:, 4, :], ALU.add))
            link(dve.reciprocal(ast[:, 5, :], ast[:, 5, :]))
            dve.wait_ge(o_out.sem, o_out.due(t, 8))
            link(dve.tensor_tensor(h3(y[:, :]), ps[:, 7, :].rearrange("p (h c) -> p h c", c=HD),
                                   per_head(ast[:, 5, :]), ALU.mult))
            link(dve.tensor_tensor(work[:, :], y[:, :], y[:, :], ALU.mult))
            link(dve.tensor_reduce(ast[:, 6, :], h3(work[:, :]), AX.X, ALU.add))
            dve.tensor_scalar(ast[:, 6, :], ast[:, 6, :], 1.0 / HD, RMS_EPS, ALU.mult, ALU.add)\
               .then_inc(o_var.sem, 1)
            dve.wait_ge(o_std.sem, o_std.due(t, 1))
            link(dve.reciprocal(ast[:, 7, :], ast[:, 6, :]))
            link(dve.tensor_tensor(h3(y[:, :]), h3(y[:, :]), per_head(ast[:, 7, :]), ALU.mult))
            link(dve.tensor_tensor(cat[:, RW:D], y[:, :], B(OUTG, RW), ALU.mult))
            dve.sem_inc(cat_ready.sem, 1)
            dve.sem_inc(tile_end.sem, 1)
            if sample:
                return link.n
            link.close()

        def gpsimd_tile(pool, t, sample):
            pool.wait_ge(tile_end.sem, tile_end.due(t, 5))
            pool.wait_ge(exps_ready.sem, exps_ready.due(t, 5))
            for n in range(8 if sample else 4):
                if n >= 2:
                    pool.wait_ge(g_ready.sem, g_ready.due(t, n - 1))
                b = (2 * (n % 4) + n // 4) if sample else n
                pool.tensor_tensor(pcd[:, n % 2, :, :], ident2[:, :].unsqueeze(1).to_broadcast([P, PAIRS, HD]),
                                   pc[:, :, b:b + 1].to_broadcast([P, PAIRS, HD]), ALU.mult)\
                    .then_inc(pcd_ready.sem, 1)
            pool.wait_ge(pcd_ready.sem, pcd_ready.due(t, 8 if sample else 4))
            pool.sem_inc(tile_end.sem, 1)

        def tensor_tile(pe, t, sample):
            v = 1 if sample else 0
            half = lambda o: slice(o * HD, (o + 1) * HD)
            pe.wait_ge(tile_end.sem, tile_end.due(t, 5))
            pe.wait_ge(lora_in.sem, lora_in.due(t, 1))
            pe.transpose(ps[:, 0, 0:P], lora[:, 0:P], ident[:, :])
            pe.transpose(ps[:, 0, P:2 * P], lora[:, P:2 * P], ident[:, :])
            pe.transpose(ps[0:GLORA - P, 0, 2 * P:3 * P], lora[:, 2 * P:], ident[:, :]).then_inc(loraT_out.sem, 1)
            pe.wait_ge(loraT_ready.sem, loraT_ready.due(t, 1))
            pe.matmul(ps[:, 1, :], loraT[:, 0:P], w2a2[:, 0:RW], start=True, stop=True)
            pe.matmul(ps[:, 2, :], loraT[:, 0:P], w2a2[:, RW:], start=True, stop=True).then_inc(lora_out.sem, 1)
            pe.matmul(ps[:, 3, :], loraT[:, P:2 * P], g2a[:, :], start=True, stop=False)
            pe.matmul(ps[:, 3, :], loraT[0:GLORA - P, 2 * P:3 * P], g2b[:, :], start=False, stop=True)\
              .then_inc(lora_out.sem, 1)
            pe.wait_ge(sig_ready.sem, sig_ready.due(t, 1))
            pe.matmul(ps[:, 5, :], rc[:, v, TRI_X:TRI_X + P], sa[:, 0, :], start=True, stop=True)
            pe.matmul(ps[:, 4, :], rc[:, v, TRI_I:TRI_I + P], sa[:, 0, :], start=True, stop=True)
            pe.matmul(ps[:, 6, :], rc[:, v, TRI_S:TRI_S + P], sa[:, 0, :], start=True, stop=True)
            for q in range(PAIRS):
                last = pe.matmul(ps[:, 7, 8 * q:8 * q + 8], sa[:, 0, q * P:(q + 1) * P], rc[:, v, IND:IND + 8],
                                 start=True, stop=True)
            last.then_inc(cum_done.sem, 1)
            pe.wait_ge(gate_ready.sem, gate_ready.due(t, 1))
            pe.wait_ge(factors.sem, factors.due(t, 6))
            for n in range(4):
                for q in range(PAIRS):
                    last = pe.transpose(ps[:, n, q * P:(q + 1) * P], fac[:, n, q * P:(q + 1) * P], ident[:, :])
                last.then_inc(facT_out.sem, 1)
            pe.wait_ge(exps_ready.sem, exps_ready.due(t, 5))
            pe.wait_ge(facT_ready.sem, facT_ready.due(t, 4))
            for left, bank, done in ((bT, 4, pb_out), (kT, 0, pk_out)):
                for o in range(2):
                    for q in range(PAIRS):
                        last = pe.matmul(ps[:, bank + 2 * o + q // 2, (q % 2) * 256:(q % 2) * 256 + 256],
                                         left[half(o), q, :], arT[half(o), q, :], start=True, stop=True)
                last.then_inc(done.sem, 1)
            pe.wait_ge(pqb_ready.sem, pqb_ready.due(t, 2))
            for o in range(2):
                for q in range(PAIRS):
                    last = pe.matmul(ps[:, 4 + o, q * P:(q + 1) * P], arT[half(o), q, 0:P], bT[half(o), q, :],
                                     start=True, stop=True)
            last.then_inc(n_out.sem, 1)
            pe.wait_ge(pqk_ready.sem, pqk_ready.due(t, 2))
            for o in range(2):
                for q in range(PAIRS):
                    last = pe.matmul(ps[:, 6, (4 * o + q) * HD:(4 * o + q + 1) * HD], pqk[:, o, q, 0:P],
                                     v_of(2 * q + o), start=True, stop=True)
            last.then_inc(w0_out.sem, 1)
            pe.wait_ge(n_ready.sem, n_ready.due(t, 1))
            for i in range(5):
                if i:
                    pe.wait_ge(sq_ready.sem, sq_ready.due(t, i))
                powT = lambda h: pqb[:, h // 4, h % 4, 0:P] if i == 0 else pwT[:, (i - 1) % 2, h, :]
                if i < 4:
                    for h in range(HEADS):
                        pe.matmul(ps[:, 2 + h // 4, (h % 4) * P:(h % 4 + 1) * P], pw[:, i % 2, h, :], powT(h),
                                  start=True, stop=True)
                    for h in range(HEADS):
                        last = pe.matmul(ps[:, 4 + h // 4, (h % 4) * P:(h % 4 + 1) * P], powT(h), pw[:, i % 2, h, :],
                                         start=True, stop=True)
                    last.then_inc(sq_out.sem, 1)
                if i:
                    pe.wait_ge(x_ready.sem, x_ready.due(t, i))
                else:
                    pe.wait_ge(x0_ready.sem, x0_ready.due(t, 1))
                for h in range(HEADS):
                    last = pe.matmul(ps[:, h // 4, (h % 4) * P:(h % 4 + 1) * P], powT(h), X[:, h, :],
                                     start=True, stop=True)
                last.then_inc(ap_out.sem, 1)
            pe.wait_ge(x_ready.sem, x_ready.due(t, 5))
            for o in range(2):
                for q in range(PAIRS):
                    last = pe.matmul(ps[half(o), 6, q * P:(q + 1) * P], X[:, 4 * o + q, 0:HD], pqb[:, o, q, P:2 * P],
                                     start=True, stop=True)
            last.then_inc(rp_out.sem, 1)
            for h in range(HEADS):
                o, q = h % 2, h // 2
                pe.matmul(ps[:, 7, h * HD:(h + 1) * HD], pqb[:, o, q, P:2 * P], X[:, 4 * o + q, HD:P],
                          start=True, stop=False)
                last = pe.matmul(ps[:, 7, h * HD:(h + 1) * HD], pqk[:, o, q, P:2 * P], v_of(h),
                                 start=False, stop=True)
            last.then_inc(y0_out.sem, 1)

            def transition(n):
                b, e = n % 4, n // 4
                rows = slice(32 * b, 32 * b + 32)
                for h in range(HEADS):
                    o, q = h % 2, h // 2
                    beta = bk[rows, 0, e, h * HD:(h + 1) * HD]
                    kappa = bk[rows, 1, e, h * HD:(h + 1) * HD]
                    value = xs[rows, 2 * RW + h * HD:2 * RW + (h + 1) * HD]
                    tp = (32 * b, o * HD)
                    pe.matmul(ps[half(o), b, q * HD:(q + 1) * HD], X[rows, 4 * o + q, 0:HD], beta,
                              start=True, stop=True, tile_position=tp)
                    pe.matmul(ps[half(o), b, 256 + q * HD:256 + (q + 1) * HD], beta, X[rows, 4 * o + q, HD:P],
                              start=True, stop=False, tile_position=tp)
                    last = pe.matmul(ps[half(o), b, 256 + q * HD:256 + (q + 1) * HD], kappa, value,
                                     start=False, stop=True, tile_position=tp)
                last.then_inc(gh_out.sem, 1)

            def state_product(n, bank):
                for q in range(PAIRS):
                    last = pe.matmul(ps[:, bank, q * P:(q + 1) * P], G[:, n % 4, q, :], S[:, q, :],
                                     start=True, stop=True)
                last.then_inc(st_out.sem, 1)

            for n in range(4):
                transition(n)
            pe.wait_ge(rp_ready.sem, rp_ready.due(t, 1))
            if sample:
                for n in range(8):
                    b = 2 * (n % 4) + n // 4
                    pe.wait_ge(s_loaded.sem, 32 * (n + 1))
                    pe.wait_ge(g_ready.sem, g_ready.due(t, n + 1))
                    rows = slice(32 * (n % 4), 32 * (n % 4) + 32)
                    e = n // 4
                    for q in range(PAIRS):
                        pe.matmul(ps[rows, 5, q * P:(q + 1) * P], rpT[:, e, q, rows], S[:, q, :],
                                  start=(e == 0 and q == 0), stop=e == 1, skip_group_check=True)
                    if n >= 2:
                        pe.wait_ge(s_ready.sem, s_ready.due(t, n - 1))
                    state_product(n, 4 if n % 2 == 0 else 6)
                    if n < 4:
                        pe.wait_ge(h_ready.sem, h_ready.due(t, n + 1))
                        transition(n + 4)
            else:
                for n in range(4):
                    pe.wait_ge(g_ready.sem, g_ready.due(t, n + 1))
                    if n:
                        pe.wait_ge(s_ready.sem, s_ready.due(t, n))
                    rows = slice(32 * n, 32 * n + 32)
                    for q in range(PAIRS):
                        pe.matmul(ps[rows, 5, q * P:(q + 1) * P], rpT[:, 0, q, rows], S[:, q, :],
                                  start=True, stop=True)
                    state_product(n, 4 if n % 2 == 0 else 6)
            nk = SAMPLES + 1 if sample else 2
            pe.wait_ge(h_ready.sem, h_ready.due(t, 8 if sample else 4))
            pe.wait_ge(g_ready.sem, g_ready.due(t, 8 if sample else 4))
            pe.wait_ge(kv_in.sem, kv_in.due(t, 16))
            if sample:
                pe.wait_ge(kv_in2.sem, 16 * 2 * SAMPLES)
            for j in range(4):
                pe.transpose(ps[:, 0, j * P:(j + 1) * P], p_cur[:, Q0 + j * P:Q0 + (j + 1) * P], ident[:, :])
            for n in range(nk):
                last = pe.transpose(ps[:, 1 + n // 4, (n % 4) * P:(n % 4 + 1) * P], kv[:, n, 0:P], ident[:, :])
            last.then_inc(qkT_out.sem, 1)
            pe.wait_ge(qkT_ready.sem, qkT_ready.due(t, 1))
            pe.wait_ge(y_done.sem, y_done.due(t, 1))
            for h in range(HEADS):
                g = h // 4
                if h:
                    pe.wait_ge(max_ready.sem, max_ready.due(t, h))
                for n in range(0, nk, 4):
                    w = min(4, nk - n) * P
                    last = pe.matmul(ps[:, 4 + n // 4, 0:w], qT[half(g), h % 4, :], keyT[half(g), n * P:n * P + w],
                                     start=True, stop=True)
                last.then_inc(sc_out.sem, 1)
                pe.wait_ge(pr_ready.sem, pr_ready.due(t, h + 1))
                if h:
                    pe.wait_ge(prT_ready.sem, prT_ready.due(t, h))
                for n in range(nk):
                    last = pe.transpose(ps[:, n // 4, (n % 4) * P:(n % 4 + 1) * P], sc[:, n * P:(n + 1) * P],
                                        ident[:, :])
                last.then_inc(prT_out.sem, 1)
                pe.wait_ge(prT_ready.sem, prT_ready.due(t, h + 1))
                for n in range(nk):
                    last = pe.matmul(ps[:, 7, h * HD:(h + 1) * HD], prT[:, n * P:(n + 1) * P],
                                     kv[:, n, P + g * HD:P + (g + 1) * HD], start=n == 0, stop=n == nk - 1)
                last.then_inc(o_out.sem, 1)
            pe.wait_ge(o_out.sem, o_out.due(t, 8))
            pe.sem_inc(tile_end.sem, 1)

        block = ctx.enter_context(nc.Block())

        @block.sync
        def _(sp):
            for dst, src in ((ident[:, :], A["ident"]), (ident2[:, :], A["ident2"]),
                             (rc[:, :, :], A["rc"]), (rowm[:, :], A["rowm"]), (colm[:, :, :], A["colm"]),
                             (w2a2[0:LORA, 0:RW], A["w2"]), (w2a2[LORA:P, RW:], A["a2"]),
                             (g2a[:, :], A["g2"][0:P, :]), (g2b[:, :], A["g2"][P:GLORA, :])):
                sp.dma_start(dst, src).then_inc(consts.sem, 16)
            for name, at, n in (("mu", MU, P_RWKV), ("w0", W0A0, RW), ("a0", W0A0 + RW, RW), ("k_k", KKC, RW),
                                ("k_a", KAC, RW), ("r_k", RKC, RW), ("ln_w", LNW, RW), ("ln_b", LNB, RW),
                                ("out_g", OUTG, RW), ("sinks", SINK, HEADS)):
                sp.dma_start(bc[:, at:at + n], row(A[name]).to_broadcast([P, n])).then_inc(consts.sem, 16)
            sp.wait_ge(consts.sem, ALL_CONSTS)
            sp.sem_inc(tile_end.sem, 1)
            copies = ((A["shift_prompt"], proj[P + SEQ - 1:P + SEQ, 0:P_RWKV]),
                      (A["k_prompt"], proj[SEQ:P + SEQ, K0:V0]),
                      (A["v_prompt"], proj[SEQ:P + SEQ, V0:P_TOTAL]),
                      (A["shift_sample"], proj[P + SEQ + STEPS - 1:P + TOKENS:STEPS, 0:P_RWKV]),
                      (A["k_sample"][:, P - STEPS:, :], proj[P + SEQ:, K0:V0].rearrange("(b s) c -> b s c", s=STEPS)),
                      (A["v_sample"][:, P - STEPS:, :], proj[P + SEQ:, V0:].rearrange("(b s) c -> b s c", s=STEPS)),
                      (A["k_sample"][:, 0:P - STEPS, :], A["cache_k"][:, STEPS:, :]),
                      (A["v_sample"][:, 0:P - STEPS, :], A["cache_v"][:, STEPS:, :]))
            for dst, src in copies:
                sp.dma_start(dst, src).then_inc(consts.sem, 16)
            with sp.Fori(0, T8) as t:
                sync_tile(sp, t, False)
            for o in range(2):
                sp.dma_start(A["wkvT_prompt"][o], S[o * HD:(o + 1) * HD, :, o * HD:(o + 1) * HD])\
                  .then_inc(s_stored.sem, 16)
            sync_tile(sp, T8, True)
            sp.wait_ge(s_stored.sem, 32 * (SAMPLES + 1))
            sp.wait_ge(consts.sem, ALL_CONSTS + 16 * len(copies))

        @block.scalar
        def _(act):
            act.sem_inc(tile_end.sem, 1)
            with act.Fori(0, T8) as t:
                scalar_tile(act, t, False)
            scalar_tile(act, T8, True)

        @block.vector
        def _(dve):
            dve.memset(S[:, :, :], 0.0)
            dve.memset(S2[:, :, :], 0.0)
            dve.memset(w2a2[0:LORA, RW:], 0.0)
            dve.memset(w2a2[LORA:P, 0:RW], 0.0)
            dve.memset(G[:, :, :, :], 0.0)
            dve.memset(H[:, :, :, :], 0.0).then_inc(dve_start.sem, 1)
            dve.wait_ge(dve_start.sem, 1)
            dve.sem_inc(tile_end.sem, 1)
            with dve.Fori(0, T8) as t:
                vector_tile(dve, t, False, dve_link)
            vector_tile(dve, T8, True, dve_link)

        @block.gpsimd
        def _(pool):
            pool.sem_inc(tile_end.sem, 1)
            with pool.Fori(0, T8) as t:
                gpsimd_tile(pool, t, False)
            gpsimd_tile(pool, T8, True)

        @block.tensor
        def _(pe):
            pe.sem_inc(tile_end.sem, 1)
            with pe.Fori(0, T8) as t:
                tensor_tile(pe, t, False)
            tensor_tile(pe, T8, True)


CAND = [(0, 1, 16), (1, 1, 8), (2, 1, 5), (3, 1, 4), (4, 1, 3), (5, 3, 2), (8, 8, 1)]
NCAND = sum(n * m for _, n, m in CAND)
PEER_LINKS = 45
RING = 8
GROUP = 4


def peer(nc, A):
    with ExitStack() as ctx:
        def sb(name, shape, dt=F32):
            return ctx.enter_context(nc.sbuf_tensor("pr_" + name, shape, dt))

        def signal(name, per=1):
            return Signal(ctx, nc, name, per)

        ident = sb("ident_p", [P, P])
        w_out = sb("w_out_sb", [P, KC, D])
        w_q = sb("w_q_sb", [P, KC, 2 * D])
        keysT = sb("keysT", [P, 2, P])
        gain = sb("gain_ffn", [P, D])
        gain_f = sb("gain_final", [P, D])
        iota = sb("iota50", [P, NCAND])
        x2 = sb("x2", [P, D])
        tn = sb("tn", [P, D])
        big = sb("big", [P, 2, D])
        s12 = sb("s12", [P, 16, P])
        aT = sb("aT", [P, KC, P])
        s12b = big[:, :, :].rearrange("p a d -> p (a d)").rearrange("p (h n) -> p h n", n=P)
        qT = s12
        v16 = sb("v16", [P, 16, TOPK])
        i16 = sb("i16", [P, 16, TOPK], U32)
        f16 = sb("f16", [P, 16, TOPK])
        cand = sb("cand", [P, 8, NCAND])
        s_flat = s12[:, :, :].rearrange("p h n -> p (h n)")
        candb, cidx = (s_flat[:, n * 8 * NCAND:(n + 1) * 8 * NCAND].rearrange("p (h n) -> p h n", n=NCAND)
                       for n in range(2))
        best = sb("best", [P, 8, TOPK])
        pos = sb("pos", [P, 8, TOPK], U32)
        posf = sb("posf", [P, 8, TOPK])
        hot = big[:, 0, 0:TOPK * NCAND].rearrange("p (k n) -> p k n", n=NCAND)
        expf = sb("expf", [P, 8, TOPK])
        expert = sb("expert", [P, SLOTS], U32)
        gate = sb("gate", [P, 8, TOPK])
        gsum = sb("gsum", [P, 2, 8])
        st = sb("stat", [P, 8])
        rows = sb("rows", [P, RING, 2 * D])
        u = sb("u", [P, SLOTS])
        ge = sb("ge", [P, SLOTS])
        coef = sb("coef", [P, SLOTS])
        diag = aT
        ps = ctx.enter_context(nc.psum_tensor("ps_p", [P, 8, 512], F32))
        NGR = SLOTS // GROUP

        consts = signal("peer_consts")
        tile_end = signal("peer_tile_end", 5)
        mixed_in = signal("mixed_in", 16)
        x_in = signal("xr_in", 16)
        mT_out = signal("mT_out")
        mT_ready = signal("mT_ready")
        wo_out = signal("wo_out")
        ssq_ready = signal("ssq_ready")
        std_ready = signal("std_p_ready")
        tn_ready = signal("tn_ready")
        tT_out = signal("tT_out")
        tT_ready = signal("tT_ready")
        q_out = signal("q_out", 4)
        q_ready = signal("q_ready", 4)
        s_out = signal("s_out", 4)
        s_ready = signal("s_p_ready", 4)
        smax_in = signal("smax_in")
        sexp = signal("sexp")
        experts = signal("experts")
        gates = signal("gates")
        row_in = [signal(f"row_in{r}", 16 * SLOTS // RING) for r in range(RING)]
        row_free = signal("row_free")
        dotted = signal("dotted", SLOTS)
        gelued = signal("gelued", NGR)
        coefs = signal("coefs", NGR)
        diags = signal("diags", SLOTS)
        row_used = signal("row_used", SLOTS)
        ssq2_ready = signal("ssq2_ready")
        std2_ready = signal("std2_ready")
        y_ready = signal("y_ready")
        y_stored = signal("y_stored", 16)
        links = signal("peer_dve_link", PEER_LINKS)
        passed = signal("peer_dve_passed")

        block = ctx.enter_context(nc.Block())

        @block.sync
        def _(sp):
            sp.dma_start(ident[:, :], A["ident"]).then_inc(consts.sem, 16)
            sp.dma_start(w_out[:, :, :], A["w_out"].rearrange("(k p) n -> p k n", p=P)).then_inc(consts.sem, 16)
            sp.dma_start(w_q[:, :, :], A["w_q"].rearrange("(k p) n -> p k n", p=P)).then_inc(consts.sem, 16)
            sp.dma_start(keysT[:, 0, :], A["key1T"]).then_inc(consts.sem, 16)
            sp.dma_start(keysT[:, 1, :], A["key2T"]).then_inc(consts.sem, 16)
            sp.dma_start(gain[:, :], row(A["norm_ffn"]).to_broadcast([P, D])).then_inc(consts.sem, 16)
            sp.dma_start(gain_f[:, :], row(A["norm_final"]).to_broadcast([P, D])).then_inc(consts.sem, 16)
            sp.dma_start(iota[:, :], row(A["iota"]).to_broadcast([P, NCAND])).then_inc(consts.sem, 16)
            sp.wait_ge(consts.sem, 16 * 8)
            sp.sem_inc(tile_end.sem, 1)
            with sp.Fori(0, TILES) as t:
                sp.wait_ge(tile_end.sem, tile_end.due(t, 5))
                sp.dma_start(big[:, 0, :], A["mixed"][bass.ds(t * P, P), :]).then_inc(mixed_in.sem, 16)
                sp.dma_start(x2[:, :], A["x"][bass.ds(t * P, P), :]).then_inc(x_in.sem, 16)
                sp.wait_ge(y_ready.sem, y_ready.due(t, 1))
                sp.dma_start(A["y"][bass.ds(t * P, P), :], tn[:, :]).then_inc(y_stored.sem, 16)
                sp.wait_ge(y_stored.sem, y_stored.due(t, 16))
                sp.sem_inc(tile_end.sem, 1)

        @block.gpsimd
        def _(pool):
            pool.sem_inc(tile_end.sem, 1)
            with pool.Fori(0, TILES) as t:
                pool.wait_ge(experts.sem, experts.due(t, 1)).then_inc(row_free.sem, 1)
                for s in range(SLOTS):
                    r = s % RING
                    pool.wait_ge(row_used.sem, row_used.due(t, s + 1)).then_inc(row_free.sem, 1)
                    pool.indirect_dma_start(rows[:, r, :], None, A["experts"],
                                            bass.IndirectOffsetOnAxis(expert[:, s:s + 1], 0))\
                        .then_inc(row_in[r].sem, 16)
                pool.wait_ge(row_used.sem, row_used.due(t, SLOTS + RING)).then_inc(row_free.sem, 1)
                pool.sem_inc(tile_end.sem, 1)

        @block.scalar
        def _(act):
            act.sem_inc(tile_end.sem, 1)
            with act.Fori(0, TILES) as t:
                act.wait_ge(tile_end.sem, tile_end.due(t, 5))
                act.wait_ge(mT_out.sem, mT_out.due(t, 1))
                act.activation(aT[:, :, :], ps[:, 0:2, :].rearrange("p b (k n) -> p (b k) n", n=P), ACT.Copy)\
                   .then_inc(mT_ready.sem, 1)
                act.wait_ge(ssq_ready.sem, ssq_ready.due(t, 1))
                act.activation(st[:, 1:2], st[:, 1:2], ACT.Sqrt).then_inc(std_ready.sem, 1)
                act.wait_ge(tT_out.sem, tT_out.due(t, 1))
                act.activation(aT[:, :, :], ps[:, 0:2, :].rearrange("p b (k n) -> p (b k) n", n=P), ACT.Copy)\
                   .then_inc(tT_ready.sem, 1)
                for g in range(4):
                    act.wait_ge(q_out.sem, q_out.due(t, g + 1))
                    act.activation(qT[:, 4 * g:4 * g + 4, :], ps[:, 4 + g, :].rearrange("p (k n) -> p k n", n=P),
                                   ACT.Copy).then_inc(q_ready.sem, 1)
                for g in range(4):
                    act.wait_ge(s_out.sem, s_out.due(t, g + 1))
                    act.activation(s12[:, 4 * g:4 * g + 4, :], ps[:, g, :].rearrange("p (k n) -> p k n", n=P),
                                   ACT.Copy).then_inc(s_ready.sem, 1)
                act.wait_ge(smax_in.sem, smax_in.due(t, 1))
                act.activation(gate[:, :, :], gate[:, :, :], ACT.Exp).then_inc(sexp.sem, 1)
                for g in range(NGR):
                    c = slice(g * GROUP, (g + 1) * GROUP)
                    act.wait_ge(dotted.sem, dotted.due(t, (g + 1) * GROUP))
                    act.activation(ge[:, c], u[:, c], ACT.Gelu).then_inc(gelued.sem, 1)
                    act.wait_ge(coefs.sem, coefs.due(t, g + 1))
                    for s in range(g * GROUP, (g + 1) * GROUP):
                        act.wait_ge(row_used.sem, row_used.due(t, s + 1))
                        act.activation(diag[:, s % RING, :], ident[:, :], ACT.Copy, scale=coef[:, s:s + 1])\
                           .then_inc(diags.sem, 1)
                act.wait_ge(ssq2_ready.sem, ssq2_ready.due(t, 1))
                act.activation(st[:, 3:4], st[:, 3:4], ACT.Sqrt).then_inc(std2_ready.sem, 1)
                act.wait_ge(std2_ready.sem, std2_ready.due(t, 1))
                act.sem_inc(tile_end.sem, 1)

        @block.vector
        def _(dve):
            dve.sem_inc(tile_end.sem, 1)
            with dve.Fori(0, TILES) as t:
                link = Link(dve, links, t)
                dve.wait_ge(tile_end.sem, tile_end.due(t, 5))
                dve.wait_ge(x_in.sem, x_in.due(t, 16))
                dve.wait_ge(wo_out.sem, wo_out.due(t, 1))
                flat = ps[:, 2:4, :].rearrange("p b n -> p (b n)")
                link(dve.tensor_tensor(x2[:, :], x2[:, :], flat, ALU.add))
                link(dve.tensor_tensor_reduce(out=tn[:, :], in0=x2[:, :], in1=x2[:, :], scale=1.0, scalar=0.0,
                                              op0=ALU.mult, op1=ALU.add, accum_out=st[:, 0:1]))
                dve.tensor_scalar(st[:, 1:2], st[:, 0:1], 1.0 / D, RMS_EPS, ALU.mult, ALU.add)\
                   .then_inc(ssq_ready.sem, 1)
                dve.wait_ge(std_ready.sem, std_ready.due(t, 1))
                link(dve.reciprocal(st[:, 1:2], st[:, 1:2]))
                dve.scalar_tensor_tensor(out=tn[:, :], in0=x2[:, :], scalar=st[:, 1:2], in1=gain[:, :],
                                         op0=ALU.mult, op1=ALU.mult).then_inc(tn_ready.sem, 1)
                dve.wait_ge(s_ready.sem, s_ready.due(t, 4)).then_inc(passed.sem, 1)
                for h in range(16):
                    last = dve.max(v16[:, h, 0:8], s12[:, h, :])
                link.hold(last, passed)
                for h in range(16):
                    dve.max_index(i16[:, h, 0:8], v16[:, h, 0:8], s12[:, h, :])
                for h in range(16):
                    last = dve.match_replace(s12b[:, h, :], v16[:, h, 0:8], s12[:, h, :], NEG)
                link.hold(last, passed)
                for h in range(16):
                    last = dve.max(v16[:, h, 8:16], s12b[:, h, :])
                link.hold(last, passed)
                for h in range(16):
                    last = dve.max_index(i16[:, h, 8:16], v16[:, h, 8:16], s12b[:, h, :])
                link(last)
                link(dve.tensor_copy(f16[:, :, :], i16[:, :, :]))
                first = lambda x: x.rearrange("p (h s) k -> p h s k", s=2)
                v, f = first(v16[:, :, :]), first(f16[:, :, :])
                link(dve.tensor_scalar(f[:, :, 0, :], f[:, :, 0, :], 128.0, None, ALU.mult))
                for dst, src in ((cand, v), (cidx, f)):
                    at = 0
                    for a, n, m in CAND:
                        out = dst[:, :, at:at + n * m]
                        if n == 1:
                            last = dve.tensor_tensor(out, src[:, :, 1, 0:m],
                                                     src[:, :, 0, a:a + 1].to_broadcast([P, 8, m]), ALU.add)
                        elif m == 1:
                            last = dve.tensor_tensor(out, src[:, :, 0, a:a + n],
                                                     src[:, :, 1, 0:1].to_broadcast([P, 8, n]), ALU.add)
                        else:
                            last = dve.tensor_tensor(out.rearrange("p h (n m) -> p h n m", m=m),
                                                     src[:, :, 1, 0:m].unsqueeze(2).to_broadcast([P, 8, n, m]),
                                                     src[:, :, 0, a:a + n].unsqueeze(3).to_broadcast([P, 8, n, m]),
                                                     ALU.add)
                        at += n * m
                link.hold(last, passed)
                for h in range(8):
                    last = dve.max(best[:, h, 0:8], cand[:, h, :])
                link.hold(last, passed)
                for h in range(8):
                    dve.max_index(pos[:, h, 0:8], best[:, h, 0:8], cand[:, h, :])
                for h in range(8):
                    last = dve.match_replace(candb[:, h, :], best[:, h, 0:8], cand[:, h, :], NEG)
                link.hold(last, passed)
                for h in range(8):
                    last = dve.max(best[:, h, 8:16], candb[:, h, :])
                link.hold(last, passed)
                for h in range(8):
                    last = dve.max_index(pos[:, h, 8:16], best[:, h, 8:16], candb[:, h, :])
                link(last)
                link(dve.tensor_copy(posf[:, :, :], pos[:, :, :]))
                for h in range(8):
                    link(dve.tensor_tensor(hot[:, :, :], iota[:, :].unsqueeze(1).to_broadcast([P, TOPK, NCAND]),
                                           posf[:, h, :].unsqueeze(2).to_broadcast([P, TOPK, NCAND]), ALU.is_equal))
                    link(dve.tensor_tensor(hot[:, :, :], hot[:, :, :],
                                           cidx[:, h, :].unsqueeze(1).to_broadcast([P, TOPK, NCAND]), ALU.mult))
                    last = dve.tensor_reduce(expf[:, h, :], hot[:, :, :], AX.X, ALU.add)
                    link(last)
                dve.tensor_copy(expert[:, :], expf[:, :, :].rearrange("p h k -> p (h k)")).then_inc(experts.sem, 1)
                dve.tensor_tensor(gate[:, :, :], best[:, :, :], best[:, :, 0:1].to_broadcast([P, 8, TOPK]),
                                  ALU.subtract).then_inc(smax_in.sem, 1)
                dve.wait_ge(sexp.sem, sexp.due(t, 1))
                link(dve.tensor_reduce(gsum[:, 0, :], gate[:, :, :], AX.X, ALU.add))
                link(dve.reciprocal(gsum[:, 1, :], gsum[:, 0, :]))
                link(dve.tensor_tensor(gate[:, :, :], gate[:, :, :],
                                       gsum[:, 1, :].unsqueeze(2).to_broadcast([P, 8, TOPK]), ALU.mult))
                gflat = gate[:, :, :].rearrange("p h k -> p (h k)")

                def coefficients(g):
                    c = slice(g * GROUP, (g + 1) * GROUP)
                    dve.wait_ge(gelued.sem, gelued.due(t, g + 1))
                    dve.tensor_tensor(coef[:, c], ge[:, c], gflat[:, c], ALU.mult).then_inc(coefs.sem, 1)

                for s in range(SLOTS):
                    dve.wait_ge(row_in[s % RING].sem, row_in[s % RING].due(t, 16 * (s // RING + 1)))
                    dve.tensor_tensor_reduce(out=rows[:, s % RING, 0:D], in0=rows[:, s % RING, 0:D], in1=tn[:, :],
                                             scale=1.0, scalar=0.0, op0=ALU.mult, op1=ALU.add,
                                             accum_out=u[:, s:s + 1]).then_inc(dotted.sem, 1)
                    if s % GROUP == 0 and s:
                        coefficients(s // GROUP - 1)
                coefficients(NGR - 1)
                dve.wait_ge(row_used.sem, row_used.due(t, SLOTS + RING))
                flat = ps[:, 0:2, :].rearrange("p b n -> p (b n)")
                link(dve.tensor_tensor(x2[:, :], x2[:, :], flat, ALU.add))
                link(dve.tensor_tensor_reduce(out=tn[:, :], in0=x2[:, :], in1=x2[:, :], scale=1.0, scalar=0.0,
                                              op0=ALU.mult, op1=ALU.add, accum_out=st[:, 2:3]))
                dve.tensor_scalar(st[:, 3:4], st[:, 2:3], 1.0 / D, RMS_EPS, ALU.mult, ALU.add)\
                   .then_inc(ssq2_ready.sem, 1)
                dve.wait_ge(std2_ready.sem, std2_ready.due(t, 1))
                link(dve.reciprocal(st[:, 3:4], st[:, 3:4]))
                dve.scalar_tensor_tensor(out=tn[:, :], in0=x2[:, :], scalar=st[:, 3:4], in1=gain_f[:, :],
                                         op0=ALU.mult, op1=ALU.mult).then_inc(y_ready.sem, 1)
                dve.wait_ge(y_ready.sem, y_ready.due(t, 1))
                dve.sem_inc(tile_end.sem, 1)
                link.close()

        @block.tensor
        def _(pe):
            pe.sem_inc(tile_end.sem, 1)
            pe.sem_inc(row_used.sem, RING)
            with pe.Fori(0, TILES) as t:
                pe.wait_ge(tile_end.sem, tile_end.due(t, 5))
                pe.wait_ge(mixed_in.sem, mixed_in.due(t, 16))
                for k in range(KC):
                    last = pe.transpose(ps[:, k // 4, (k % 4) * P:(k % 4 + 1) * P], big[:, 0, k * P:(k + 1) * P],
                                        ident[:, :])
                last.then_inc(mT_out.sem, 1)
                pe.wait_ge(mT_ready.sem, mT_ready.due(t, 1))
                for n in range(2):
                    for k in range(KC):
                        last = pe.matmul(ps[:, 2 + n, :], aT[:, k, :], w_out[:, k, n * 512:(n + 1) * 512],
                                         start=k == 0, stop=k == KC - 1)
                last.then_inc(wo_out.sem, 1)
                pe.wait_ge(tn_ready.sem, tn_ready.due(t, 1))
                for k in range(KC):
                    last = pe.transpose(ps[:, k // 4, (k % 4) * P:(k % 4 + 1) * P], tn[:, k * P:(k + 1) * P],
                                        ident[:, :])
                last.then_inc(tT_out.sem, 1)
                pe.wait_ge(tT_ready.sem, tT_ready.due(t, 1))
                for g in range(4):
                    for j in range(4):
                        c = (4 * g + j) * P
                        for k in range(KC):
                            last = pe.matmul(ps[:, 4 + g, j * P:(j + 1) * P], w_q[:, k, c:c + P], aT[:, k, :],
                                             start=k == 0, stop=k == KC - 1)
                    last.then_inc(q_out.sem, 1)
                for g in range(4):
                    pe.wait_ge(q_ready.sem, q_ready.due(t, g + 1))
                    for j in range(4):
                        last = pe.matmul(ps[:, g, j * P:(j + 1) * P], qT[:, 4 * g + j, :], keysT[:, j % 2, :],
                                         start=True, stop=True)
                    last.then_inc(s_out.sem, 1)
                pe.wait_ge(s_ready.sem, s_ready.due(t, 4))
                for s in range(SLOTS):
                    pe.wait_ge(diags.sem, diags.due(t, s + 1))
                    for n in range(2):
                        last = pe.matmul(ps[:, n, :], diag[:, s % RING, :],
                                         rows[:, s % RING, D + n * 512:D + (n + 1) * 512],
                                         start=s == 0, stop=s == SLOTS - 1)
                    last.then_inc(row_used.sem, 1)
                pe.wait_ge(row_used.sem, row_used.due(t, SLOTS + RING))
                pe.sem_inc(tile_end.sem, 1)


def build(nc, A):
    A["proj"] = nc.dram_tensor("proj_rows", (P + TOKENS, P_TOTAL), F32, kind="Internal").ap()
    A["mixed"] = nc.dram_tensor("mixed_rows", (TOKENS, D), F32, kind="Internal").ap()
    project(nc, A)
    mix(nc, A)
    peer(nc, A)


def shape_constants():
    i = np.arange(P)
    tok, col = i[:, None], i[None, :]
    rc = np.zeros((P, 2, RC_COLS), np.float32)
    decay = np.float32(-math.exp(-0.5))
    for v, c in enumerate((32, STEPS)):
        same = tok // c == col // c
        rc[:, v, TRI_I:TRI_I + P] = decay * (same & (tok <= col))
        rc[:, v, TRI_X:TRI_X + P] = decay * (same & (tok < col))
        rc[:, v, TRI_S:TRI_S + P] = decay * (same & (tok > col))
        rc[:, v, IND:IND + P // c] = decay * (tok // c == np.arange(P // c)[None, :])
        rc[:, v, MASK2:MASK2 + P] = same & (tok < col)
        rc[:, v, MASK2 + P:MASK2 + 2 * P] = same & (tok <= col)
        rc[:, v, MASKN:MASKN + P] = same & (tok > col)
    rowm = np.stack([(i // STEPS) % 2 == 0, (i // STEPS) % 2 == 1], 1).astype(np.float32)
    colm = np.broadcast_to(rowm.T[None], (P, 2, P)).astype(np.float32)
    key = np.arange(2 * P)[None, :] - P
    mp = np.zeros((PROMPT_TILES, P, 2 * P), np.float32)
    for t in range(PROMPT_TILES):
        qc, kc = (t * P + tok) // 64, (t * P + key) // 64
        mp[t] = np.where((kc >= qc - 2) & (kc <= qc) & (kc >= 0), 0, NEG)
    cached = np.arange(SAMPLES * P)[None, :] // P == tok // STEPS
    new = col // STEPS == tok // STEPS
    ms = np.where(np.concatenate([cached, new], 1), 0, NEG).astype(np.float32)
    return {
        "ident": np.eye(P, dtype=np.float32),
        "ident2": np.concatenate([np.eye(HD, dtype=np.float32)] * 2, 0),
        "rc": rc, "rowm": rowm, "colm": np.ascontiguousarray(colm),
        "mask_prompt": mp.reshape(-1, 2 * P), "mask_sample": ms,
        "iota": np.arange(NCAND, dtype=np.float32),
    }


OUTPUTS = {
    "y": (TOKENS, D), "shift_prompt": (1, P_RWKV), "wkvT_prompt": (2, HD, PAIRS, HD),
    "k_prompt": (P, 128), "v_prompt": (P, 128), "shift_sample": (SAMPLES, P_RWKV),
    "wkvT_sample": (SAMPLES, 2, HD, PAIRS, HD), "k_sample": (SAMPLES, P, 128), "v_sample": (SAMPLES, P, 128),
}


def kernel(**inputs):
    import concourse.bacc as bacc
    from concourse.bass_utils import run_bass_kernel_spmd

    a = {name: np.asarray(x) for name, x in inputs.items()}
    wkv = a["state_rwkv_wkv"][0].reshape(SAMPLES, PAIRS, 2, HD, HD)
    w_in = a["w_in"][0]
    w_q = w_in[:, Q0:K0].reshape(D, 2, 4, HD).transpose(0, 2, 1, 3).reshape(D, RW)
    w_in = np.concatenate([w_in[:, :Q0], w_q, w_in[:, K0:]], 1)
    arrays = {
        "x": np.concatenate([a["x_prompt"].reshape(-1, D), a["x_sample"].reshape(-1, D)], 0),
        "norm_mix_col": np.ascontiguousarray(a["norm_mix_g"][0].reshape(KC, P).T),
        "w_in": w_in, "w_out": a["w_out"][0], "w_q": a["peer_w_q"][0],
        "mu": a["rwkv_mu"][0], "w0": a["rwkv_w0"][0], "a0": a["rwkv_a0"][0],
        "w2": a["rwkv_w2"][0], "a2": a["rwkv_a2"][0], "g2": a["rwkv_g2"][0],
        "k_k": a["rwkv_k_k"][0], "k_a": a["rwkv_k_a"][0], "r_k": a["rwkv_r_k"][0].reshape(-1),
        "ln_w": a["rwkv_ln_w"][0], "ln_b": a["rwkv_ln_b"][0], "out_g": a["attn_out_g"][0],
        "sinks": a["attn_sinks"][0], "norm_ffn": a["norm_ffn_g"][0], "norm_final": a["norm_final_g"],
        "state_shift": a["state_rwkv_shift"][0].reshape(SAMPLES, P_RWKV),
        "state_wkvT": np.ascontiguousarray(wkv.transpose(0, 2, 4, 1, 3)),
        "cache_k": a["cache_swa_k"][0].reshape(SAMPLES, P, 128),
        "cache_v": a["cache_swa_v"][0].reshape(SAMPLES, P, 128),
        "key1T": np.ascontiguousarray(a["peer_key1"][0].T), "key2T": np.ascontiguousarray(a["peer_key2"][0].T),
        "experts": np.concatenate([a["peer_down"][0], a["peer_up"][0]], 1),
    }
    arrays.update(shape_constants())
    nc = bacc.Bacc("TRN2", target_bir_lowering=False, num_devices=1)
    A = {name: nc.dram_tensor(name, x.shape, F32, kind="ExternalInput").ap() for name, x in arrays.items()}
    A.update({name: nc.dram_tensor(name, shape, F32, kind="ExternalOutput").ap() for name, shape in OUTPUTS.items()})
    build(nc, A)
    r = run_bass_kernel_spmd(nc, [arrays], core_ids=[0]).results[0]
    wkv_p = r["wkvT_prompt"].transpose(2, 0, 3, 1).reshape(1, 1, HEADS, HD, HD)
    wkv_s = r["wkvT_sample"].transpose(0, 3, 1, 4, 2).reshape(1, SAMPLES, HEADS, HD, HD)
    return (r["y"][:SEQ].reshape(1, SEQ, D), r["y"][SEQ:].reshape(SAMPLES, STEPS, D),
            r["shift_prompt"].reshape(1, 1, 1, P_RWKV), np.ascontiguousarray(wkv_p),
            r["k_prompt"].reshape(1, 1, P, 2, HD), r["v_prompt"].reshape(1, 1, P, 2, HD),
            r["shift_sample"].reshape(1, SAMPLES, 1, P_RWKV), np.ascontiguousarray(wkv_s),
            r["k_sample"].reshape(1, SAMPLES, P, 2, HD), r["v_sample"].reshape(1, SAMPLES, P, 2, HD))
```

```python
import math
from contextlib import ExitStack

import numpy as np

import concourse.bass as bass
from concourse import mybir

F32 = mybir.dt.float32
U32 = mybir.dt.uint32
ALU = mybir.AluOpType
ACT = mybir.ActivationFunctionType
AX = mybir.AxisListType

P = 128
D = 1024
SEQ = 1024
SAMPLES, STEPS = 8, 16
TOKENS = SEQ + SAMPLES * STEPS
TILES = TOKENS // P
PROMPT_TILES = SEQ // P
HEADS, HD = 8, 64
RW = HEADS * HD
LORA = 64
GLORA = 160
P_RWKV = 3 * RW + 2 * LORA + GLORA
Q0, K0, V0 = P_RWKV, P_RWKV + RW, P_RWKV + RW + 128
P_TOTAL = V0 + 128
KC = D // P
PAIRS = HEADS // 2
RMS_EPS = 1e-6
LN_EPS = 64e-5
L2_EPS = 1e-12
SCALE = HD ** -0.5
PGROUPS = 6
PG = P_TOTAL // PGROUPS
EXPERTS = 128 * 128
TOPK = 16
SLOTS = 8 * TOPK
TRI_I, TRI_X, TRI_S, IND, MASK2, MASKN, RC_COLS = 0, 128, 256, 384, 392, 648, 776
RKC, LNW, LNB, OUTG, SINK = 0, RW, 2 * RW, 3 * RW, 4 * RW
BC_COLS = 4 * RW + HEADS
NEG = -1e30


DVE_LINKS = 55
DVE_LINKS_SAMPLE = 58
ROUTE_LINKS = 43
END_LINKS = 5


class Signal:

    def __init__(self, ctx, nc, name, per=1, first=None):
        self.sem, self.per, self.first = ctx.enter_context(nc.semaphore(name)), per, first or per

    def due(self, t, k):
        return k if isinstance(t, int) and t == 0 else t * self.per + (self.first - self.per + k)

    def of(self, t):
        return self.first if isinstance(t, int) and t == 0 else self.per


class Link:

    def __init__(self, eng, ended, t):
        self.eng, self.ended, self.t, self.n = eng, ended, t, 0

    def __call__(self, ins):
        self.n += 1
        ins.then_inc(self.ended.sem, 1)
        self.eng.wait_ge(self.ended.sem, self.ended.due(self.t, self.n))

    def hold(self, ins, passed):
        self.n += 1
        ins.then_inc(self.ended.sem, 1)
        self.eng.wait_ge(self.ended.sem, self.ended.due(self.t, self.n)).then_inc(passed.sem, 1)

    def close(self):
        assert self.n == self.ended.of(self.t), (self.ended.sem, self.n, self.ended.of(self.t))


def row(vec):
    return vec.rearrange("(a n) -> a n", a=1)


def project(nc, A):
    with ExitStack() as ctx:
        def sb(name, shape, dt=F32):
            return ctx.enter_context(nc.sbuf_tensor("pj_" + name, shape, dt))

        def signal(name, per=1):
            return Signal(ctx, nc, name, per)

        w = sb("w_in_sb", [P, KC, P_TOTAL])
        gain = sb("gain_col", [P, KC])
        ident = sb("ident_a", [P, P])
        x = sb("x_in", [P, 2, D])
        junk = sb("squares", [P, D])
        ssq = sb("ssq_a", [P, 2])
        rstd = sb("rstd_a", [P, 2])
        hT = sb("hT", [P, 2, KC, P])
        pbuf = sb("proj_sb", [P, 2, P_TOTAL])
        psT = ctx.enter_context(nc.psum_tensor("psT", [P, KC, P], F32))
        psP = ctx.enter_context(nc.psum_tensor("psP", [P, PGROUPS, 512], F32))

        w_in_loaded = signal("w_in_loaded")
        const_loaded = signal("const_a_loaded")
        x_loaded = [signal("x_loaded0", 16), signal("x_loaded1", 16)]
        squared = signal("squared")
        transposed = signal("transposed")
        std_ready = signal("std_ready")
        var_ready = signal("var_ready")
        rstd_ready = signal("rstd_ready")
        hT_ready = signal("hT_ready", 2)
        proj_done = signal("proj_done", PGROUPS)
        act_evac = signal("act_evac", 3)
        dve_evac = signal("dve_evac", 3)
        stored = [signal("proj_stored0", 16), signal("proj_stored1", 16)]
        zeroed = signal("zeroed")

        out = A["proj"]

        block = ctx.enter_context(nc.Block())

        @block.sync
        def _(sp):
            sp.dma_start(ident[:, :], A["ident"]).then_inc(const_loaded.sem, 16)
            sp.dma_start(gain[:, :], A["norm_mix_col"]).then_inc(const_loaded.sem, 16)

            def load(t, par, n):
                sp.wait_ge(squared.sem, t + 1)
                sp.wait_ge(transposed.sem, t + 1)
                sp.dma_start(x[:, par, :], A["x"][bass.ds(t * P, P), :]).then_inc(x_loaded[par].sem, 16)

            load(0, 0, 0)
            load(1, 1, 0)
            for k in range(KC):
                sp.dma_start(w[:, k, :], A["w_in"][k * P:(k + 1) * P, :]).then_inc(w_in_loaded.sem, 16)
            with sp.Fori(1, TILES // 2) as u:
                load(2 * u, 0, u)
                load(2 * u + 1, 1, u)
            load(TILES - 1, 0, 0)
            sp.wait_ge(zeroed.sem, 1)
            sp.dma_start(out[0:P, :], pbuf[:, 1, :]).then_inc(zeroed.sem, 16)
            sp.wait_ge(zeroed.sem, 17)
            sp.wait_ge(stored[0].sem, 16 * (1 + 5))
            sp.wait_ge(stored[1].sem, 16 * (1 + 4))

        @block.scalar
        def _(act):
            act.sem_inc(squared.sem, 2)
            act.sem_inc(act_evac.sem, 3)
            act.sem_inc(stored[0].sem, 16)
            act.sem_inc(stored[1].sem, 16)

            def square(t, par, u):
                act.wait_ge(x_loaded[par].sem, 16 * u + 16)
                act.wait_ge(squared.sem, t + 2)
                act.activation(junk[:, :], x[:, par, :], ACT.Square,
                               accum_out=ssq[:, par:par + 1]).then_inc(squared.sem, 1)
                act.wait_ge(var_ready.sem, t + 1)
                act.activation(rstd[:, par:par + 1], ssq[:, par:par + 1], ACT.Sqrt).then_inc(std_ready.sem, 1)

            def evacuate(t, par, u):
                act.wait_ge(rstd_ready.sem, t + 1)
                act.wait_ge(stored[par].sem, 16 * u + 16)
                for g in range(0, PGROUPS, 2):
                    act.wait_ge(proj_done.sem, 12 + 6 * t + g + 1)
                    act.activation(pbuf[:, par, g * PG:(g + 1) * PG], psP[:, g, 0:PG], ACT.Copy,
                                   scale=rstd[:, par:par + 1]).then_inc(act_evac.sem, 1)
                act.wait_ge(act_evac.sem, 3 * t + 6)
                act.wait_ge(dve_evac.sem, 3 * t + 6)
                act.dma_start(out[bass.ds(P + t * P, P), :], pbuf[:, par, :]).then_inc(stored[par].sem, 16)

            square(0, 0, 0)
            with act.Fori(0, TILES // 2) as u:
                square(2 * u + 1, 1, u)
                evacuate(2 * u, 0, u)
                square(2 * u + 2, 0, u + 1)
                evacuate(2 * u + 1, 1, u)
            evacuate(TILES - 1, 0, TILES // 2)

        @block.vector
        def _(dve):
            dve.sem_inc(dve_evac.sem, 3)
            dve.wait_ge(const_loaded.sem, 32)

            def normalise(t, par, u):
                dve.wait_ge(squared.sem, t + 3)
                dve.tensor_scalar(ssq[:, par:par + 1], ssq[:, par:par + 1], 1.0 / D, RMS_EPS,
                                  ALU.mult, ALU.add).then_inc(var_ready.sem, 1)
                dve.wait_ge(transposed.sem, t + 3)
                dve.wait_ge(proj_done.sem, 6 * t + 6)
                for k in range(0, KC, 4):
                    dve.tensor_tensor(hT[:, par, k:k + 4, :], psT[:, k:k + 4, :],
                                      gain[:, k:k + 4].unsqueeze(2).to_broadcast([P, 4, P]),
                                      ALU.mult).then_inc(hT_ready.sem, 1)
                dve.wait_ge(std_ready.sem, t + 1)
                dve.reciprocal(rstd[:, par:par + 1], rstd[:, par:par + 1]).then_inc(rstd_ready.sem, 1)

            def evacuate(t, par, u):
                dve.wait_ge(rstd_ready.sem, t + 1)
                dve.wait_ge(stored[par].sem, 16 * u + 16)
                for g in range(1, PGROUPS, 2):
                    dve.wait_ge(proj_done.sem, 12 + 6 * t + g + 1)
                    dve.tensor_scalar(pbuf[:, par, g * PG:(g + 1) * PG], psP[:, g, 0:PG],
                                      rstd[:, par:par + 1], None, ALU.mult).then_inc(dve_evac.sem, 1)

            normalise(0, 0, 0)
            with dve.Fori(0, TILES // 2) as u:
                normalise(2 * u + 1, 1, u)
                evacuate(2 * u, 0, u)
                normalise(2 * u + 2, 0, u + 1)
                evacuate(2 * u + 1, 1, u)
            evacuate(TILES - 1, 0, TILES // 2)
            dve.wait_ge(stored[1].sem, 16 * 5)
            dve.memset(pbuf[:, 1, :], 0.0).then_inc(zeroed.sem, 1)

        @block.tensor
        def _(pe):
            pe.sem_inc(transposed.sem, 2)
            pe.sem_inc(proj_done.sem, 12)
            pe.wait_ge(const_loaded.sem, 32)

            def transposes(t, par, u, first=False):
                pe.wait_ge(x_loaded[par].sem, 16 * u + 16)
                if not first:
                    pe.wait_ge(hT_ready.sem, 2 * t)
                for k in range(KC):
                    last = pe.transpose(psT[:, k, :], x[:, par, k * P:(k + 1) * P], ident[:, :])
                last.then_inc(transposed.sem, 1)

            def products(t, par, u):
                pe.wait_ge(hT_ready.sem, 2 * t + 2)
                for g in range(PGROUPS):
                    pe.wait_ge((dve_evac if g % 2 else act_evac).sem, 3 * t + g // 2 + 1)
                    for k in range(KC):
                        last = pe.matmul(psP[:, g, 0:PG], hT[:, par, k, :], w[:, k, g * PG:(g + 1) * PG],
                                         start=k == 0, stop=k == KC - 1)
                    last.then_inc(proj_done.sem, 1)

            transposes(0, 0, 0, True)
            pe.wait_ge(w_in_loaded.sem, 16 * KC)
            with pe.Fori(0, TILES // 2) as u:
                transposes(2 * u + 1, 1, u)
                products(2 * u, 0, u)
                transposes(2 * u + 2, 0, u + 1)
                products(2 * u + 1, 1, u)
            products(TILES - 1, 0, TILES // 2)



CAND = [(0, 1, 16), (1, 1, 8), (2, 1, 5), (3, 1, 4), (4, 1, 3), (5, 3, 2), (8, 8, 1)]
NCAND = sum(n * m for _, n, m in CAND)
DOWN_RING, UP_RING = 6, 8
UP_LAG = 2
DIAGS = 8
WRING = 6
MARKS = 56
ON_VECTOR = [s for s in range(SLOTS) if s % 6 == 5]
ON_PE = [s for s in range(SLOTS) if s % 6 != 5]


class Experts:

    def __init__(self, *work, last=None):
        self.work, self.last, self.mark, self.done = work, last, 0, [0] * len(work)

    def upto(self, mark):
        while self.mark < mark:
            self.mark += 1
            for n, (run, lag) in enumerate(self.work):
                end = SLOTS * max(0, min(self.mark - lag, MARKS)) // MARKS
                if end > self.done[n]:
                    run(range(self.done[n], end))
                    self.done[n] = end

    def finish(self):
        self.upto(MARKS + 2)
        assert all(n == SLOTS for n in self.done)
        self.last()


def mix_and_route(nc, A):
    with ExitStack() as ctx:
        def sb(name, shape, dt=F32):
            return ctx.enter_context(nc.sbuf_tensor("mx_" + name, shape, dt))

        def flag(name, per=1, first=None):
            return Signal(ctx, nc, name, per, first)

        ident = sb("ident", [P, P])
        ident2 = sb("ident2", [P, HD])
        rc = sb("rc", [P, RC_COLS])
        bc = sb("bc", [P, BC_COLS])
        w2a2 = sb("w2a2", [P, 2 * RW])
        g2a = sb("g2a", [P, RW])
        g2b = sb("g2b", [GLORA - P, RW])
        keysT = sb("keysT", [P, 2, P])
        gain_f = sb("gain_final", [P, D])
        iota = sb("iota", [P, NCAND])
        p_cur = sb("p_cur", [P, P_TOTAL])
        xs = sb("xs", [P, P_RWKV])
        lora = sb("lora", [P, 2 * LORA + GLORA])
        loraT = sb("loraT", [P, 3 * P])
        sa = sb("sa", [P, 2, RW])
        gate_r = sb("gate_r", [P, RW])
        ex = sb("ex", [P, 4, RW])
        pc = sb("pc", [P, PAIRS, 8])
        kk = sb("kk", [P, RW])
        k2 = sb("k2", [P, RW])
        work = sb("work", [P, RW])
        work2 = sb("work2", [P, RW])
        small = sb("small", [P, 8, HEADS])
        bonus = sb("bonus", [P, HEADS])
        fac = sb("fac", [P, 4, RW])
        bk = sb("bk", [P, 2, RW])
        arT = sb("arT", [P, PAIRS, 2 * P])
        bkT = sb("bkT", [P, 2, PAIRS, P])
        pqb = sb("pqb", [P, 2, PAIRS, 2 * P])
        pqk = sb("pqk", [P, 2, PAIRS, 2 * P])
        y = sb("y", [P, RW])
        G = sb("G", [P, 4, PAIRS, P])
        H = sb("H", [P, 4, PAIRS, P])
        S = sb("S", [P, PAIRS, P])
        ast = sb("ast", [P, 8, HEADS])
        best = sb("best", [P, 8, TOPK])
        gate = sb("gate", [P, 8, TOPK])
        expert = sb("expert", [P, SLOTS], U32)
        stat = sb("stat", [P, 4])

        def part(buf, at, shape):
            names = "abcd"[:len(buf.shape) - 1]
            flat = buf[tuple([slice(None)] * len(buf.shape))]
            if len(buf.shape) > 2:
                flat = flat.rearrange(f"p {' '.join(names)} -> p ({' '.join(names)})")
            n = math.prod(shape)
            flat = flat[:, at:at + n]
            if len(shape) == 2:
                flat = flat.rearrange("p (a b) -> p a b", b=shape[1])
            if len(shape) == 3:
                flat = flat.rearrange("p (a b c) -> p a b c", b=shape[1], c=shape[2])
            return flat

        bT, kT = bkT[:, 0, :, :], bkT[:, 1, :, :]
        x2, tn = part(bkT, 0, (D,)), part(bk, 0, (D,))
        pw, pwT = part(ex, 0, (2, HEADS, P)), part(fac, 0, (2, HEADS, P))
        X = part(p_cur, 0, (HEADS, P))
        rpT = part(p_cur, HEADS * P, (PAIRS, P))
        mu = part(pqb, 0, (P_RWKV,))
        w0a0 = part(pqk, 0, (2, RW))
        kkc, kac = part(pqk, 2 * RW, (RW,)), part(pqk, 3 * RW, (RW,))
        cat = part(sa, 0, (D,))
        qT = part(kk, 0, (PAIRS, P))
        big = part(pqb, 0, (16, P))
        gain = part(pqb, 0, (D,))
        s12 = part(pqk, 0, (16, P))
        aT = part(arT, 0, (KC, P))
        wring = [part(buf, at, (D,)) for buf, at in ((ex, 0), (ex, D), (fac, 0), (fac, D), (p_cur, 0), (xs, 0))]
        hot = part(pqb, 0, (TOPK, NCAND))
        candb, cidx = part(pqk, 0, (8, NCAND)), part(pqk, 8 * NCAND, (8, NCAND))
        v16, i16f, f16 = (part(fac, n * 256, (16, TOPK)) for n in range(3))
        i16 = i16f.bitcast(U32)
        pos, posf, expf = (part(fac, 768 + n * 128, (8, TOPK)) for n in range(3))
        pos = pos.bitcast(U32)
        gsum = part(fac, 1160, (2, 8))
        cand = part(fac, 1280, (8, NCAND))

        ps = ctx.enter_context(nc.psum_tensor("mx_ps", [P, 8, 512], F32))
        bank = lambda n: ps[:, n, :]
        banks = lambda n, m: ps[:, n:n + m, :].rearrange("p b n -> p (b n)")
        v_of = lambda h: xs[:, 2 * RW + h * HD:2 * RW + (h + 1) * HD]
        GB = (0, 1, 4, 5)

        consts = flag("mix_consts")
        late_consts = flag("late_consts")
        tile_end = flag("mix_tile_end", 4)
        p_in = flag("p_in", 16)
        prev_in = flag("prev_in", 16)
        prev_fix = flag("prev_fix")
        vec_in = flag("vec_in", 16 * 5)
        kv_in = flag("kv_in", 16)
        kv_in2 = flag("kv_in2")
        mask_in = flag("mask_in", 16)
        xs_ready = flag("xs_ready")
        lora_in = flag("lora_in")
        loraT_out = flag("loraT_out")
        loraT_ready = flag("loraT_ready")
        lora_out = flag("lora_out", 2)
        pre_ready = flag("pre_ready")
        sig_ready = flag("sig_ready")
        gate_ready = flag("gate_ready")
        cum_done = flag("cum_done")
        exps_ready = flag("exps_ready", 5)
        kk_ss = flag("kk_ss")
        kk_norm = flag("kk_norm")
        factors = flag("factors", 5)
        facT_out = flag("facT_out", 4)
        facT_ready = flag("facT_ready", 4)
        pb_out = flag("pb_out", 2)
        pk_out = flag("pk_out", 2)
        pqb_ready = flag("pqb_ready", 2)
        pqk_ready = flag("pqk_ready", 2)
        n_out = flag("n_out")
        w0_out = flag("w0_out")
        n_ready = flag("n_ready")
        x0_ready = flag("x0_ready")
        sq_out = flag("sq_out", 4)
        sq_ready = flag("sq_ready", 4)
        ap_out = flag("ap_out", 5)
        x_ready = flag("x_ready", 5)
        rp_out = flag("rp_out")
        y0_out = flag("y0_out")
        rp_ready = flag("rp_ready")
        y0_ready = flag("y0_ready")
        gh_out = flag("gh_out", 4, SAMPLES)
        g_ready = flag("g_ready", 4, SAMPLES)
        h_ready = flag("h_ready", 4, SAMPLES)
        st_out = flag("st_out", 4, SAMPLES)
        s_ready = flag("s_ready", 4, SAMPLES)
        s_loaded = flag("s_loaded")
        s_stored = flag("s_stored")
        gn_var = flag("gn_var")
        gn_std = flag("gn_std")
        y_done = flag("y_done")
        qkT_out = flag("qkT_out")
        qkT_ready = flag("qkT_ready")
        sc_out = flag("sc_out", 8)
        max_ready = flag("max_ready", 8)
        pr_ready = flag("pr_ready", 8)
        prT_out = flag("prT_out", 8)
        prT_ready = flag("prT_ready", 8)
        o_out = flag("o_out", 8)
        sink_in = flag("sink_in")
        sink_exp = flag("sink_exp")
        o_var = flag("o_var")
        o_std = flag("o_std")
        cat_ready = flag("cat_ready")
        dve_link = flag("mix_dve_link", DVE_LINKS, DVE_LINKS_SAMPLE)
        gain_in = flag("gain_in", 16)
        x_in = flag("xr_in", 16)
        w_loaded = [flag(f"w_loaded{n}", 16 * 24 // WRING) for n in range(WRING)]
        w_used = flag("w_used", 24)
        mT_out = flag("mT_out")
        mT_ready = flag("mT_ready")
        wo_out = flag("wo_out")
        ssq_ready = flag("ssq_ready")
        std_ready = flag("std_p_ready")
        tn_ready = flag("tn_ready")
        tT_out = flag("tT_out")
        tT_ready = flag("tT_ready")
        q_out = flag("q_out", 4)
        q_ready = flag("q_ready", 4)
        sco_out = flag("sco_out", 4)
        sco_ready = flag("sco_ready", 4)
        smax_in = flag("smax_in")
        sexp = flag("sexp")
        route_link = flag("route_dve_link", ROUTE_LINKS)
        passed = flag("dve_passed")
        handed = flag("handed")
        down_in = [flag(f"down_in{r}", 16 * len(range(r, SLOTS, DOWN_RING))) for r in range(DOWN_RING)]
        up_in = [flag(f"up_in{r}", 16 * len(range(r, SLOTS, UP_RING))) for r in range(UP_RING)]
        row_free = flag("row_free")
        dotted = flag("dotted", SLOTS)
        gelued = flag("gelued", SLOTS)
        coefs = flag("coefs", SLOTS)
        diags = flag("diags", len(ON_PE))
        pe_used = flag("pe_used", len(ON_PE))
        dve_used = flag("dve_used", len(ON_VECTOR))
        ssq2_ready = flag("ssq2_ready")
        std2_ready = flag("std2_ready")
        y_ready = flag("y_ready")
        y_stored = flag("y_stored", 16)
        end_link = flag("end_dve_link", END_LINKS)

        proj = A["proj"]

        def mix_sync(sp, t, m, src):
            sample = m["sample"]
            sp.wait_ge(tile_end.sem, tile_end.due(t, 4))
            sp.dma_start(p_cur[:, :], proj[bass.ds(P + src, P), :]).then_inc(p_in.sem, 16)
            sp.dma_start(xs[:, :], proj[bass.ds(P - 1 + src, P), 0:P_RWKV]).then_inc(prev_in.sem, 16)
            for dst, name in ((mu, "mu"), (w0a0[:, 0, :], "w0"), (w0a0[:, 1, :], "a0"), (kkc, "k_k"), (kac, "k_a")):
                sp.dma_start(dst, row(A[name]).to_broadcast([P, A[name].shape[0]])).then_inc(vec_in.sem, 16)
            if sample:
                sp.wait_ge(prev_in.sem, prev_in.due(t, 16))
                sp.dma_start(xs[0:P:STEPS, :], A["state_shift"]).then_inc(prev_fix.sem, 16)
                for b in range(SAMPLES):
                    sp.dma_start(m["kv"][:, b, 0:P], A["cache_k"][b]).then_inc(kv_in2.sem, 16)
                    sp.dma_start(m["kv"][:, b, P:2 * P], A["cache_v"][b]).then_inc(kv_in2.sem, 16)
                sp.dma_start(m["kv"][:, SAMPLES, :], proj[bass.ds(P + src, P), K0:P_TOTAL]).then_inc(kv_in.sem, 16)
                sp.dma_start(m["amask"][:, :], A["mask_sample"]).then_inc(mask_in.sem, 16)
                for n in range(SAMPLES):
                    b = 2 * (n % 4) + n // 4
                    if n:
                        sp.wait_ge(s_stored.sem, 32 * n)
                    for o in range(2):
                        sp.dma_start(S[o * HD:(o + 1) * HD, :, o * HD:(o + 1) * HD],
                                     A["state_wkvT"][b, o]).then_inc(s_loaded.sem, 16)
                    sp.wait_ge(s_ready.sem, s_ready.due(t, n + 1))
                    for o in range(2):
                        sp.dma_start(A["wkvT_sample"][b, o],
                                     m["S_next"][o * HD:(o + 1) * HD, :, o * HD:(o + 1) * HD])\
                          .then_inc(s_stored.sem, 16)
            else:
                sp.dma_start(m["kv"][:, :, :], proj[bass.ds(src, 2 * P), K0:P_TOTAL]
                             .rearrange("(n p) c -> p n c", p=P)).then_inc(kv_in.sem, 16)
                sp.dma_start(m["amask"][:, :], A["mask_prompt"][bass.ds(src, P), :]).then_inc(mask_in.sem, 16)

        def mix_scalar(act, t, m, slots):
            sample, nk = m["sample"], m["nk"]
            blocks = lambda ap, n: ap.rearrange("p (a n) -> p a n", n=n)
            act.wait_ge(tile_end.sem, tile_end.due(t, 4))
            slots.upto(1)
            act.wait_ge(xs_ready.sem, xs_ready.due(t, 1))
            act.activation(lora[:, 0:LORA], xs[:, 3 * RW:3 * RW + LORA], ACT.Tanh)
            act.activation(lora[:, LORA:2 * LORA], xs[:, 3 * RW + LORA:3 * RW + 2 * LORA], ACT.Copy)
            act.activation(lora[:, 2 * LORA:], xs[:, 3 * RW + 2 * LORA:P_RWKV], ACT.Sigmoid)\
               .then_inc(lora_in.sem, 1)
            slots.upto(2)
            act.wait_ge(loraT_out.sem, loraT_out.due(t, 1))
            act.activation(loraT[:, 0:2 * P], ps[:, 0, 0:2 * P], ACT.Copy)
            act.activation(loraT[0:GLORA - P, 2 * P:3 * P], ps[0:GLORA - P, 0, 2 * P:3 * P], ACT.Copy)\
               .then_inc(loraT_ready.sem, 1)
            slots.upto(3)
            act.wait_ge(kk_ss.sem, kk_ss.due(t, 1))
            act.activation(small[:, 1, :], small[:, 0, :], ACT.Sqrt).then_inc(kk_norm.sem, 1)
            act.wait_ge(pre_ready.sem, pre_ready.due(t, 1))
            act.activation(sa[:, :, :], sa[:, :, :], ACT.Sigmoid).then_inc(sig_ready.sem, 1)
            act.wait_ge(lora_out.sem, lora_out.due(t, 2))
            act.activation(gate_r[:, :], bank(3), ACT.Copy).then_inc(gate_ready.sem, 1)
            slots.upto(5)
            act.wait_ge(cum_done.sem, cum_done.due(t, 1))
            act.activation(ex[:, 1, :], bank(4), ACT.Exp).then_inc(exps_ready.sem, 1)
            act.activation(ex[:, 2, :], bank(5), ACT.Exp, scale=-1.0).then_inc(exps_ready.sem, 1)
            act.activation(ex[:, 0, :], bank(5), ACT.Exp).then_inc(exps_ready.sem, 1)
            act.activation(ex[:, 3, :], bank(0), ACT.Exp).then_inc(exps_ready.sem, 1)
            act.activation(pc[:, :, :], blocks(ps[:, 1, 0:32], 8), ACT.Exp).then_inc(exps_ready.sem, 1)
            slots.upto(7)
            for n, dst in enumerate((arT[:, :, 0:P], arT[:, :, P:2 * P], bT, kT)):
                act.wait_ge(facT_out.sem, facT_out.due(t, n + 1))
                act.activation(dst, blocks(bank(2 + n), P), ACT.Copy).then_inc(facT_ready.sem, 1)
            for o in range(2):
                act.activation(X[:, 4 * o:4 * o + 4, 0:HD],
                               fac[:, 0, :].rearrange("p (q o c) -> p o q c", o=2, c=HD)[:, o], ACT.Copy)
            slots.upto(11)
            act.wait_ge(w0_out.sem, w0_out.due(t, 1))
            act.activation(X[:, :, HD:P], blocks(bank(4), HD), ACT.Copy).then_inc(x0_ready.sem, 1)
            for i in range(4):
                slots.upto(12 + i)
                act.wait_ge(sq_out.sem, sq_out.due(t, i + 1))
                if i:
                    act.wait_ge(ap_out.sem, ap_out.due(t, i))
                ins = act.activation(pwT[:, i % 2, :, :], blocks(banks(2, 2), P), ACT.Copy)
                if i < 3:
                    ins = act.activation(pw[:, (i + 1) % 2, :, :], blocks(banks(4, 2), P), ACT.Copy)
                ins.then_inc(sq_ready.sem, 1)
            slots.upto(17)
            act.wait_ge(y0_out.sem, y0_out.due(t, 1))
            act.activation(y[:, :], bank(3), ACT.Copy).then_inc(y0_ready.sem, 1)
            for n in range(m["maps"]):
                slots.upto(18 + n)
                if n >= 4:
                    act.wait_ge(st_out.sem, st_out.due(t, n - 3))
                    act.wait_ge(s_ready.sem, s_ready.due(t, n - 3))
                act.wait_ge(g_ready.sem, g_ready.due(t, n + 1))
                for o in range(2):
                    q = slice(o * HD, (o + 1) * HD)
                    ins = act.activation(H[q, n % 4, :, q], blocks(ps[q, GB[n % 4], 256:512], HD), ACT.Copy)
                ins.then_inc(h_ready.sem, 1)
            slots.upto(26)
            act.wait_ge(gn_var.sem, gn_var.due(t, 1))
            act.activation(small[:, 5, :], small[:, 4, :], ACT.Sqrt).then_inc(gn_std.sem, 1)
            slots.upto(28)
            act.wait_ge(qkT_out.sem, qkT_out.due(t, 1))
            act.activation(qT[:, :, :], blocks(bank(1), P), ACT.Copy)
            act.activation(m["keyT"], banks(m["kt_bank"], 3)[:, 0:nk * P], ACT.Copy).then_inc(qkT_ready.sem, 1)
            for h in range(HEADS):
                d = h % m["deep"]
                slots.upto(29 + h)
                act.wait_ge(max_ready.sem, max_ready.due(t, h + 1))
                act.activation(m["sc"][d], m["sc"][d], ACT.Exp, bias=ast[:, 2, h:h + 1],
                               scale=SCALE, accum_out=ast[:, 3, h:h + 1]).then_inc(pr_ready.sem, 1)
                act.wait_ge(prT_out.sem, prT_out.due(t, h + 1))
                act.activation(m["prT"][d], banks(m["prT_bank"][d], m["sc_banks"])[:, 0:nk * P],
                               ACT.Copy).then_inc(prT_ready.sem, 1)
            slots.upto(37)
            act.wait_ge(sink_in.sem, sink_in.due(t, 1))
            act.activation(ast[:, 4, :], ast[:, 4, :], ACT.Exp).then_inc(sink_exp.sem, 1)
            slots.upto(38)
            act.wait_ge(o_var.sem, o_var.due(t, 1))
            act.activation(ast[:, 6, :], ast[:, 6, :], ACT.Sqrt).then_inc(o_std.sem, 1)

        def mix_vector(dve, t, m, slots):
            link = Link(dve, dve_link, t)
            sample, nk = m["sample"], m["nk"]
            B = lambda c, n: bc[:, c:c + n]
            h3 = lambda ap: ap.rearrange("p (h c) -> p h c", c=HD)
            blocks = lambda ap, n: ap.rearrange("p (a n) -> p a n", n=n)
            per_head = lambda ap: ap.unsqueeze(2).to_broadcast([P, HEADS, HD])
            r, k, vv = (xs[:, n * RW:(n + 1) * RW] for n in range(3))
            slots.upto(1)
            dve.wait_ge(p_in.sem, p_in.due(t, 16))
            dve.wait_ge(prev_in.sem, prev_in.due(t, 16))
            dve.wait_ge(vec_in.sem, vec_in.due(t, 16 * 5))
            if sample:
                dve.wait_ge(prev_fix.sem, 16)
            link(dve.tensor_tensor(xs[:, :], xs[:, :], p_cur[:, 0:P_RWKV], ALU.subtract))
            link(dve.tensor_tensor(xs[:, :], xs[:, :], mu, ALU.mult))
            dve.tensor_tensor(xs[:, :], xs[:, :], p_cur[:, 0:P_RWKV], ALU.add).then_inc(xs_ready.sem, 1)
            dve.wait_ge(xs_ready.sem, xs_ready.due(t, 1))
            link(dve.tensor_tensor(kk[:, :], k, kkc, ALU.mult))
            link(dve.tensor_tensor(work[:, :], kk[:, :], kk[:, :], ALU.mult))
            dve.tensor_reduce(small[:, 0, :], h3(work[:, :]), AX.X, ALU.add).then_inc(kk_ss.sem, 1)
            slots.upto(3)
            dve.wait_ge(lora_out.sem, lora_out.due(t, 1))
            dve.tensor_tensor(sa[:, :, :], ps[:, 1:3, :], w0a0, ALU.add).then_inc(pre_ready.sem, 1)
            dve.wait_ge(kk_norm.sem, kk_norm.due(t, 1))
            link(dve.tensor_scalar(small[:, 1, :], small[:, 1, :], L2_EPS, None, ALU.max))
            link(dve.reciprocal(small[:, 1, :], small[:, 1, :]))
            link(dve.tensor_tensor(h3(kk[:, :]), h3(kk[:, :]), per_head(small[:, 1, :]), ALU.mult))
            slots.upto(4)
            dve.wait_ge(sig_ready.sem, sig_ready.due(t, 1))
            a = sa[:, 1, :]
            link(dve.scalar_tensor_tensor(out=work[:, :], in0=a, scalar=-1.0, in1=kac, op0=ALU.add, op1=ALU.mult))
            link(dve.scalar_tensor_tensor(out=k2[:, :], in0=work[:, :], scalar=1.0, in1=k, op0=ALU.add, op1=ALU.mult))
            link(dve.tensor_tensor(work2[:, :], kk[:, :], a, ALU.mult))
            link(dve.tensor_tensor(work[:, :], r, k2[:, :], ALU.mult))
            link(dve.tensor_tensor(work[:, :], work[:, :], B(RKC, RW), ALU.mult))
            dve.tensor_reduce(bonus[:, :], h3(work[:, :]), AX.X, ALU.add)
            slots.upto(5)
            dve.wait_ge(exps_ready.sem, exps_ready.due(t, 1))
            dve.scalar_tensor_tensor(out=fac[:, 0, :], in0=kk[:, :], scalar=-1.0, in1=ex[:, 1, :],
                                     op0=ALU.mult, op1=ALU.mult).then_inc(factors.sem, 1)
            dve.wait_ge(exps_ready.sem, exps_ready.due(t, 3))
            dve.tensor_tensor(fac[:, 1, :], r, ex[:, 0, :], ALU.mult).then_inc(factors.sem, 1)
            dve.tensor_tensor(fac[:, 2, :], work2[:, :], ex[:, 2, :], ALU.mult).then_inc(factors.sem, 1)
            dve.tensor_tensor(fac[:, 3, :], k2[:, :], ex[:, 2, :], ALU.mult).then_inc(factors.sem, 1)
            slots.upto(6)
            dve.wait_ge(exps_ready.sem, exps_ready.due(t, 4))
            for n, f in enumerate((work2, k2)):
                if sample:
                    link(dve.tensor_tensor(bk[:, n, :], f[:, :], ex[:, 3, :], ALU.mult))
                    dve.tensor_scalar(m["bk_odd"][:, n, :], bk[:, n, :], m["rowm"][:, 1:2], None, ALU.mult)
                    ins = dve.tensor_scalar(bk[:, n, :], bk[:, n, :], m["rowm"][:, 0:1], None, ALU.mult)
                else:
                    ins = dve.tensor_tensor(bk[:, n, :], f[:, :], ex[:, 3, :], ALU.mult)
            ins.then_inc(factors.sem, 1)
            m2 = rc[:, MASK2:MASK2 + 2 * P].unsqueeze(1).to_broadcast([P, PAIRS, 2 * P])
            at = 8
            for dst, out, ready, first in ((pqb, pb_out, pqb_ready, (0, 2)), (pqk, pk_out, pqk_ready, (4, 0))):
                for o in range(2):
                    slots.upto(at)
                    at += 1 if o == 0 else 0
                    dve.wait_ge(out.sem, out.due(t, o + 1))
                    dve.tensor_tensor(dst[:, o, :, :], blocks(banks(first[o], 2), 2 * P), m2, ALU.mult)\
                       .then_inc(ready.sem, 1)
            slots.upto(10)
            dve.wait_ge(n_out.sem, n_out.due(t, 1))
            dve.tensor_tensor(pw[:, 0, :, :], blocks(banks(2, 2), P),
                              rc[:, MASKN:MASKN + P].unsqueeze(1).to_broadcast([P, HEADS, P]), ALU.mult)\
               .then_inc(n_ready.sem, 1)
            for i in range(5):
                slots.upto(12 + i)
                if i == 0:
                    dve.wait_ge(x0_ready.sem, x0_ready.due(t, 1))
                dve.wait_ge(ap_out.sem, ap_out.due(t, i + 1))
                dve.tensor_tensor(X, X, blocks(banks(0, 2), P), ALU.add).then_inc(x_ready.sem, 1)
            slots.upto(17)
            dve.wait_ge(rp_out.sem, rp_out.due(t, 1))
            ins = dve.tensor_tensor(rpT, blocks(bank(2), P), arT[:, :, P:2 * P], ALU.add)
            if sample:
                link(ins)
                cm = lambda e: m["colm"][:, e, :].unsqueeze(1).to_broadcast([P, PAIRS, P])
                dve.tensor_tensor(m["rpT_odd"][:, :, :], rpT, cm(1), ALU.mult)
                ins = dve.tensor_tensor(rpT, rpT, cm(0), ALU.mult)
            ins.then_inc(rp_ready.sem, 1)

            def state_map(n):
                dve.wait_ge(gh_out.sem, gh_out.due(t, n + 1))
                b = m["column"](n)
                for o in range(2):
                    s = slice(o * HD, (o + 1) * HD)
                    for q in range(PAIRS):
                        ins = dve.scalar_tensor_tensor(out=G[s, n % 4, q, s], in0=ident2[s, :],
                                                       scalar=pc[s, q, b:b + 1],
                                                       in1=ps[s, GB[n % 4], q * HD:(q + 1) * HD],
                                                       op0=ALU.mult, op1=ALU.add)
                ins.then_inc(g_ready.sem, 1)

            def next_state(n):
                dve.wait_ge(st_out.sem, st_out.due(t, n + 1))
                dve.wait_ge(h_ready.sem, h_ready.due(t, n + 1))
                if sample and n:
                    dve.wait_ge(s_stored.sem, 32 * n)
                dve.tensor_tensor(m["S_next"][:, :, :], blocks(bank(2 + n % 2), P), H[:, n % 4, :, :], ALU.add)\
                   .then_inc(s_ready.sem, 1)

            for n in range(4):
                slots.upto(18 + n)
                state_map(n)
            for n in range(m["maps"]):
                slots.upto(22 + n)
                next_state(n)
                if n + 4 < m["maps"]:
                    state_map(n + 4)
            dve.wait_ge(y0_ready.sem, y0_ready.due(t, 1))
            link(dve.tensor_tensor(y[:, :], y[:, :], bank(m["y_bank"]), ALU.add))
            link(dve.tensor_reduce(small[:, 2, :], h3(y[:, :]), AX.X, ALU.add))
            link(dve.tensor_scalar(small[:, 2, :], small[:, 2, :], 1.0 / HD, None, ALU.mult))
            link(dve.tensor_tensor(h3(y[:, :]), h3(y[:, :]), per_head(small[:, 2, :]), ALU.subtract))
            link(dve.tensor_tensor(work[:, :], y[:, :], y[:, :], ALU.mult))
            link(dve.tensor_reduce(small[:, 3, :], h3(work[:, :]), AX.X, ALU.add))
            dve.tensor_scalar(small[:, 4, :], small[:, 3, :], 1.0 / HD, LN_EPS, ALU.mult, ALU.add)\
               .then_inc(gn_var.sem, 1)
            link(dve.tensor_tensor(h3(work[:, :]), per_head(bonus[:, :]), h3(vv), ALU.mult))
            slots.upto(27)
            dve.wait_ge(gn_std.sem, gn_std.due(t, 1))
            link(dve.reciprocal(small[:, 5, :], small[:, 5, :]))
            link(dve.tensor_tensor(h3(y[:, :]), h3(y[:, :]), per_head(small[:, 5, :]), ALU.mult))
            link(dve.tensor_tensor(y[:, :], y[:, :], B(LNW, RW), ALU.mult))
            link(dve.tensor_tensor(y[:, :], y[:, :], B(LNB, RW), ALU.add))
            link(dve.tensor_tensor(y[:, :], y[:, :], work[:, :], ALU.add))
            dve.wait_ge(gate_ready.sem, gate_ready.due(t, 1))
            dve.tensor_tensor(cat[:, 0:RW], y[:, :], gate_r[:, :], ALU.mult).then_inc(y_done.sem, 1)
            dve.wait_ge(mask_in.sem, mask_in.due(t, 16))
            for h in range(HEADS):
                d = h % m["deep"]
                slots.upto(29 + h)
                dve.wait_ge(sc_out.sem, sc_out.due(t, h + 1))
                if h >= m["deep"]:
                    dve.wait_ge(prT_out.sem, prT_out.due(t, h + 1 - m["deep"]))
                link(dve.tensor_tensor(m["sc"][d], banks(m["sc_bank"][d], m["sc_banks"])[:, 0:nk * P],
                                       m["amask"][:, :], ALU.add))
                link(dve.tensor_reduce(ast[:, 0, h:h + 1], m["sc"][d], AX.X, ALU.max))
                link(dve.tensor_scalar(ast[:, 1, h:h + 1], ast[:, 0, h:h + 1], SCALE, bc[:, SINK + h:SINK + h + 1],
                                       ALU.mult, ALU.max))
                dve.tensor_scalar(ast[:, 2, h:h + 1], ast[:, 1, h:h + 1], -1.0, None, ALU.mult)\
                   .then_inc(max_ready.sem, 1)
            slots.upto(37)
            dve.tensor_tensor(ast[:, 4, :], B(SINK, HEADS), ast[:, 1, :], ALU.subtract).then_inc(sink_in.sem, 1)
            dve.wait_ge(sink_exp.sem, sink_exp.due(t, 1))
            link(dve.tensor_tensor(ast[:, 5, :], ast[:, 3, :], ast[:, 4, :], ALU.add))
            link(dve.reciprocal(ast[:, 5, :], ast[:, 5, :]))
            dve.wait_ge(o_out.sem, o_out.due(t, 8))
            link(dve.tensor_tensor(h3(y[:, :]), h3(bank(m["o_bank"])), per_head(ast[:, 5, :]), ALU.mult))
            link(dve.tensor_tensor(work[:, :], y[:, :], y[:, :], ALU.mult))
            link(dve.tensor_reduce(ast[:, 6, :], h3(work[:, :]), AX.X, ALU.add))
            dve.tensor_scalar(ast[:, 6, :], ast[:, 6, :], 1.0 / HD, RMS_EPS, ALU.mult, ALU.add)\
               .then_inc(o_var.sem, 1)
            slots.upto(38)
            dve.wait_ge(o_std.sem, o_std.due(t, 1))
            link(dve.reciprocal(ast[:, 7, :], ast[:, 6, :]))
            link(dve.tensor_tensor(h3(y[:, :]), h3(y[:, :]), per_head(ast[:, 7, :]), ALU.mult))
            dve.tensor_tensor(cat[:, RW:D], y[:, :], B(OUTG, RW), ALU.mult).then_inc(cat_ready.sem, 1)
            link.close()

        def mix_tensor(pe, t, m, slots):
            sample, nk = m["sample"], m["nk"]
            half = lambda o: slice(o * HD, (o + 1) * HD)
            pe.wait_ge(tile_end.sem, tile_end.due(t, 4))
            slots.upto(2)
            pe.wait_ge(lora_in.sem, lora_in.due(t, 1))
            pe.transpose(ps[:, 0, 0:P], lora[:, 0:P], ident[:, :])
            pe.transpose(ps[:, 0, P:2 * P], lora[:, P:2 * P], ident[:, :])
            pe.transpose(ps[0:GLORA - P, 0, 2 * P:3 * P], lora[:, 2 * P:], ident[:, :]).then_inc(loraT_out.sem, 1)
            slots.upto(3)
            pe.wait_ge(loraT_ready.sem, loraT_ready.due(t, 1))
            pe.matmul(bank(1), loraT[:, 0:P], w2a2[:, 0:RW], start=True, stop=True)
            pe.matmul(bank(2), loraT[:, 0:P], w2a2[:, RW:], start=True, stop=True).then_inc(lora_out.sem, 1)
            pe.matmul(bank(3), loraT[:, P:2 * P], g2a[:, :], start=True, stop=False)
            pe.matmul(bank(3), loraT[0:GLORA - P, 2 * P:3 * P], g2b[:, :], start=False, stop=True)\
              .then_inc(lora_out.sem, 1)
            slots.upto(5)
            pe.wait_ge(sig_ready.sem, sig_ready.due(t, 1))
            pe.matmul(bank(4), rc[:, TRI_X:TRI_X + P], sa[:, 0, :], start=True, stop=True)
            pe.matmul(bank(5), rc[:, TRI_I:TRI_I + P], sa[:, 0, :], start=True, stop=True)
            pe.matmul(bank(0), rc[:, TRI_S:TRI_S + P], sa[:, 0, :], start=True, stop=True)
            for q in range(PAIRS):
                last = pe.matmul(ps[:, 1, 8 * q:8 * q + 8], sa[:, 0, q * P:(q + 1) * P], rc[:, IND:IND + 8],
                                 start=True, stop=True)
            last.then_inc(cum_done.sem, 1)
            slots.upto(7)
            pe.wait_ge(gate_ready.sem, gate_ready.due(t, 1))
            pe.wait_ge(exps_ready.sem, exps_ready.due(t, 5))
            pe.wait_ge(factors.sem, factors.due(t, 5))
            for n in range(4):
                for q in range(PAIRS):
                    last = pe.transpose(ps[:, 2 + n, q * P:(q + 1) * P], fac[:, n, q * P:(q + 1) * P], ident[:, :])
                last.then_inc(facT_out.sem, 1)
            slots.upto(8)
            pe.wait_ge(facT_ready.sem, facT_ready.due(t, 4))

            def products(left, o, first, done):
                for q in range(PAIRS):
                    last = pe.matmul(ps[:, first + q // 2, (q % 2) * 256:(q % 2) * 256 + 256],
                                     left[half(o), q, :], arT[half(o), q, :], start=True, stop=True)
                last.then_inc(done.sem, 1)

            products(bT, 0, 0, pb_out)
            products(bT, 1, 2, pb_out)
            slots.upto(9)
            products(kT, 0, 4, pk_out)
            pe.wait_ge(pqb_ready.sem, pqb_ready.due(t, 1))
            products(kT, 1, 0, pk_out)
            pe.wait_ge(pqb_ready.sem, pqb_ready.due(t, 2))
            slots.upto(10)
            for o in range(2):
                for q in range(PAIRS):
                    last = pe.matmul(ps[:, 2 + o, q * P:(q + 1) * P], arT[half(o), q, 0:P], bT[half(o), q, :],
                                     start=True, stop=True)
            last.then_inc(n_out.sem, 1)
            slots.upto(11)
            pe.wait_ge(pqk_ready.sem, pqk_ready.due(t, 2))
            for o in range(2):
                for q in range(PAIRS):
                    last = pe.matmul(ps[:, 4, (4 * o + q) * HD:(4 * o + q + 1) * HD], pqk[:, o, q, 0:P],
                                     v_of(2 * q + o), start=True, stop=True)
            last.then_inc(w0_out.sem, 1)
            pe.wait_ge(n_ready.sem, n_ready.due(t, 1))
            for i in range(5):
                slots.upto(12 + i)
                if i:
                    pe.wait_ge(sq_ready.sem, sq_ready.due(t, i))
                    pe.wait_ge(x_ready.sem, x_ready.due(t, i))
                else:
                    pe.wait_ge(x0_ready.sem, x0_ready.due(t, 1))
                powT = lambda h: pqb[:, h // 4, h % 4, 0:P] if i == 0 else pwT[:, (i - 1) % 2, h, :]
                if i < 4:
                    for h in range(HEADS):
                        last = pe.matmul(ps[:, 2 + h // 4, (h % 4) * P:(h % 4 + 1) * P], pw[:, i % 2, h, :], powT(h),
                                         start=True, stop=True)
                    for h in range(HEADS if i < 3 else 0):
                        last = pe.matmul(ps[:, 4 + h // 4, (h % 4) * P:(h % 4 + 1) * P], powT(h), pw[:, i % 2, h, :],
                                         start=True, stop=True)
                    last.then_inc(sq_out.sem, 1)
                for h in range(HEADS):
                    last = pe.matmul(ps[:, h // 4, (h % 4) * P:(h % 4 + 1) * P], powT(h), X[:, h, :],
                                     start=True, stop=True)
                last.then_inc(ap_out.sem, 1)
            slots.upto(17)
            pe.wait_ge(x_ready.sem, x_ready.due(t, 5))
            for o in range(2):
                for q in range(PAIRS):
                    last = pe.matmul(ps[half(o), 2, q * P:(q + 1) * P], X[:, 4 * o + q, 0:HD], pqb[:, o, q, P:2 * P],
                                     start=True, stop=True)
            last.then_inc(rp_out.sem, 1)
            for h in range(HEADS):
                o, q = h % 2, h // 2
                pe.matmul(ps[:, 3, h * HD:(h + 1) * HD], pqb[:, o, q, P:2 * P], X[:, 4 * o + q, HD:P],
                          start=True, stop=False)
                last = pe.matmul(ps[:, 3, h * HD:(h + 1) * HD], pqk[:, o, q, P:2 * P], v_of(h),
                                 start=False, stop=True)
            last.then_inc(y0_out.sem, 1)

            def transition(n):
                b = n % 4
                factor = m["bk_odd"] if n >= 4 else bk
                rows = slice(32 * b, 32 * b + 32)
                for h in range(HEADS):
                    o, q = h % 2, h // 2
                    beta = factor[rows, 0, h * HD:(h + 1) * HD]
                    kappa = factor[rows, 1, h * HD:(h + 1) * HD]
                    value = xs[rows, 2 * RW + h * HD:2 * RW + (h + 1) * HD]
                    tp = (32 * b, o * HD)
                    pe.matmul(ps[half(o), GB[b], q * HD:(q + 1) * HD], X[rows, 4 * o + q, 0:HD], beta,
                              start=True, stop=True, tile_position=tp)
                    pe.matmul(ps[half(o), GB[b], 256 + q * HD:256 + (q + 1) * HD], beta, X[rows, 4 * o + q, HD:P],
                              start=True, stop=False, tile_position=tp)
                    last = pe.matmul(ps[half(o), GB[b], 256 + q * HD:256 + (q + 1) * HD], kappa, value,
                                     start=False, stop=True, tile_position=tp)
                last.then_inc(gh_out.sem, 1)

            def state_product(n):
                for q in range(PAIRS):
                    last = pe.matmul(ps[:, 2 + n % 2, q * P:(q + 1) * P], G[:, n % 4, q, :], S[:, q, :],
                                     start=True, stop=True)
                last.then_inc(st_out.sem, 1)

            for n in range(4):
                slots.upto(18 + n)
                transition(n)
            pe.wait_ge(rp_ready.sem, rp_ready.due(t, 1))
            pe.wait_ge(y0_ready.sem, y0_ready.due(t, 1))
            y_bank = m["y_bank"]
            for n in range(m["maps"]):
                slots.upto(22 + n)
                b, odd = n % 4, n >= 4
                rows = slice(32 * b, 32 * b + 32)
                pe.wait_ge(g_ready.sem, g_ready.due(t, n + 1))
                pe.wait_ge(h_ready.sem, h_ready.due(t, n + 1))
                if sample:
                    pe.wait_ge(s_loaded.sem, 32 * (n + 1))
                    if n >= 2:
                        pe.wait_ge(s_ready.sem, s_ready.due(t, n - 1))
                elif n:
                    pe.wait_ge(s_ready.sem, s_ready.due(t, n))
                for q in range(PAIRS):
                    pe.matmul(ps[rows, y_bank, q * P:(q + 1) * P], (m["rpT_odd"] if odd else rpT)[:, q, rows],
                              S[:, q, :], start=not sample or (q == 0 and not odd), stop=not sample or odd,
                              skip_group_check=sample)
                state_product(n)
                if n + 4 < m["maps"]:
                    transition(n + 4)
            slots.upto(28)
            pe.wait_ge(kv_in.sem, kv_in.due(t, 16))
            if sample:
                pe.wait_ge(kv_in2.sem, 16 * 2 * SAMPLES)
                pe.wait_ge(y_done.sem, y_done.due(t, 1))
            pe.wait_ge(s_ready.sem, s_ready.due(t, m["maps"]))
            for j in range(4):
                pe.transpose(ps[:, 1, j * P:(j + 1) * P], p_cur[:, Q0 + j * P:Q0 + (j + 1) * P], ident[:, :])
            for n in range(nk):
                last = pe.transpose(ps[:, m["kt_bank"] + n // 4, (n % 4) * P:(n % 4 + 1) * P],
                                    m["kv"][:, n, 0:P], ident[:, :])
            last.then_inc(qkT_out.sem, 1)

            def scores(h):
                g = h // 4
                if h >= m["deep"]:
                    pe.wait_ge(max_ready.sem, max_ready.due(t, h + 1 - m["deep"]))
                for n in range(0, nk, 4):
                    w = min(4, nk - n) * P
                    last = pe.matmul(ps[:, m["sc_bank"][h % m["deep"]] + n // 4, 0:w], qT[half(g), h % 4, :],
                                     m["keyT"][half(g), n * P:n * P + w], start=True, stop=True)
                last.then_inc(sc_out.sem, 1)

            pe.wait_ge(qkT_ready.sem, qkT_ready.due(t, 1))
            scores(0)
            pe.wait_ge(y_done.sem, y_done.due(t, 1))
            for h in range(HEADS):
                g, d = h // 4, h % m["deep"]
                if m["deep"] > 1 and h + 1 < HEADS:
                    scores(h + 1)
                slots.upto(29 + h)
                pe.wait_ge(pr_ready.sem, pr_ready.due(t, h + 1))
                if h >= m["deep"]:
                    pe.wait_ge(prT_ready.sem, prT_ready.due(t, h + 1 - m["deep"]))
                for n in range(nk):
                    last = pe.transpose(ps[:, m["prT_bank"][d] + n // 4, (n % 4) * P:(n % 4 + 1) * P],
                                        m["sc"][d][:, n * P:(n + 1) * P], ident[:, :])
                last.then_inc(prT_out.sem, 1)
                if m["deep"] == 1 and h + 1 < HEADS:
                    scores(h + 1)
                pe.wait_ge(prT_ready.sem, prT_ready.due(t, h + 1))
                for n in range(nk):
                    last = pe.matmul(ps[:, m["o_bank"], h * HD:(h + 1) * HD], m["prT"][d][:, n * P:(n + 1) * P],
                                     m["kv"][:, n, P + g * HD:P + (g + 1) * HD], start=n == 0, stop=n == nk - 1)
                last.then_inc(o_out.sem, 1)

        def w_block(n):
            return A["w_out"][n * P:(n + 1) * P, :] if n < KC else A["w_q"][n - KC]

        def route_sync(sp, t, xrow):
            sp.wait_ge(y_done.sem, y_done.due(t, 1))
            sp.dma_start(x2[:, :], A["x"][bass.ds(xrow, P), :]).then_inc(x_in.sem, 16)
            sp.dma_start(gain, row(A["norm_ffn"]).to_broadcast([P, D])).then_inc(gain_in.sem, 16)
            for n in range(24):
                if n >= WRING:
                    sp.wait_ge(w_used.sem, w_used.due(t, n - WRING + 1))
                sp.dma_start(wring[n % WRING], w_block(n)).then_inc(w_loaded[n % WRING].sem, 16)

        def route_scalar(act, t, slots):
            blocks = lambda ap: ap.rearrange("p (a n) -> p a n", n=P)
            slots.upto(39)
            act.wait_ge(mT_out.sem, mT_out.due(t, 1))
            act.activation(aT, blocks(banks(0, 2)), ACT.Copy).then_inc(mT_ready.sem, 1)
            slots.upto(42)
            act.wait_ge(ssq_ready.sem, ssq_ready.due(t, 1))
            act.activation(stat[:, 1:2], stat[:, 1:2], ACT.Sqrt).then_inc(std_ready.sem, 1)
            slots.upto(43)
            act.wait_ge(tT_out.sem, tT_out.due(t, 1))
            act.activation(aT, blocks(banks(0, 2)), ACT.Copy).then_inc(tT_ready.sem, 1)
            for g in range(4):
                slots.upto(44 + g)
                act.wait_ge(q_out.sem, q_out.due(t, g + 1))
                act.activation(s12[:, 4 * g:4 * g + 4, :], blocks(bank(2 + g)), ACT.Copy).then_inc(q_ready.sem, 1)
            slots.upto(48)
            for g in range(4):
                act.wait_ge(sco_out.sem, sco_out.due(t, g + 1))
                act.activation(s12[:, 4 * g:4 * g + 4, :], blocks(bank(g)), ACT.Copy).then_inc(sco_ready.sem, 1)
            slots.upto(55)
            act.wait_ge(smax_in.sem, smax_in.due(t, 1))
            act.activation(gate[:, :, :], gate[:, :, :], ACT.Exp).then_inc(sexp.sem, 1)
            act.wait_ge(sexp.sem, sexp.due(t, 1))

        def route_tensor(pe, t, slots):
            def weights(n):
                pe.wait_ge(w_loaded[n % WRING].sem, w_loaded[n % WRING].due(t, 16 * (n // WRING + 1)))
                return wring[n % WRING]

            slots.upto(39)
            pe.wait_ge(cat_ready.sem, cat_ready.due(t, 1))
            for k in range(KC):
                last = pe.transpose(ps[:, k // 4, (k % 4) * P:(k % 4 + 1) * P], cat[:, k * P:(k + 1) * P], ident[:, :])
            last.then_inc(mT_out.sem, 1)
            slots.upto(40)
            pe.wait_ge(mT_ready.sem, mT_ready.due(t, 1))
            for k in range(KC):
                if k == 4:
                    slots.upto(41)
                w = weights(k)
                for n in range(2):
                    last = pe.matmul(bank(2 + n), aT[:, k, :], w[:, n * 512:(n + 1) * 512],
                                     start=k == 0, stop=k == KC - 1)
                last.then_inc(w_used.sem, 1)
            pe.wait_ge(w_used.sem, w_used.due(t, KC))
            pe.sem_inc(wo_out.sem, 1)
            slots.upto(43)
            pe.wait_ge(tn_ready.sem, tn_ready.due(t, 1))
            for k in range(KC):
                last = pe.transpose(ps[:, k // 4, (k % 4) * P:(k % 4 + 1) * P], tn[:, k * P:(k + 1) * P], ident[:, :])
            last.then_inc(tT_out.sem, 1)
            slots.upto(44)
            pe.wait_ge(tT_ready.sem, tT_ready.due(t, 1))
            for g in range(4):
                slots.upto(44 + g)
                for j in range(4):
                    w = weights(KC + 4 * g + j).rearrange("p (k n) -> p k n", n=P)
                    for k in range(KC):
                        last = pe.matmul(ps[:, 2 + g, j * P:(j + 1) * P], w[:, k, :], aT[:, k, :],
                                         start=k == 0, stop=k == KC - 1)
                    last.then_inc(w_used.sem, 1)
                pe.wait_ge(w_used.sem, w_used.due(t, KC + 4 * g + 4))
                pe.sem_inc(q_out.sem, 1)
            slots.upto(48)
            for g in range(4):
                pe.wait_ge(q_ready.sem, q_ready.due(t, g + 1))
                for j in range(4):
                    last = pe.matmul(ps[:, g, j * P:(j + 1) * P], s12[:, 4 * g + j, :], keysT[:, j % 2, :],
                                     start=True, stop=True)
                last.then_inc(sco_out.sem, 1)

        def route_vector(dve, t, slots):
            link = Link(dve, route_link, t)
            slots.upto(42)
            dve.wait_ge(x_in.sem, x_in.due(t, 16))
            dve.wait_ge(gain_in.sem, gain_in.due(t, 16))
            dve.wait_ge(wo_out.sem, wo_out.due(t, 1))
            link(dve.tensor_tensor(x2[:, :], x2[:, :], banks(2, 2), ALU.add))
            link(dve.tensor_tensor_reduce(out=tn[:, :], in0=x2[:, :], in1=x2[:, :], scale=1.0, scalar=0.0,
                                          op0=ALU.mult, op1=ALU.add, accum_out=stat[:, 0:1]))
            dve.tensor_scalar(stat[:, 1:2], stat[:, 0:1], 1.0 / D, RMS_EPS, ALU.mult, ALU.add)\
               .then_inc(ssq_ready.sem, 1)
            dve.wait_ge(std_ready.sem, std_ready.due(t, 1))
            link(dve.reciprocal(stat[:, 1:2], stat[:, 1:2]))
            dve.scalar_tensor_tensor(out=tn[:, :], in0=x2[:, :], scalar=stat[:, 1:2], in1=gain,
                                     op0=ALU.mult, op1=ALU.mult).then_inc(tn_ready.sem, 1)
            slots.upto(49)
            dve.wait_ge(sco_ready.sem, sco_ready.due(t, 4)).then_inc(passed.sem, 1)
            for h in range(16):
                last = dve.max(v16[:, h, 0:8], s12[:, h, :])
            link.hold(last, passed)
            slots.upto(50)
            for h in range(16):
                dve.max_index(i16[:, h, 0:8], v16[:, h, 0:8], s12[:, h, :])
            for h in range(16):
                last = dve.match_replace(big[:, h, :], v16[:, h, 0:8], s12[:, h, :], NEG)
            link.hold(last, passed)
            slots.upto(51)
            for h in range(16):
                last = dve.max(v16[:, h, 8:16], big[:, h, :])
            link.hold(last, passed)
            for h in range(16):
                last = dve.max_index(i16[:, h, 8:16], v16[:, h, 8:16], big[:, h, :])
            link(last)
            slots.upto(52)
            link(dve.tensor_copy(f16, i16))
            halves = lambda x: x.rearrange("p (h s) k -> p h s k", s=2)
            v, f = halves(v16), halves(f16)
            link(dve.tensor_scalar(f[:, :, 0, :], f[:, :, 0, :], 128.0, None, ALU.mult))
            for dst, src in ((cand, v), (cidx, f)):
                at = 0
                for a, n, w in CAND:
                    out = dst[:, :, at:at + n * w]
                    if n == 1:
                        last = dve.tensor_tensor(out, src[:, :, 1, 0:w],
                                                 src[:, :, 0, a:a + 1].to_broadcast([P, 8, w]), ALU.add)
                    elif w == 1:
                        last = dve.tensor_tensor(out, src[:, :, 0, a:a + n],
                                                 src[:, :, 1, 0:1].to_broadcast([P, 8, n]), ALU.add)
                    else:
                        last = dve.tensor_tensor(out.rearrange("p h (n m) -> p h n m", m=w),
                                                 src[:, :, 1, 0:w].unsqueeze(2).to_broadcast([P, 8, n, w]),
                                                 src[:, :, 0, a:a + n].unsqueeze(3).to_broadcast([P, 8, n, w]),
                                                 ALU.add)
                    at += n * w
            link.hold(last, passed)
            slots.upto(53)
            for h in range(8):
                last = dve.max(best[:, h, 0:8], cand[:, h, :])
            link.hold(last, passed)
            for h in range(8):
                dve.max_index(pos[:, h, 0:8], best[:, h, 0:8], cand[:, h, :])
            for h in range(8):
                last = dve.match_replace(candb[:, h, :], best[:, h, 0:8], cand[:, h, :], NEG)
            link.hold(last, passed)
            for h in range(8):
                last = dve.max(best[:, h, 8:16], candb[:, h, :])
            link.hold(last, passed)
            for h in range(8):
                last = dve.max_index(pos[:, h, 8:16], best[:, h, 8:16], candb[:, h, :])
            link(last)
            dve.tensor_tensor(gate[:, :, :], best[:, :, :], best[:, :, 0:1].to_broadcast([P, 8, TOPK]),
                              ALU.subtract).then_inc(smax_in.sem, 1)
            link(dve.tensor_copy(posf, pos))
            for h in range(8):
                if h % 3 == 0:
                    slots.upto(54 + h // 3)
                link(dve.tensor_tensor(hot, iota[:, :].unsqueeze(1).to_broadcast([P, TOPK, NCAND]),
                                       posf[:, h, :].unsqueeze(2).to_broadcast([P, TOPK, NCAND]), ALU.is_equal))
                link(dve.tensor_tensor(hot, hot, cidx[:, h, :].unsqueeze(1).to_broadcast([P, TOPK, NCAND]), ALU.mult))
                link(dve.tensor_reduce(expf[:, h, :], hot, AX.X, ALU.add))
            link(dve.tensor_copy(expert[:, :], expf.rearrange("p h k -> p (h k)")))
            dve.wait_ge(sexp.sem, sexp.due(t, 1))
            link(dve.tensor_reduce(gsum[:, 0, :], gate[:, :, :], AX.X, ALU.add))
            link(dve.reciprocal(gsum[:, 1, :], gsum[:, 0, :]))
            link(dve.tensor_tensor(gate[:, :, :], gate[:, :, :],
                                   gsum[:, 1, :].unsqueeze(2).to_broadcast([P, 8, TOPK]), ALU.mult))
            link.close()

        none = Experts()

        with ExitStack() as own:
            def sb1(name, shape):
                return own.enter_context(nc.sbuf_tensor("st_" + name, shape, F32))

            NK = SAMPLES + 1
            wide = [sb1(n, [P, NK * P]) for n in ("scores", "probsT", "keyT", "amask")]
            m = {
                "sample": True, "nk": NK, "maps": SAMPLES, "deep": 1, "column": lambda n: 2 * (n % 4) + n // 4,
                "kv": sb1("kv", [P, NK, 256]), "amask": wide[3], "keyT": wide[2][:, :],
                "sc": [wide[0][:, :]], "prT": [wide[1][:, :]],
                "bk_odd": sb1("bk_odd", [P, 2, RW]), "rpT_odd": sb1("rpT_odd", [P, PAIRS, P]),
                "rowm": sb1("rowm", [P, 2]), "colm": sb1("colm", [P, 2, P]), "S_next": sb1("S_next", [P, PAIRS, P]),
                "kt_bank": 2, "sc_bank": [5], "sc_banks": 3, "prT_bank": [2], "o_bank": 0, "y_bank": 6,
            }
            block = own.enter_context(nc.Block())

            @block.sync
            def _(sp):
                loads = [(ident[:, :], A["ident"]), (ident2[:, :], A["ident2"]),
                         (rc[:, :], A["rc"][1]), (m["rowm"][:, :], A["rowm"]), (m["colm"][:, :, :], A["colm"]),
                         (w2a2[0:LORA, 0:RW], A["w2"]), (w2a2[LORA:P, RW:], A["a2"]),
                         (g2a[:, :], A["g2"][0:P, :]), (g2b[:, :], A["g2"][P:GLORA, :]),
                         (keysT[:, 0, :], A["key1T"]), (keysT[:, 1, :], A["key2T"]),
                         (gain_f[:, :], row(A["norm_final"]).to_broadcast([P, D])),
                         (iota[:, :], row(A["iota"]).to_broadcast([P, NCAND]))]
                for name, at, n in (("r_k", RKC, RW), ("ln_w", LNW, RW), ("ln_b", LNB, RW), ("out_g", OUTG, RW),
                                    ("sinks", SINK, HEADS)):
                    loads.append((bc[:, at:at + n], row(A[name]).to_broadcast([P, n])))
                for dst, src in loads:
                    sp.dma_start(dst, src).then_inc(consts.sem, 16)
                sp.wait_ge(consts.sem, 16 * len(loads))
                sp.sem_inc(tile_end.sem, 1)
                copies = ((A["shift_prompt"], proj[P + SEQ - 1:P + SEQ, 0:P_RWKV]),
                          (A["k_prompt"], proj[SEQ:P + SEQ, K0:V0]),
                          (A["v_prompt"], proj[SEQ:P + SEQ, V0:P_TOTAL]),
                          (A["shift_sample"], proj[P + SEQ + STEPS - 1:P + TOKENS:STEPS, 0:P_RWKV]),
                          (A["k_sample"][:, P - STEPS:, :], proj[P + SEQ:, K0:V0].rearrange("(b s) c -> b s c", s=STEPS)),
                          (A["v_sample"][:, P - STEPS:, :], proj[P + SEQ:, V0:].rearrange("(b s) c -> b s c", s=STEPS)),
                          (A["k_sample"][:, 0:P - STEPS, :], A["cache_k"][:, STEPS:, :]),
                          (A["v_sample"][:, 0:P - STEPS, :], A["cache_v"][:, STEPS:, :]))
                for dst, src in copies:
                    sp.dma_start(dst, src).then_inc(consts.sem, 16)
                mix_sync(sp, 0, m, SEQ)
                sp.wait_ge(s_stored.sem, 32 * SAMPLES)
                sp.wait_ge(consts.sem, 16 * (len(loads) + len(copies)))

            @block.scalar
            def _(act):
                act.sem_inc(tile_end.sem, 1)
                mix_scalar(act, 0, m, none)

            @block.vector
            def _(dve):
                for z in (S[:, :, :], m["S_next"][:, :, :], w2a2[0:LORA, RW:], w2a2[LORA:P, 0:RW], G[:, :, :, :]):
                    dve.memset(z, 0.0)
                dve.memset(H[:, :, :, :], 0.0).then_inc(passed.sem, 1)
                dve.wait_ge(passed.sem, 1)
                dve.sem_inc(tile_end.sem, 1)
                mix_vector(dve, 0, m, none)

            @block.tensor
            def _(pe):
                pe.sem_inc(tile_end.sem, 1)
                mix_tensor(pe, 0, m, none)

        with ExitStack() as own:
            def sb2(name, shape, dt=F32):
                return own.enter_context(nc.sbuf_tensor("ex_" + name, shape, dt))

            two = lambda buf, at: [part(buf, at + n * 2 * P, (2 * P,)) for n in range(2)]
            m = {
                "sample": False, "nk": 2, "maps": 4, "deep": 2, "column": lambda n: n, "S_next": S,
                "kv": sb2("kv", [P, 2, 256]), "amask": sb2("amask", [P, 2 * P]), "keyT": part(work2, 0, (2 * P,)),
                "sc": two(k2, 0), "prT": two(sb2("probsT", [P, 4 * P]), 0),
                "kt_bank": 4, "sc_bank": [5, 2], "sc_banks": 1, "prT_bank": [3, 4], "o_bank": 1, "y_bank": 0,
            }
            x2c = sb2("x2c", [P, D])
            tnc = sb2("tnc", [P, D])
            y_out = sb2("y_out", [P, D])
            expert_c = sb2("expert_c", [P, SLOTS], U32)
            gate_c = sb2("gate_c", [P, SLOTS])
            u = sb2("u", [P, SLOTS])
            ge = sb2("ge", [P, SLOTS])
            coef = sb2("coef", [P, SLOTS])
            diag = sb2("diag", [P, DIAGS, P])
            down = sb2("down_rows", [P, DOWN_RING, D])
            up = sb2("up_rows", [P, UP_RING, D])

            def experts_gpsimd(pool, t):
                def gather(dst, table, s, arrived):
                    pool.indirect_dma_start(dst, None, table, bass.IndirectOffsetOnAxis(expert_c[:, s:s + 1], 0))\
                        .then_inc(arrived.sem, 16)

                pool.wait_ge(handed.sem, handed.due(t, 1)).then_inc(row_free.sem, 1)
                for s in range(SLOTS + UP_LAG):
                    if s < SLOTS:
                        if s >= DOWN_RING:
                            pool.wait_ge(dotted.sem, dotted.due(t, s - DOWN_RING + 1)).then_inc(row_free.sem, 1)
                        gather(down[:, s % DOWN_RING, :], A["down"], s, down_in[s % DOWN_RING])
                    v = s - UP_LAG
                    if v >= 0:
                        old = v - UP_RING if v >= UP_RING else max(range(v, SLOTS, UP_RING))
                        used, on, credit = (dve_used, ON_VECTOR, 1) if old in ON_VECTOR else (pe_used, ON_PE, DIAGS)
                        count = on.index(old) + 1 + credit - (len(on) if v < UP_RING else 0)
                        assert count > 0
                        pool.wait_ge(used.sem, used.due(t, count)).then_inc(row_free.sem, 1)
                        gather(up[:, v % UP_RING, :], A["up"], v, up_in[v % UP_RING])

            def experts_scalar(act, t):
                def coefficients(slots):
                    for s in slots:
                        act.wait_ge(dotted.sem, dotted.due(t, s + 1))
                        act.activation(ge[:, s:s + 1], u[:, s:s + 1], ACT.Gelu).then_inc(gelued.sem, 1)
                    for s in slots:
                        act.wait_ge(gelued.sem, gelued.due(t, s + 1))
                        act.activation(coef[:, s:s + 1], ge[:, s:s + 1], ACT.Copy, scale=gate_c[:, s:s + 1])\
                           .then_inc(coefs.sem, 1)
                    for s in slots:
                        if s in ON_PE:
                            n = ON_PE.index(s)
                            act.wait_ge(coefs.sem, coefs.due(t, s + 1))
                            act.wait_ge(pe_used.sem, pe_used.due(t, n + 1))
                            act.activation(diag[:, n % DIAGS, :], ident[:, :], ACT.Copy, scale=coef[:, s:s + 1])\
                               .then_inc(diags.sem, 1)

                def last():
                    act.wait_ge(ssq2_ready.sem, ssq2_ready.due(t, 1))
                    act.activation(stat[:, 3:4], stat[:, 3:4], ACT.Sqrt).then_inc(std2_ready.sem, 1)

                return Experts((coefficients, 1), last=last)

            def experts_tensor(pe, t):
                def add(slots):
                    for s in slots:
                        if s in ON_PE:
                            n, r = ON_PE.index(s), s % UP_RING
                            pe.wait_ge(up_in[r].sem, up_in[r].due(t, 16 * (s // UP_RING + 1)))
                            pe.wait_ge(diags.sem, diags.due(t, n + 1))
                            for c in range(2):
                                last = pe.matmul(bank(6 + c), diag[:, n % DIAGS, :], up[:, r, c * 512:(c + 1) * 512],
                                                 start=n == 0, stop=n == len(ON_PE) - 1)
                            last.then_inc(pe_used.sem, 1)

                return Experts((add, 2), last=lambda: None)

            def hand_over(dve, t):
                if not (isinstance(t, int) and t == 0):
                    for n in up_in:
                        dve.wait_ge(n.sem, n.due(t, 0))
                dve.tensor_copy(expert_c[:, :], expert[:, :]).then_inc(handed.sem, 1)

            def experts_vector(dve, t):
                dve.tensor_copy(gate_c[:, :], gate[:, :, :].rearrange("p h k -> p (h k)"))
                dve.tensor_copy(tnc[:, :], tn[:, :])
                dve.tensor_copy(x2c[:, :], x2[:, :]).then_inc(end_link.sem, 1)
                dve.wait_ge(end_link.sem, end_link.due(t, 1))

                def dots(slots):
                    for s in slots:
                        r = s % DOWN_RING
                        dve.wait_ge(down_in[r].sem, down_in[r].due(t, 16 * (s // DOWN_RING + 1)))
                        dve.tensor_tensor_reduce(out=down[:, r, :], in0=down[:, r, :], in1=tnc[:, :],
                                                 scale=1.0, scalar=0.0, op0=ALU.mult, op1=ALU.add,
                                                 accum_out=u[:, s:s + 1]).then_inc(dotted.sem, 1)

                def add(slots):
                    for s in slots:
                        if s in ON_VECTOR:
                            n, r = ON_VECTOR.index(s), s % UP_RING
                            dve.wait_ge(up_in[r].sem, up_in[r].due(t, 16 * (s // UP_RING + 1)))
                            dve.wait_ge(coefs.sem, coefs.due(t, s + 1))
                            dve.wait_ge(dve_used.sem, dve_used.due(t, n + 1))
                            dve.scalar_tensor_tensor(out=x2c[:, :], in0=up[:, r, :], scalar=coef[:, s:s + 1],
                                                     in1=x2c[:, :], op0=ALU.mult, op1=ALU.add)\
                               .then_inc(dve_used.sem, 1)

                def last():
                    link = Link(dve, end_link, t)
                    link.n = 1
                    dve.wait_ge(dve_used.sem, dve_used.due(t, len(ON_VECTOR) + 1))
                    dve.wait_ge(pe_used.sem, pe_used.due(t, len(ON_PE) + DIAGS))
                    link(dve.tensor_tensor(x2c[:, :], x2c[:, :], banks(6, 2), ALU.add))
                    link(dve.tensor_tensor_reduce(out=tnc[:, :], in0=x2c[:, :], in1=x2c[:, :], scale=1.0, scalar=0.0,
                                                  op0=ALU.mult, op1=ALU.add, accum_out=stat[:, 2:3]))
                    dve.tensor_scalar(stat[:, 3:4], stat[:, 2:3], 1.0 / D, RMS_EPS, ALU.mult, ALU.add)\
                       .then_inc(ssq2_ready.sem, 1)
                    dve.wait_ge(std2_ready.sem, std2_ready.due(t, 1))
                    link(dve.reciprocal(stat[:, 3:4], stat[:, 3:4]))
                    dve.wait_ge(y_stored.sem, y_stored.due(t, 16))
                    link(dve.scalar_tensor_tensor(out=y_out[:, :], in0=x2c[:, :], scalar=stat[:, 3:4], in1=gain_f[:, :],
                                                  op0=ALU.mult, op1=ALU.mult))
                    dve.sem_inc(y_ready.sem, 1)
                    link.close()

                return Experts((dots, 0), (add, 2), last=last)

            def store_y(sp, t):
                sp.wait_ge(y_ready.sem, y_ready.due(t, 1))
                sp.dma_start(A["y"][bass.ds(t * P, P), :], y_out[:, :]).then_inc(y_stored.sem, 16)

            block = own.enter_context(nc.Block())
            T = PROMPT_TILES

            @block.sync
            def _(sp):
                sp.sem_inc(y_stored.sem, 16)
                sp.dma_start(rc[:, :], A["rc"][0]).then_inc(late_consts.sem, 16)
                route_sync(sp, 0, SEQ)
                sp.wait_ge(late_consts.sem, 16)
                sp.wait_ge(w_used.sem, w_used.due(0, 24))
                sp.sem_inc(tile_end.sem, 1)
                with sp.Fori(0, T) as t:
                    mix_sync(sp, t + 1, m, t * P)
                    route_sync(sp, t + 1, t * P)
                    store_y(sp, t)
                    sp.wait_ge(w_used.sem, w_used.due(t + 1, 24))
                    sp.sem_inc(tile_end.sem, 1)
                for o in range(2):
                    sp.dma_start(A["wkvT_prompt"][o], S[o * HD:(o + 1) * HD, :, o * HD:(o + 1) * HD])\
                      .then_inc(s_stored.sem, 16)
                store_y(sp, T)
                sp.wait_ge(y_stored.sem, 16 * (T + 2))
                sp.wait_ge(s_stored.sem, 32 * (SAMPLES + 1))

            @block.gpsimd
            def _(pool):
                with pool.Fori(0, T + 1) as t:
                    experts_gpsimd(pool, t)

            @block.scalar
            def _(act):
                route_scalar(act, 0, none)
                act.sem_inc(tile_end.sem, 1)
                with act.Fori(0, T) as t:
                    slots = experts_scalar(act, t)
                    mix_scalar(act, t + 1, m, slots)
                    route_scalar(act, t + 1, slots)
                    act.sem_inc(tile_end.sem, 1)
                    slots.finish()
                experts_scalar(act, T).finish()

            @block.vector
            def _(dve):
                dve.memset(S[:, :, :], 0.0).then_inc(passed.sem, 1)
                dve.sem_inc(dve_used.sem, 1)
                route_vector(dve, 0, none)
                dve.sem_inc(tile_end.sem, 1)
                hand_over(dve, 0)
                with dve.Fori(0, T) as t:
                    slots = experts_vector(dve, t)
                    dve.wait_ge(tile_end.sem, tile_end.due(t + 1, 4))
                    mix_vector(dve, t + 1, m, slots)
                    route_vector(dve, t + 1, slots)
                    dve.sem_inc(tile_end.sem, 1)
                    slots.upto(MARKS)
                    hand_over(dve, t + 1)
                    slots.finish()
                experts_vector(dve, T).finish()

            @block.tensor
            def _(pe):
                pe.sem_inc(pe_used.sem, DIAGS)
                route_tensor(pe, 0, none)
                pe.sem_inc(tile_end.sem, 1)
                with pe.Fori(0, T) as t:
                    slots = experts_tensor(pe, t)
                    mix_tensor(pe, t + 1, m, slots)
                    route_tensor(pe, t + 1, slots)
                    pe.wait_ge(sco_out.sem, sco_out.due(t + 1, 4))
                    pe.sem_inc(tile_end.sem, 1)
                    slots.finish()
                experts_tensor(pe, T).finish()



def build(nc, A):
    A["proj"] = nc.dram_tensor("proj_rows", (P + TOKENS, P_TOTAL), F32, kind="Internal").ap()
    project(nc, A)
    mix_and_route(nc, A)


def shape_constants():
    i = np.arange(P)
    tok, col = i[:, None], i[None, :]
    rc = np.zeros((2, P, RC_COLS), np.float32)
    decay = np.float32(-math.exp(-0.5))
    for v, c in enumerate((32, STEPS)):
        same = tok // c == col // c
        rc[v, :, TRI_I:TRI_I + P] = decay * (same & (tok <= col))
        rc[v, :, TRI_X:TRI_X + P] = decay * (same & (tok < col))
        rc[v, :, TRI_S:TRI_S + P] = decay * (same & (tok > col))
        rc[v, :, IND:IND + P // c] = decay * (tok // c == np.arange(P // c)[None, :])
        rc[v, :, MASK2:MASK2 + P] = same & (tok < col)
        rc[v, :, MASK2 + P:MASK2 + 2 * P] = same & (tok <= col)
        rc[v, :, MASKN:MASKN + P] = same & (tok > col)
    rowm = np.stack([(i // STEPS) % 2 == 0, (i // STEPS) % 2 == 1], 1).astype(np.float32)
    colm = np.broadcast_to(rowm.T[None], (P, 2, P)).astype(np.float32)
    key = np.arange(2 * P)[None, :] - P
    mp = np.zeros((PROMPT_TILES, P, 2 * P), np.float32)
    for t in range(PROMPT_TILES):
        qc, kc = (t * P + tok) // 64, (t * P + key) // 64
        mp[t] = np.where((kc >= qc - 2) & (kc <= qc) & (kc >= 0), 0, NEG)
    cached = np.arange(SAMPLES * P)[None, :] // P == tok // STEPS
    new = col // STEPS == tok // STEPS
    ms = np.where(np.concatenate([cached, new], 1), 0, NEG).astype(np.float32)
    return {
        "ident": np.eye(P, dtype=np.float32),
        "ident2": np.concatenate([np.eye(HD, dtype=np.float32)] * 2, 0),
        "rc": rc, "rowm": rowm, "colm": np.ascontiguousarray(colm),
        "mask_prompt": mp.reshape(-1, 2 * P), "mask_sample": ms,
        "iota": np.arange(NCAND, dtype=np.float32),
    }


OUTPUTS = {
    "y": (TOKENS, D), "shift_prompt": (1, P_RWKV), "wkvT_prompt": (2, HD, PAIRS, HD),
    "k_prompt": (P, 128), "v_prompt": (P, 128), "shift_sample": (SAMPLES, P_RWKV),
    "wkvT_sample": (SAMPLES, 2, HD, PAIRS, HD), "k_sample": (SAMPLES, P, 128), "v_sample": (SAMPLES, P, 128),
}


def kernel(**inputs):
    import concourse.bacc as bacc
    from concourse.bass_utils import run_bass_kernel_spmd

    a = {name: np.asarray(x) for name, x in inputs.items()}
    wkv = a["state_rwkv_wkv"][0].reshape(SAMPLES, PAIRS, 2, HD, HD)
    w_in = a["w_in"][0]
    w_q = w_in[:, Q0:K0].reshape(D, 2, 4, HD).transpose(0, 2, 1, 3).reshape(D, RW)
    w_in = np.concatenate([w_in[:, :Q0], w_q, w_in[:, K0:]], 1)
    arrays = {
        "x": np.concatenate([a["x_prompt"].reshape(-1, D), a["x_sample"].reshape(-1, D)], 0),
        "norm_mix_col": np.ascontiguousarray(a["norm_mix_g"][0].reshape(KC, P).T),
        "w_in": w_in, "w_out": a["w_out"][0], 
        "w_q": np.ascontiguousarray(a["peer_w_q"][0].reshape(KC, P, 16, P).transpose(2, 1, 0, 3)).reshape(16, P, D),
        "mu": a["rwkv_mu"][0], "w0": a["rwkv_w0"][0], "a0": a["rwkv_a0"][0],
        "w2": a["rwkv_w2"][0], "a2": a["rwkv_a2"][0], "g2": a["rwkv_g2"][0],
        "k_k": a["rwkv_k_k"][0], "k_a": a["rwkv_k_a"][0], "r_k": a["rwkv_r_k"][0].reshape(-1),
        "ln_w": a["rwkv_ln_w"][0], "ln_b": a["rwkv_ln_b"][0], "out_g": a["attn_out_g"][0],
        "sinks": a["attn_sinks"][0], "norm_ffn": a["norm_ffn_g"][0], "norm_final": a["norm_final_g"],
        "state_shift": a["state_rwkv_shift"][0].reshape(SAMPLES, P_RWKV),
        "state_wkvT": np.ascontiguousarray(wkv.transpose(0, 2, 4, 1, 3)),
        "cache_k": a["cache_swa_k"][0].reshape(SAMPLES, P, 128),
        "cache_v": a["cache_swa_v"][0].reshape(SAMPLES, P, 128),
        "key1T": np.ascontiguousarray(a["peer_key1"][0].T), "key2T": np.ascontiguousarray(a["peer_key2"][0].T),
        "down": a["peer_down"][0], "up": a["peer_up"][0],
    }
    arrays.update(shape_constants())
    nc = bacc.Bacc("TRN2", target_bir_lowering=False, num_devices=1)
    A = {name: nc.dram_tensor(name, x.shape, F32, kind="ExternalInput").ap() for name, x in arrays.items()}
    A.update({name: nc.dram_tensor(name, shape, F32, kind="ExternalOutput").ap() for name, shape in OUTPUTS.items()})
    build(nc, A)
    r = run_bass_kernel_spmd(nc, [arrays], core_ids=[0]).results[0]
    wkv_p = r["wkvT_prompt"].transpose(2, 0, 3, 1).reshape(1, 1, HEADS, HD, HD)
    wkv_s = r["wkvT_sample"].transpose(0, 3, 1, 4, 2).reshape(1, SAMPLES, HEADS, HD, HD)
    return (r["y"][P:].reshape(1, SEQ, D), r["y"][:P].reshape(SAMPLES, STEPS, D),
            r["shift_prompt"].reshape(1, 1, 1, P_RWKV), np.ascontiguousarray(wkv_p),
            r["k_prompt"].reshape(1, 1, P, 2, HD), r["v_prompt"].reshape(1, 1, P, 2, HD),
            r["shift_sample"].reshape(1, SAMPLES, 1, P_RWKV), np.ascontiguousarray(wkv_s),
            r["k_sample"].reshape(1, SAMPLES, P, 2, HD), r["v_sample"].reshape(1, SAMPLES, P, 2, HD))
```

```python
import math
from contextlib import ExitStack

import numpy as np

import concourse.bass as bass
from concourse import mybir

F32 = mybir.dt.float32
U32 = mybir.dt.uint32
ALU = mybir.AluOpType
ACT = mybir.ActivationFunctionType
AX = mybir.AxisListType

P = 128
D = 1024
SEQ = 1024
SAMPLES, STEPS = 8, 16
TOKENS = SEQ + SAMPLES * STEPS
TILES = TOKENS // P
PROMPT_TILES = SEQ // P
HEADS, HD = 8, 64
RW = HEADS * HD
LORA = 64
GLORA = 160
P_RWKV = 3 * RW + 2 * LORA + GLORA
Q0, K0, V0 = P_RWKV, P_RWKV + RW, P_RWKV + RW + 128
P_TOTAL = V0 + 128
KC = D // P
PAIRS = HEADS // 2
RMS_EPS = 1e-6
LN_EPS = 64e-5
L2_EPS = 1e-12
SCALE = HD ** -0.5
PGROUPS = 6
PG = P_TOTAL // PGROUPS
EXPERTS = 128 * 128
TOPK = 16
SLOTS = 8 * TOPK
TRI_I, TRI_X, TRI_S, IND, MASK2, MASKN, RC_COLS = 0, 128, 256, 384, 392, 648, 776
RKC, LNW, LNB, OUTG, SINK = 0, RW, 2 * RW, 3 * RW, 4 * RW
BC_COLS = 4 * RW + HEADS
NEG = -1e30
W0_ROW, A0_ROW, KK_ROW = 32, 64, 96


DVE_LINKS = 55
DVE_LINKS_SAMPLE = 58
ROUTE_LINKS = 43
END_LINKS = 5


class Signal:

    def __init__(self, ctx, nc, name, per=1, first=None):
        self.sem, self.per, self.first = ctx.enter_context(nc.semaphore(name)), per, first or per

    def due(self, t, k):
        return k if isinstance(t, int) and t == 0 else t * self.per + (self.first - self.per + k)

    def of(self, t):
        return self.first if isinstance(t, int) and t == 0 else self.per


class Link:

    def __init__(self, eng, ended, t):
        self.eng, self.ended, self.t, self.n = eng, ended, t, 0

    def __call__(self, ins):
        self.n += 1
        ins.then_inc(self.ended.sem, 1)
        self.eng.wait_ge(self.ended.sem, self.ended.due(self.t, self.n))

    def hold(self, ins, passed):
        self.n += 1
        ins.then_inc(self.ended.sem, 1)
        self.eng.wait_ge(self.ended.sem, self.ended.due(self.t, self.n)).then_inc(passed.sem, 1)

    def close(self):
        assert self.n == self.ended.of(self.t), (self.ended.sem, self.n, self.ended.of(self.t))


def row(vec):
    return vec.rearrange("(a n) -> a n", a=1)


def project(nc, A, C):
    with ExitStack() as ctx:
        def sb(name, shape, dt=F32):
            return ctx.enter_context(nc.sbuf_tensor("pj_" + name, shape, dt))

        def signal(name, per=1):
            return Signal(ctx, nc, name, per)

        w = sb("w_in_sb", [P, KC, P_TOTAL])
        gain = sb("gain_col", [P, KC])
        ident = sb("ident_a", [P, P])
        x = sb("x_in", [P, 2, D])
        junk = sb("squares", [P, D])
        ssq = sb("ssq_a", [P, 2])
        rstd = sb("rstd_a", [P, 2])
        hT = sb("hT", [P, 2, KC, P])
        pbuf = sb("proj_sb", [P, 2, P_TOTAL])
        psT = ctx.enter_context(nc.psum_tensor("psT", [P, KC, P], F32))
        psP = ctx.enter_context(nc.psum_tensor("psP", [P, PGROUPS, 512], F32))

        w_in_loaded = [signal(f"w_in_loaded{k}", 16) for k in range(KC)]
        later_loaded = signal("later_constants_loaded")
        later_zeroed = signal("later_constants_zeroed")
        const_loaded = signal("const_a_loaded")
        x_loaded = [signal("x_loaded0", 16), signal("x_loaded1", 16)]
        squared = signal("squared")
        transposed = signal("transposed")
        std_ready = signal("std_ready")
        var_ready = signal("var_ready")
        rstd_ready = signal("rstd_ready")
        hT_ready = signal("hT_ready", 2)
        proj_done = signal("proj_done", PGROUPS)
        act_evac = signal("act_evac", 3)
        dve_evac = signal("dve_evac", 3)
        stored = [signal("proj_stored0", 16), signal("proj_stored1", 16)]
        zeroed = signal("zeroed")

        out = A["proj"]

        block = ctx.enter_context(nc.Block())

        @block.sync
        def _(sp):
            sp.dma_start(ident[:, :], A["ident"]).then_inc(const_loaded.sem, 16)
            sp.dma_start(gain[:, :], A["norm_mix_col"]).then_inc(const_loaded.sem, 16)

            def load(t, par, n):
                sp.wait_ge(squared.sem, t + 1)
                sp.wait_ge(transposed.sem, t + 1)
                sp.dma_start(x[:, par, :], A["x"][bass.ds(t * P, P), :]).then_inc(x_loaded[par].sem, 16)

            load(0, 0, 0)
            load(1, 1, 0)
            for k in range(KC):
                sp.dma_start(w[:, k, :], A["w_in"][k * P:(k + 1) * P, :]).then_inc(w_in_loaded[k].sem, 16)
            sp.wait_ge(zeroed.sem, 1)
            sp.dma_start(out[0:P, :], pbuf[:, 1, :]).then_inc(stored[1].sem, 16)
            later = constant_loads(A, C)
            for dst, src in later:
                sp.dma_start(dst, src).then_inc(later_loaded.sem, 16)
            with sp.Fori(1, TILES // 2) as u:
                load(2 * u, 0, u)
                load(2 * u + 1, 1, u)
            load(TILES - 1, 0, 0)
            sp.wait_ge(later_loaded.sem, 16 * len(later))
            sp.wait_ge(later_zeroed.sem, len(constant_zeros(C)))
            sp.wait_ge(stored[0].sem, 16 * (1 + 5))
            sp.wait_ge(stored[1].sem, 16 * (1 + 4))

        @block.gpsimd
        def _(pool):
            for n, z in enumerate(constant_zeros(C)):
                pool.memset(z, 0.0).then_inc(later_zeroed.sem, 1)
                pool.wait_ge(later_zeroed.sem, n + 1)

        @block.scalar
        def _(act):
            act.sem_inc(squared.sem, 2)
            act.sem_inc(act_evac.sem, 3)
            act.sem_inc(stored[0].sem, 16)

            def square(t, par, u):
                act.wait_ge(x_loaded[par].sem, 16 * u + 16)
                act.wait_ge(squared.sem, t + 2)
                act.activation(junk[:, :], x[:, par, :], ACT.Square,
                               accum_out=ssq[:, par:par + 1]).then_inc(squared.sem, 1)
                act.wait_ge(var_ready.sem, t + 1)
                act.activation(rstd[:, par:par + 1], ssq[:, par:par + 1], ACT.Sqrt).then_inc(std_ready.sem, 1)

            def evacuate(t, par, u):
                act.wait_ge(rstd_ready.sem, t + 1)
                act.wait_ge(stored[par].sem, 16 * u + 16)
                for g in range(0, PGROUPS, 2):
                    act.wait_ge(proj_done.sem, 12 + 6 * t + g + 1)
                    act.activation(pbuf[:, par, g * PG:(g + 1) * PG], psP[:, g, 0:PG], ACT.Copy,
                                   scale=rstd[:, par:par + 1]).then_inc(act_evac.sem, 1)
                act.wait_ge(act_evac.sem, 3 * t + 6)
                act.wait_ge(dve_evac.sem, 3 * t + 6)
                act.dma_start(out[bass.ds(P + t * P, P), :], pbuf[:, par, :]).then_inc(stored[par].sem, 16)

            square(0, 0, 0)
            with act.Fori(0, TILES // 2) as u:
                square(2 * u + 1, 1, u)
                evacuate(2 * u, 0, u)
                square(2 * u + 2, 0, u + 1)
                evacuate(2 * u + 1, 1, u)
            evacuate(TILES - 1, 0, TILES // 2)

        @block.vector
        def _(dve):
            dve.sem_inc(dve_evac.sem, 3)
            dve.memset(pbuf[:, 1, :], 0.0).then_inc(zeroed.sem, 1)
            dve.wait_ge(const_loaded.sem, 32)

            def normalise(t, par, u):
                dve.wait_ge(squared.sem, t + 3)
                dve.tensor_scalar(ssq[:, par:par + 1], ssq[:, par:par + 1], 1.0 / D, RMS_EPS,
                                  ALU.mult, ALU.add).then_inc(var_ready.sem, 1)
                dve.wait_ge(transposed.sem, t + 3)
                dve.wait_ge(proj_done.sem, 6 * t + 6)
                for k in range(0, KC, 4):
                    dve.tensor_tensor(hT[:, par, k:k + 4, :], psT[:, k:k + 4, :],
                                      gain[:, k:k + 4].unsqueeze(2).to_broadcast([P, 4, P]),
                                      ALU.mult).then_inc(hT_ready.sem, 1)
                dve.wait_ge(std_ready.sem, t + 1)
                dve.reciprocal(rstd[:, par:par + 1], rstd[:, par:par + 1]).then_inc(rstd_ready.sem, 1)

            def evacuate(t, par, u):
                dve.wait_ge(rstd_ready.sem, t + 1)
                dve.wait_ge(stored[par].sem, 16 * u + 16)
                for g in range(1, PGROUPS, 2):
                    dve.wait_ge(proj_done.sem, 12 + 6 * t + g + 1)
                    dve.tensor_scalar(pbuf[:, par, g * PG:(g + 1) * PG], psP[:, g, 0:PG],
                                      rstd[:, par:par + 1], None, ALU.mult).then_inc(dve_evac.sem, 1)

            normalise(0, 0, 0)
            with dve.Fori(0, TILES // 2) as u:
                normalise(2 * u + 1, 1, u)
                evacuate(2 * u, 0, u)
                normalise(2 * u + 2, 0, u + 1)
                evacuate(2 * u + 1, 1, u)
            evacuate(TILES - 1, 0, TILES // 2)

        @block.tensor
        def _(pe):
            pe.sem_inc(transposed.sem, 2)
            pe.sem_inc(proj_done.sem, 12)
            pe.wait_ge(const_loaded.sem, 32)

            def transposes(t, par, u, first=False):
                pe.wait_ge(x_loaded[par].sem, 16 * u + 16)
                if not first:
                    pe.wait_ge(hT_ready.sem, 2 * t)
                for k in range(KC):
                    last = pe.transpose(psT[:, k, :], x[:, par, k * P:(k + 1) * P], ident[:, :])
                last.then_inc(transposed.sem, 1)

            def products(t, par, u):
                pe.wait_ge(hT_ready.sem, 2 * t + 2)
                for g in range(PGROUPS):
                    pe.wait_ge((dve_evac if g % 2 else act_evac).sem, 3 * t + g // 2 + 1)
                    for k in range(KC):
                        last = pe.matmul(psP[:, g, 0:PG], hT[:, par, k, :], w[:, k, g * PG:(g + 1) * PG],
                                         start=k == 0, stop=k == KC - 1)
                    last.then_inc(proj_done.sem, 1)

            transposes(0, 0, 0, True)
            transposes(1, 1, 0)
            pe.wait_ge(hT_ready.sem, 2)
            pe.wait_ge(dve_evac.sem, 3)
            pe.wait_ge(act_evac.sem, 3)
            for k in range(KC):
                pe.wait_ge(w_in_loaded[k].sem, 16)
                for g in range(PGROUPS):
                    last = pe.matmul(psP[:, g, 0:PG], hT[:, 0, k, :], w[:, k, g * PG:(g + 1) * PG],
                                     start=k == 0, stop=k == KC - 1)
                    if k == KC - 1:
                        last.then_inc(proj_done.sem, 1)
            with pe.Fori(0, TILES // 2 - 1) as u:
                transposes(2 * u + 2, 0, u + 1)
                products(2 * u + 1, 1, u)
                transposes(2 * u + 3, 1, u + 1)
                products(2 * u + 2, 0, u + 1)
            transposes(TILES - 1, 0, TILES // 2)
            products(TILES - 2, 1, TILES // 2 - 1)
            products(TILES - 1, 0, TILES // 2)



CAND = [(0, 1, 16), (1, 1, 8), (2, 1, 5), (3, 1, 4), (4, 1, 3), (5, 3, 2), (8, 8, 1)]
NCAND = sum(n * m for _, n, m in CAND)
DOWN_RING, UP_RING = 7, 8
UP_LAG = 2
DIAGS = 8
WRING = 6
MARKS = 71
SHARES = [1.2 if m <= 17 else 0.6 if 41 <= m <= 48 else 1.0 for m in range(1, MARKS + 1)]
SLOTS_UPTO = [round(SLOTS * sum(SHARES[:m]) / sum(SHARES)) for m in range(MARKS + 1)]
HALF = SLOTS // 2
ON_VECTOR = [s for s in range(SLOTS) if s % 6 == 5]
ON_PE = [s for s in range(SLOTS) if s % 6 != 5]


class Experts:

    def __init__(self, *work, last=None):
        self.work, self.last, self.mark, self.done = work, last, 0, [0] * len(work)

    def upto(self, mark):
        while self.mark < mark:
            self.mark += 1
            for n, (run, lag) in enumerate(self.work):
                end = SLOTS_UPTO[max(0, min(self.mark - lag, MARKS))]
                if end > self.done[n]:
                    run(range(self.done[n], end))
                    self.done[n] = end

    def finish(self):
        self.upto(MARKS + 2)
        assert all(n == SLOTS for n in self.done)
        self.last()


def constants(nc, ctx):
    sb = lambda name, shape: ctx.enter_context(nc.sbuf_tensor("cn_" + name, shape, F32))
    return {
        "ident": sb("ident", [P, P]),
        "ident2": sb("ident2", [P, HD]),
        "rc": sb("rc", [P, RC_COLS]),
        "bc": sb("bc", [P, BC_COLS]),
        "w2a2": sb("w2a2", [P, 2 * RW]),
        "g2a": sb("g2a", [P, RW]),
        "g2b": sb("g2b", [P, RW]),
        "keysT": sb("keysT", [P, 2, P]),
        "gain_final": sb("gain_final", [P, D]),
        "iota": sb("iota", [P, NCAND]),
        "G": sb("G", [P, 4, PAIRS, P]), "H": sb("H", [P, 4, PAIRS, P]),
    }


def constant_loads(A, C):
    loads = [(C["ident"][:, :], A["ident"]), (C["ident2"][:, :], A["ident2"]), (C["rc"][:, :], A["rc"][1]),
             (C["w2a2"][0:LORA, 0:RW], A["w2"]), (C["w2a2"][LORA:P, RW:], A["a2"]),
             (C["g2a"][:, :], A["g2"][0:P, :]), (C["g2b"][0:GLORA - P, :], A["g2"][P:GLORA, :]),
             (C["g2b"][W0_ROW:W0_ROW + 1, :], row(A["w0"])), (C["g2b"][A0_ROW:A0_ROW + 1, :], row(A["a0"])),
             (C["g2b"][KK_ROW:KK_ROW + 1, :], row(A["k_k"])),
             (C["keysT"][:, 0, :], A["key1T"]), (C["keysT"][:, 1, :], A["key2T"]),
             (C["gain_final"][:, :], row(A["norm_final"]).to_broadcast([P, D])),
             (C["iota"][:, :], row(A["iota"]).to_broadcast([P, NCAND]))]
    for name, at, n in (("r_k", RKC, RW), ("ln_w", LNW, RW), ("ln_b", LNB, RW), ("out_g", OUTG, RW),
                        ("sinks", SINK, HEADS)):
        loads.append((C["bc"][:, at:at + n], row(A[name]).to_broadcast([P, n])))
    return loads


def constant_zeros(C):
    return (C["w2a2"][0:LORA, RW:], C["w2a2"][LORA:P, 0:RW], C["G"][:, :, :, :], C["H"][:, :, :, :])


def mix_and_route(nc, A, C):
    with ExitStack() as ctx:
        def sb(name, shape, dt=F32):
            return ctx.enter_context(nc.sbuf_tensor("mx_" + name, shape, dt))

        def flag(name, per=1, first=None):
            return Signal(ctx, nc, name, per, first)

        ident, ident2, rc, bc, w2a2, g2a, g2b, keysT, gain_f, iota, G, H = (C[n] for n in (
            "ident", "ident2", "rc", "bc", "w2a2", "g2a", "g2b", "keysT", "gain_final", "iota", "G", "H"))
        p_cur = sb("p_cur", [P, P_TOTAL])
        xs = sb("xs", [P, P_RWKV])
        lora = sb("lora", [P, 2 * LORA + GLORA])
        loraT = sb("loraT", [P, 3 * P])
        sa = sb("sa", [P, 2, RW])
        gate_r = sb("gate_r", [P, RW])
        ex = sb("ex", [P, 4, RW])
        pc = sb("pc", [P, PAIRS, 8])
        kk = sb("kk", [P, RW])
        k2 = sb("k2", [P, RW])
        work = sb("work", [P, RW])
        work2 = sb("work2", [P, RW])
        small = sb("small", [P, 8, HEADS])
        bonus = sb("bonus", [P, HEADS])
        fac = sb("fac", [P, 4, RW])
        bk = sb("bk", [P, 2, RW])
        arT = sb("arT", [P, PAIRS, 2 * P])
        bkT = sb("bkT", [P, 2, PAIRS, P])
        pqb = sb("pqb", [P, 2, PAIRS, 2 * P])
        pqk = sb("pqk", [P, 2, PAIRS, 2 * P])
        y = sb("y", [P, RW])
        S = sb("S", [P, PAIRS, P])
        ast = sb("ast", [P, 8, HEADS])
        best = sb("best", [P, 8, TOPK])
        gate = sb("gate", [P, 8, TOPK])
        expert = sb("expert", [P, SLOTS], U32)
        stat = sb("stat", [P, 4])

        def part(buf, at, shape):
            names = "abcd"[:len(buf.shape) - 1]
            flat = buf[tuple([slice(None)] * len(buf.shape))]
            if len(buf.shape) > 2:
                flat = flat.rearrange(f"p {' '.join(names)} -> p ({' '.join(names)})")
            n = math.prod(shape)
            flat = flat[:, at:at + n]
            if len(shape) == 2:
                flat = flat.rearrange("p (a b) -> p a b", b=shape[1])
            if len(shape) == 3:
                flat = flat.rearrange("p (a b c) -> p a b c", b=shape[1], c=shape[2])
            return flat

        bT, kT = bkT[:, 0, :, :], bkT[:, 1, :, :]
        x2, tn = part(bkT, 0, (D,)), part(bk, 0, (D,))
        pw, pwT = part(ex, 0, (2, HEADS, P)), part(fac, 0, (2, HEADS, P))
        X = part(p_cur, 0, (HEADS, P))
        rpT = part(p_cur, HEADS * P, (PAIRS, P))
        mu = part(pqb, 0, (P_RWKV,))
        kac = part(pqk, 0, (RW,))
        cat = part(sa, 0, (D,))
        qT = part(kk, 0, (PAIRS, P))
        big = part(pqb, 0, (16, P))
        gain = part(pqb, 0, (D,))
        s12 = part(pqk, 0, (16, P))
        aT = part(arT, 0, (KC, P))
        wring = [part(buf, at, (D,)) for buf, at in ((ex, 0), (ex, D), (fac, 0), (fac, D), (p_cur, 0), (xs, 0))]
        hot = part(pqb, 0, (TOPK, NCAND))
        candb, cidx = part(pqk, 0, (8, NCAND)), part(pqk, 8 * NCAND, (8, NCAND))
        v16, i16f, f16 = (part(fac, n * 256, (16, TOPK)) for n in range(3))
        i16 = i16f.bitcast(U32)
        pos, posf, expf = (part(fac, 768 + n * 128, (8, TOPK)) for n in range(3))
        pos = pos.bitcast(U32)
        gsum = part(fac, 1160, (2, 8))
        cand = part(fac, 1280, (8, NCAND))

        ps = ctx.enter_context(nc.psum_tensor("mx_ps", [P, 8, 512], F32))
        bank = lambda n: ps[:, n, :]
        banks = lambda n, m: ps[:, n:n + m, :].rearrange("p b n -> p (b n)")
        ones = lambda at: loraT[at:at + 1, 2 * P:3 * P]
        v_of = lambda h: xs[:, 2 * RW + h * HD:2 * RW + (h + 1) * HD]
        GB = (0, 1, 4, 5)

        consts = flag("mix_consts")
        copied = flag("copied")
        ones_ready = flag("ones_ready")
        late_consts = flag("late_consts")
        tile_end = flag("mix_tile_end", 4)
        p_in = flag("p_in", 16)
        prev_in = flag("prev_in", 16)
        prev_fix = flag("prev_fix")
        vec_in = flag("vec_in", 16 * 2)
        kv_in = flag("kv_in", 16)
        kv_in2 = flag("kv_in2")
        mask_in = flag("mask_in", 16)
        xs_ready = flag("xs_ready")
        lora_in = flag("lora_in")
        loraT_out = flag("loraT_out")
        loraT_ready = flag("loraT_ready")
        lora_out = flag("lora_out", 2)
        kkc_out = flag("kkc_out")
        sig_ready = flag("sig_ready")
        gate_ready = flag("gate_ready")
        cum_done = flag("cum_done")
        exps_ready = flag("exps_ready", 5)
        kk_ss = flag("kk_ss")
        kk_norm = flag("kk_norm")
        factors = flag("factors", 5)
        facT_out = flag("facT_out", 4)
        facT_ready = flag("facT_ready", 4)
        pb_out = flag("pb_out", 2)
        pk_out = flag("pk_out", 2)
        pqb_ready = flag("pqb_ready", 2)
        pqk_ready = flag("pqk_ready", 2)
        n_out = flag("n_out")
        w0_out = flag("w0_out")
        n_ready = flag("n_ready")
        x0_ready = flag("x0_ready")
        sq_out = flag("sq_out", 4, 3)
        sq_ready = flag("sq_ready", 4, 3)
        ap_out = flag("ap_out", 5, 4)
        x_ready = flag("x_ready", 5, 4)
        rp_out = flag("rp_out")
        y0_out = flag("y0_out")
        rp_ready = flag("rp_ready")
        y0_ready = flag("y0_ready")
        gh_out = flag("gh_out", 4, SAMPLES)
        g_ready = flag("g_ready", 4, SAMPLES)
        h_ready = flag("h_ready", 4, SAMPLES)
        st_out = flag("st_out", 4, SAMPLES)
        s_ready = flag("s_ready", 4, SAMPLES)
        s_zeroed = flag("s_zeroed")
        s_loaded = flag("s_loaded")
        s_stored = flag("s_stored")
        gn_var = flag("gn_var")
        gn_std = flag("gn_std")
        y_done = flag("y_done")
        qkT_out = flag("qkT_out")
        qkT_ready = flag("qkT_ready")
        sc_out = flag("sc_out", 8)
        max_ready = flag("max_ready", 8)
        pr_ready = flag("pr_ready", 8)
        prT_out = flag("prT_out", 8)
        prT_ready = flag("prT_ready", 8)
        o_out = flag("o_out", 8)
        sink_in = flag("sink_in")
        sink_exp = flag("sink_exp")
        o_var = flag("o_var")
        o_std = flag("o_std")
        cat_ready = flag("cat_ready")
        dve_link = flag("mix_dve_link", DVE_LINKS, DVE_LINKS_SAMPLE)
        gain_in = flag("gain_in", 16)
        x_in = flag("xr_in", 16)
        w_loaded = [flag(f"w_loaded{n}", 16 * 24 // WRING) for n in range(WRING)]
        w_used = flag("w_used", 24)
        mT_out = flag("mT_out")
        mT_ready = flag("mT_ready")
        wo_out = flag("wo_out")
        ssq_ready = flag("ssq_ready")
        std_ready = flag("std_p_ready")
        tn_ready = flag("tn_ready")
        tT_out = flag("tT_out")
        tT_ready = flag("tT_ready")
        q_out = flag("q_out", 4)
        q_ready = flag("q_ready", 4)
        sco_out = flag("sco_out", 4)
        sco_ready = flag("sco_ready", 4)
        smax_in = flag("smax_in")
        sexp = flag("sexp")
        route_link = flag("route_dve_link", ROUTE_LINKS)
        passed = flag("dve_passed")
        handed = flag("handed", 2)
        down_in = [flag(f"down_in{r}", 16 * len(range(r, SLOTS, DOWN_RING))) for r in range(DOWN_RING)]
        up_in = [flag(f"up_in{r}", 16 * len(range(r, SLOTS, UP_RING))) for r in range(UP_RING)]
        row_free = flag("row_free")
        dotted = flag("dotted", SLOTS)
        gelued = flag("gelued", SLOTS)
        coefs = flag("coefs", SLOTS)
        diags = flag("diags", len(ON_PE))
        pe_used = flag("pe_used", len(ON_PE))
        dve_used = flag("dve_used", len(ON_VECTOR))
        ssq2_ready = flag("ssq2_ready")
        std2_ready = flag("std2_ready")
        y_ready = flag("y_ready")
        y_stored = flag("y_stored", 16)
        end_link = flag("end_dve_link", END_LINKS)

        proj = A["proj"]

        def mix_sync(sp, t, m, src):
            sample = m["sample"]
            if not sample:
                sp.wait_ge(tile_end.sem, tile_end.due(t, 0))
            sp.dma_start(p_cur[:, :], proj[bass.ds(P + src, P), :]).then_inc(p_in.sem, 16)
            sp.dma_start(xs[:, :], proj[bass.ds(P - 1 + src, P), 0:P_RWKV]).then_inc(prev_in.sem, 16)
            for dst, name in ((mu, "mu"), (kac, "k_a")):
                sp.dma_start(dst, row(A[name]).to_broadcast([P, A[name].shape[0]])).then_inc(vec_in.sem, 16)
            if sample:
                sp.wait_ge(prev_in.sem, prev_in.due(t, 16))
                sp.dma_start(xs[0:P:STEPS, :], A["state_shift"]).then_inc(prev_fix.sem, 16)
                for b in range(SAMPLES):
                    sp.dma_start(m["kv"][:, b, 0:P], A["cache_k"][b]).then_inc(kv_in2.sem, 16)
                    sp.dma_start(m["kv"][:, b, P:2 * P], A["cache_v"][b]).then_inc(kv_in2.sem, 16)
                sp.dma_start(m["kv"][:, SAMPLES, :], proj[bass.ds(P + src, P), K0:P_TOTAL]).then_inc(kv_in.sem, 16)
                sp.dma_start(m["amask"][:, :], A["mask_sample"]).then_inc(mask_in.sem, 16)
                sp.wait_ge(s_zeroed.sem, 1)
                for b in range(SAMPLES):
                    for o in range(2):
                        sp.dma_start(m["S"](b)[o * HD:(o + 1) * HD, :, o * HD:(o + 1) * HD],
                                     A["state_wkvT"][b, o]).then_inc(s_loaded.sem, 16)
            else:
                sp.dma_start(m["kv"][:, :, :], proj[bass.ds(src, 2 * P), K0:P_TOTAL]
                             .rearrange("(n p) c -> p n c", p=P)).then_inc(kv_in.sem, 16)
                sp.dma_start(m["amask"][:, :], A["mask_prompt"][bass.ds(src, P), :]).then_inc(mask_in.sem, 16)

        def mix_scalar(act, t, m, slots):
            sample, nk, width = m["sample"], m["nk"], m["width"]
            blocks = lambda ap, n: ap.rearrange("p (a n) -> p a n", n=n)
            if not sample:
                act.wait_ge(tile_end.sem, tile_end.due(t, 0))
            slots.upto(1)
            act.wait_ge(xs_ready.sem, xs_ready.due(t, 1))
            act.activation(lora[:, 0:LORA], xs[:, 3 * RW:3 * RW + LORA], ACT.Tanh)
            act.activation(lora[:, LORA:2 * LORA], xs[:, 3 * RW + LORA:3 * RW + 2 * LORA], ACT.Copy)
            act.activation(lora[:, 2 * LORA:], xs[:, 3 * RW + 2 * LORA:P_RWKV], ACT.Sigmoid)\
               .then_inc(lora_in.sem, 1)
            slots.upto(2)
            act.wait_ge(loraT_out.sem, loraT_out.due(t, 1))
            act.activation(loraT[:, 0:2 * P], ps[:, 0, 0:2 * P], ACT.Copy)
            act.activation(loraT[0:GLORA - P, 2 * P:3 * P], ps[0:GLORA - P, 0, 2 * P:3 * P], ACT.Copy)\
               .then_inc(loraT_ready.sem, 1)
            slots.upto(3)
            act.wait_ge(kk_ss.sem, kk_ss.due(t, 1))
            act.activation(small[:, 1, :], small[:, 0, :], ACT.Sqrt).then_inc(kk_norm.sem, 1)
            act.wait_ge(lora_out.sem, lora_out.due(t, 1))
            act.activation(sa[:, :, :], ps[:, 1:3, :], ACT.Sigmoid).then_inc(sig_ready.sem, 1)
            act.wait_ge(lora_out.sem, lora_out.due(t, 2))
            act.activation(gate_r[:, :], bank(3), ACT.Copy).then_inc(gate_ready.sem, 1)
            slots.upto(5)
            act.wait_ge(cum_done.sem, cum_done.due(t, 1))
            act.activation(ex[:, 1, :], bank(4), ACT.Exp).then_inc(exps_ready.sem, 1)
            act.activation(ex[:, 2, :], bank(5), ACT.Exp, scale=-1.0).then_inc(exps_ready.sem, 1)
            act.activation(ex[:, 0, :], bank(5), ACT.Exp).then_inc(exps_ready.sem, 1)
            act.activation(ex[:, 3, :], bank(0), ACT.Exp).then_inc(exps_ready.sem, 1)
            act.activation(pc[:, :, :], blocks(ps[:, 1, 0:32], 8), ACT.Exp).then_inc(exps_ready.sem, 1)
            slots.upto(7)
            for n, dst in enumerate((arT[:, :, 0:P], arT[:, :, P:2 * P], bT, kT)):
                act.wait_ge(facT_out.sem, facT_out.due(t, n + 1))
                act.activation(dst, blocks(bank(2 + n), P), ACT.Copy).then_inc(facT_ready.sem, 1)
            for o in range(2):
                act.activation(X[:, 4 * o:4 * o + 4, 0:HD],
                               fac[:, 0, :].rearrange("p (q o c) -> p o q c", o=2, c=HD)[:, o], ACT.Copy)
            slots.upto(11)
            act.wait_ge(w0_out.sem, w0_out.due(t, 1))
            act.activation(X[:, :, HD:P], blocks(bank(4), HD), ACT.Copy).then_inc(x0_ready.sem, 1)
            for i in range(m["applied"] - 1):
                slots.upto(12 + i)
                act.wait_ge(sq_out.sem, sq_out.due(t, i + 1))
                if i:
                    act.wait_ge(ap_out.sem, ap_out.due(t, i))
                ins = act.activation(pwT[:, i % 2, :, :], blocks(banks(2, 2), P), ACT.Copy)
                if i < m["applied"] - 2:
                    ins = act.activation(pw[:, (i + 1) % 2, :, :], blocks(banks(4, 2), P), ACT.Copy)
                ins.then_inc(sq_ready.sem, 1)
            slots.upto(17)
            act.wait_ge(y0_out.sem, y0_out.due(t, 1))
            act.activation(y[:, :], bank(3), ACT.Copy).then_inc(y0_ready.sem, 1)
            for n in range(m["maps"]):
                slots.upto(18 + n)
                if n >= 4:
                    act.wait_ge(st_out.sem, st_out.due(t, n - 3))
                    act.wait_ge(s_ready.sem, s_ready.due(t, n - 3))
                act.wait_ge(g_ready.sem, g_ready.due(t, n + 1))
                for o in range(2):
                    q = slice(o * HD, (o + 1) * HD)
                    ins = act.activation(H[q, n % 4, :, q], blocks(ps[q, GB[n % 4], 256:512], HD), ACT.Copy)
                ins.then_inc(h_ready.sem, 1)
            slots.upto(26)
            act.wait_ge(gn_var.sem, gn_var.due(t, 1))
            act.activation(small[:, 5, :], small[:, 4, :], ACT.Sqrt).then_inc(gn_std.sem, 1)
            slots.upto(28)
            act.wait_ge(qkT_out.sem, qkT_out.due(t, 1))
            act.activation(qT[:, :, :], blocks(bank(1), P), ACT.Copy)
            act.activation(m["keyT"], banks(m["kt_bank"], 3)[:, 0:nk * P], ACT.Copy).then_inc(qkT_ready.sem, 1)
            for h in range(HEADS):
                d = h % 2
                slots.upto(29 + h)
                act.wait_ge(max_ready.sem, max_ready.due(t, h + 1))
                act.activation(m["sc"][d], m["sc"][d], ACT.Exp, bias=ast[:, 2, h:h + 1],
                               scale=SCALE, accum_out=ast[:, 3, h:h + 1]).then_inc(pr_ready.sem, 1)
                act.wait_ge(prT_out.sem, prT_out.due(t, h + 1))
                act.activation(m["prT"][d], bank(m["prT_bank"][d])[:, 0:width],
                               ACT.Copy).then_inc(prT_ready.sem, 1)
            slots.upto(37)
            act.wait_ge(sink_in.sem, sink_in.due(t, 1))
            act.activation(ast[:, 4, :], ast[:, 4, :], ACT.Exp).then_inc(sink_exp.sem, 1)
            slots.upto(38)
            act.wait_ge(o_var.sem, o_var.due(t, 1))
            act.activation(ast[:, 6, :], ast[:, 6, :], ACT.Sqrt).then_inc(o_std.sem, 1)

        def mix_vector(dve, t, m, slots):
            link = Link(dve, dve_link, t)
            sample, nk, width = m["sample"], m["nk"], m["width"]
            B = lambda c, n: bc[:, c:c + n]
            h3 = lambda ap: ap.rearrange("p (h c) -> p h c", c=HD)
            blocks = lambda ap, n: ap.rearrange("p (a n) -> p a n", n=n)
            per_head = lambda ap: ap.unsqueeze(2).to_broadcast([P, HEADS, HD])
            r, k, vv = (xs[:, n * RW:(n + 1) * RW] for n in range(3))
            slots.upto(1)
            dve.wait_ge(p_in.sem, p_in.due(t, 16))
            dve.wait_ge(prev_in.sem, prev_in.due(t, 16))
            dve.wait_ge(vec_in.sem, vec_in.due(t, 16 * 2))
            if sample:
                dve.wait_ge(prev_fix.sem, 16)
            link(dve.tensor_tensor(xs[:, :], xs[:, :], p_cur[:, 0:P_RWKV], ALU.subtract))
            link(dve.tensor_tensor(xs[:, :], xs[:, :], mu, ALU.mult))
            dve.tensor_tensor(xs[:, :], xs[:, :], p_cur[:, 0:P_RWKV], ALU.add).then_inc(xs_ready.sem, 1)
            dve.wait_ge(xs_ready.sem, xs_ready.due(t, 1))
            dve.wait_ge(kkc_out.sem, kkc_out.due(t, 1))
            link(dve.tensor_tensor(kk[:, :], k, bank(4), ALU.mult))
            link(dve.tensor_tensor(work[:, :], kk[:, :], kk[:, :], ALU.mult))
            dve.tensor_reduce(small[:, 0, :], h3(work[:, :]), AX.X, ALU.add).then_inc(kk_ss.sem, 1)
            slots.upto(3)
            dve.wait_ge(kk_norm.sem, kk_norm.due(t, 1))
            link(dve.tensor_scalar(small[:, 1, :], small[:, 1, :], L2_EPS, None, ALU.max))
            link(dve.reciprocal(small[:, 1, :], small[:, 1, :]))
            link(dve.tensor_tensor(h3(kk[:, :]), h3(kk[:, :]), per_head(small[:, 1, :]), ALU.mult))
            slots.upto(4)
            dve.wait_ge(sig_ready.sem, sig_ready.due(t, 1))
            a = sa[:, 1, :]
            link(dve.scalar_tensor_tensor(out=work[:, :], in0=a, scalar=-1.0, in1=kac, op0=ALU.add, op1=ALU.mult))
            link(dve.scalar_tensor_tensor(out=k2[:, :], in0=work[:, :], scalar=1.0, in1=k, op0=ALU.add, op1=ALU.mult))
            link(dve.tensor_tensor(work2[:, :], kk[:, :], a, ALU.mult))
            link(dve.tensor_tensor(work[:, :], r, k2[:, :], ALU.mult))
            link(dve.tensor_tensor(work[:, :], work[:, :], B(RKC, RW), ALU.mult))
            dve.tensor_reduce(bonus[:, :], h3(work[:, :]), AX.X, ALU.add)
            slots.upto(5)
            dve.wait_ge(exps_ready.sem, exps_ready.due(t, 1))
            dve.scalar_tensor_tensor(out=fac[:, 0, :], in0=kk[:, :], scalar=-1.0, in1=ex[:, 1, :],
                                     op0=ALU.mult, op1=ALU.mult).then_inc(factors.sem, 1)
            dve.wait_ge(exps_ready.sem, exps_ready.due(t, 3))
            dve.tensor_tensor(fac[:, 1, :], r, ex[:, 0, :], ALU.mult).then_inc(factors.sem, 1)
            dve.tensor_tensor(fac[:, 2, :], work2[:, :], ex[:, 2, :], ALU.mult).then_inc(factors.sem, 1)
            dve.tensor_tensor(fac[:, 3, :], k2[:, :], ex[:, 2, :], ALU.mult).then_inc(factors.sem, 1)
            slots.upto(6)
            dve.wait_ge(exps_ready.sem, exps_ready.due(t, 4))
            for n, f in enumerate((work2, k2)):
                if sample:
                    link(dve.tensor_tensor(bk[:, n, :], f[:, :], ex[:, 3, :], ALU.mult))
                    dve.tensor_scalar(m["bk_odd"][:, n, :], bk[:, n, :], m["rowm"][:, 1:2], None, ALU.mult)
                    ins = dve.tensor_scalar(bk[:, n, :], bk[:, n, :], m["rowm"][:, 0:1], None, ALU.mult)
                else:
                    ins = dve.tensor_tensor(bk[:, n, :], f[:, :], ex[:, 3, :], ALU.mult)
            ins.then_inc(factors.sem, 1)
            m2 = rc[:, MASK2:MASK2 + 2 * P].unsqueeze(1).to_broadcast([P, PAIRS, 2 * P])
            at = 8
            for dst, out, ready, first in ((pqb, pb_out, pqb_ready, (0, 2)), (pqk, pk_out, pqk_ready, (4, 0))):
                for o in range(2):
                    slots.upto(at)
                    at += 1 if o == 0 else 0
                    dve.wait_ge(out.sem, out.due(t, o + 1))
                    dve.tensor_tensor(dst[:, o, :, :], blocks(banks(first[o], 2), 2 * P), m2, ALU.mult)\
                       .then_inc(ready.sem, 1)
            slots.upto(10)
            dve.wait_ge(n_out.sem, n_out.due(t, 1))
            dve.tensor_tensor(pw[:, 0, :, :], blocks(banks(2, 2), P),
                              rc[:, MASKN:MASKN + P].unsqueeze(1).to_broadcast([P, HEADS, P]), ALU.mult)\
               .then_inc(n_ready.sem, 1)
            for i in range(m["applied"]):
                slots.upto(12 + i)
                if i == 0:
                    dve.wait_ge(x0_ready.sem, x0_ready.due(t, 1))
                dve.wait_ge(ap_out.sem, ap_out.due(t, i + 1))
                dve.tensor_tensor(X, X, blocks(banks(0, 2), P), ALU.add).then_inc(x_ready.sem, 1)
            slots.upto(17)
            dve.wait_ge(rp_out.sem, rp_out.due(t, 1))
            ins = dve.tensor_tensor(rpT, blocks(bank(2), P), arT[:, :, P:2 * P], ALU.add)
            if sample:
                link(ins)
                cm = lambda e: m["colm"][:, e, :].unsqueeze(1).to_broadcast([P, PAIRS, P])
                dve.tensor_tensor(m["rpT_odd"][:, :, :], rpT, cm(1), ALU.mult)
                ins = dve.tensor_tensor(rpT, rpT, cm(0), ALU.mult)
            ins.then_inc(rp_ready.sem, 1)

            def state_map(n):
                dve.wait_ge(gh_out.sem, gh_out.due(t, n + 1))
                b = m["column"](n)
                for o in range(2):
                    s = slice(o * HD, (o + 1) * HD)
                    for q in range(PAIRS):
                        ins = dve.scalar_tensor_tensor(out=G[s, n % 4, q, s], in0=ident2[s, :],
                                                       scalar=pc[s, q, b:b + 1],
                                                       in1=ps[s, GB[n % 4], q * HD:(q + 1) * HD],
                                                       op0=ALU.mult, op1=ALU.add)
                ins.then_inc(g_ready.sem, 1)

            def next_state(n):
                dve.wait_ge(st_out.sem, st_out.due(t, n + 1))
                dve.wait_ge(h_ready.sem, h_ready.due(t, n + 1))
                dve.tensor_tensor(m["S"](m["column"](n)), blocks(bank(2 + n % 2), P), H[:, n % 4, :, :], ALU.add)\
                   .then_inc(s_ready.sem, 1)

            for n in range(4):
                slots.upto(18 + n)
                state_map(n)
            for n in range(m["maps"]):
                slots.upto(22 + n)
                next_state(n)
                if n + 4 < m["maps"]:
                    state_map(n + 4)
            dve.wait_ge(y0_ready.sem, y0_ready.due(t, 1))
            link(dve.tensor_tensor(y[:, :], y[:, :], bank(m["y_bank"]), ALU.add))
            link(dve.tensor_reduce(small[:, 2, :], h3(y[:, :]), AX.X, ALU.add))
            link(dve.tensor_scalar(small[:, 2, :], small[:, 2, :], 1.0 / HD, None, ALU.mult))
            link(dve.tensor_tensor(h3(y[:, :]), h3(y[:, :]), per_head(small[:, 2, :]), ALU.subtract))
            link(dve.tensor_tensor(work[:, :], y[:, :], y[:, :], ALU.mult))
            link(dve.tensor_reduce(small[:, 3, :], h3(work[:, :]), AX.X, ALU.add))
            dve.tensor_scalar(small[:, 4, :], small[:, 3, :], 1.0 / HD, LN_EPS, ALU.mult, ALU.add)\
               .then_inc(gn_var.sem, 1)
            link(dve.tensor_tensor(h3(work[:, :]), per_head(bonus[:, :]), h3(vv), ALU.mult))
            slots.upto(27)
            dve.wait_ge(gn_std.sem, gn_std.due(t, 1))
            link(dve.reciprocal(small[:, 5, :], small[:, 5, :]))
            link(dve.tensor_tensor(h3(y[:, :]), h3(y[:, :]), per_head(small[:, 5, :]), ALU.mult))
            link(dve.tensor_tensor(y[:, :], y[:, :], B(LNW, RW), ALU.mult))
            link(dve.tensor_tensor(y[:, :], y[:, :], B(LNB, RW), ALU.add))
            link(dve.tensor_tensor(y[:, :], y[:, :], work[:, :], ALU.add))
            dve.wait_ge(gate_ready.sem, gate_ready.due(t, 1))
            dve.tensor_tensor(cat[:, 0:RW], y[:, :], gate_r[:, :], ALU.mult).then_inc(y_done.sem, 1)
            dve.wait_ge(mask_in.sem, mask_in.due(t, 16))
            for h in range(HEADS):
                d = h % 2
                slots.upto(29 + h)
                dve.wait_ge(sc_out.sem, sc_out.due(t, h + 1))
                if h >= 2:
                    dve.wait_ge(prT_out.sem, prT_out.due(t, h - 1))
                link(dve.tensor_tensor(m["sc"][d], bank(m["sc_bank"][d])[:, 0:width],
                                       m["amask"][:, :], ALU.add))
                link(dve.tensor_reduce(ast[:, 0, h:h + 1], m["sc"][d], AX.X, ALU.max))
                link(dve.tensor_scalar(ast[:, 1, h:h + 1], ast[:, 0, h:h + 1], SCALE, bc[:, SINK + h:SINK + h + 1],
                                       ALU.mult, ALU.max))
                dve.tensor_scalar(ast[:, 2, h:h + 1], ast[:, 1, h:h + 1], -1.0, None, ALU.mult)\
                   .then_inc(max_ready.sem, 1)
            slots.upto(37)
            dve.tensor_tensor(ast[:, 4, :], B(SINK, HEADS), ast[:, 1, :], ALU.subtract).then_inc(sink_in.sem, 1)
            dve.wait_ge(sink_exp.sem, sink_exp.due(t, 1))
            link(dve.tensor_tensor(ast[:, 5, :], ast[:, 3, :], ast[:, 4, :], ALU.add))
            link(dve.reciprocal(ast[:, 5, :], ast[:, 5, :]))
            dve.wait_ge(o_out.sem, o_out.due(t, 8))
            link(dve.tensor_tensor(h3(y[:, :]), h3(bank(m["o_bank"])), per_head(ast[:, 5, :]), ALU.mult))
            link(dve.tensor_tensor(work[:, :], y[:, :], y[:, :], ALU.mult))
            link(dve.tensor_reduce(ast[:, 6, :], h3(work[:, :]), AX.X, ALU.add))
            dve.tensor_scalar(ast[:, 6, :], ast[:, 6, :], 1.0 / HD, RMS_EPS, ALU.mult, ALU.add)\
               .then_inc(o_var.sem, 1)
            slots.upto(38)
            dve.wait_ge(o_std.sem, o_std.due(t, 1))
            link(dve.reciprocal(ast[:, 7, :], ast[:, 6, :]))
            link(dve.tensor_tensor(h3(y[:, :]), h3(y[:, :]), per_head(ast[:, 7, :]), ALU.mult))
            dve.tensor_tensor(cat[:, RW:D], y[:, :], B(OUTG, RW), ALU.mult).then_inc(cat_ready.sem, 1)
            link.close()

        def mix_tensor(pe, t, m, slots):
            sample, nk, width = m["sample"], m["nk"], m["width"]
            half = lambda o: slice(o * HD, (o + 1) * HD)
            if not sample:
                pe.wait_ge(tile_end.sem, tile_end.due(t, 0))
            pe.matmul(bank(4), ones(KK_ROW), g2b[KK_ROW:KK_ROW + 1, :], start=True, stop=True,
                      tile_position=(KK_ROW, 0)).then_inc(kkc_out.sem, 1)
            slots.upto(2)
            pe.wait_ge(lora_in.sem, lora_in.due(t, 1))
            pe.transpose(ps[:, 0, 0:P], lora[:, 0:P], ident[:, :])
            pe.transpose(ps[:, 0, P:2 * P], lora[:, P:2 * P], ident[:, :])
            pe.transpose(ps[0:GLORA - P, 0, 2 * P:3 * P], lora[:, 2 * P:], ident[:, :]).then_inc(loraT_out.sem, 1)
            slots.upto(3)
            pe.wait_ge(loraT_ready.sem, loraT_ready.due(t, 1))
            for n, at in enumerate((W0_ROW, A0_ROW)):
                pe.matmul(bank(1 + n), loraT[:, 0:P], w2a2[:, n * RW:(n + 1) * RW], start=True, stop=False)
                last = pe.matmul(bank(1 + n), ones(at), g2b[at:at + 1, :], start=False, stop=True,
                                 tile_position=(at, 0))
            last.then_inc(lora_out.sem, 1)
            pe.matmul(bank(3), loraT[:, P:2 * P], g2a[:, :], start=True, stop=False)
            pe.matmul(bank(3), loraT[0:GLORA - P, 2 * P:3 * P], g2b[0:GLORA - P, :], start=False, stop=True)\
              .then_inc(lora_out.sem, 1)
            slots.upto(5)
            pe.wait_ge(sig_ready.sem, sig_ready.due(t, 1))
            pe.matmul(bank(4), rc[:, TRI_X:TRI_X + P], sa[:, 0, :], start=True, stop=True)
            pe.matmul(bank(5), rc[:, TRI_I:TRI_I + P], sa[:, 0, :], start=True, stop=True)
            pe.matmul(bank(0), rc[:, TRI_S:TRI_S + P], sa[:, 0, :], start=True, stop=True)
            for q in range(PAIRS):
                last = pe.matmul(ps[:, 1, 8 * q:8 * q + 8], sa[:, 0, q * P:(q + 1) * P], rc[:, IND:IND + 8],
                                 start=True, stop=True)
            last.then_inc(cum_done.sem, 1)
            slots.upto(7)
            pe.wait_ge(gate_ready.sem, gate_ready.due(t, 1))
            pe.wait_ge(exps_ready.sem, exps_ready.due(t, 5))
            pe.wait_ge(factors.sem, factors.due(t, 5))
            for n in range(4):
                for q in range(PAIRS):
                    last = pe.transpose(ps[:, 2 + n, q * P:(q + 1) * P], fac[:, n, q * P:(q + 1) * P], ident[:, :])
                last.then_inc(facT_out.sem, 1)
            slots.upto(8)
            pe.wait_ge(facT_ready.sem, facT_ready.due(t, 4))

            def products(left, o, first, done):
                for q in range(PAIRS):
                    last = pe.matmul(ps[:, first + q // 2, (q % 2) * 256:(q % 2) * 256 + 256],
                                     left[half(o), q, :], arT[half(o), q, :], start=True, stop=True)
                last.then_inc(done.sem, 1)

            products(bT, 0, 0, pb_out)
            products(bT, 1, 2, pb_out)
            slots.upto(9)
            products(kT, 0, 4, pk_out)
            pe.wait_ge(pqb_ready.sem, pqb_ready.due(t, 1))
            products(kT, 1, 0, pk_out)
            pe.wait_ge(pqb_ready.sem, pqb_ready.due(t, 2))
            slots.upto(10)
            for o in range(2):
                for q in range(PAIRS):
                    last = pe.matmul(ps[:, 2 + o, q * P:(q + 1) * P], arT[half(o), q, 0:P], bT[half(o), q, :],
                                     start=True, stop=True)
            last.then_inc(n_out.sem, 1)
            slots.upto(11)
            pe.wait_ge(pqk_ready.sem, pqk_ready.due(t, 2))
            for o in range(2):
                for q in range(PAIRS):
                    last = pe.matmul(ps[:, 4, (4 * o + q) * HD:(4 * o + q + 1) * HD], pqk[:, o, q, 0:P],
                                     v_of(2 * q + o), start=True, stop=True)
            last.then_inc(w0_out.sem, 1)
            pe.wait_ge(n_ready.sem, n_ready.due(t, 1))
            for i in range(m["applied"]):
                slots.upto(12 + i)
                if i:
                    pe.wait_ge(sq_ready.sem, sq_ready.due(t, i))
                    pe.wait_ge(x_ready.sem, x_ready.due(t, i))
                else:
                    pe.wait_ge(x0_ready.sem, x0_ready.due(t, 1))
                powT = lambda h: pqb[:, h // 4, h % 4, 0:P] if i == 0 else pwT[:, (i - 1) % 2, h, :]
                if i < m["applied"] - 1:
                    for h in range(HEADS):
                        last = pe.matmul(ps[:, 2 + h // 4, (h % 4) * P:(h % 4 + 1) * P], pw[:, i % 2, h, :], powT(h),
                                         start=True, stop=True)
                    for h in range(HEADS if i < m["applied"] - 2 else 0):
                        last = pe.matmul(ps[:, 4 + h // 4, (h % 4) * P:(h % 4 + 1) * P], powT(h), pw[:, i % 2, h, :],
                                         start=True, stop=True)
                    last.then_inc(sq_out.sem, 1)
                for h in range(HEADS):
                    last = pe.matmul(ps[:, h // 4, (h % 4) * P:(h % 4 + 1) * P], powT(h), X[:, h, :],
                                     start=True, stop=True)
                last.then_inc(ap_out.sem, 1)
            slots.upto(17)
            pe.wait_ge(x_ready.sem, x_ready.due(t, m["applied"]))
            for o in range(2):
                for q in range(PAIRS):
                    last = pe.matmul(ps[half(o), 2, q * P:(q + 1) * P], X[:, 4 * o + q, 0:HD], pqb[:, o, q, P:2 * P],
                                     start=True, stop=True)
            last.then_inc(rp_out.sem, 1)
            for h in range(HEADS):
                o, q = h % 2, h // 2
                pe.matmul(ps[:, 3, h * HD:(h + 1) * HD], pqb[:, o, q, P:2 * P], X[:, 4 * o + q, HD:P],
                          start=True, stop=False)
                last = pe.matmul(ps[:, 3, h * HD:(h + 1) * HD], pqk[:, o, q, P:2 * P], v_of(h),
                                 start=False, stop=True)
            last.then_inc(y0_out.sem, 1)

            def transition(n):
                b = n % 4
                factor = m["bk_odd"] if n >= 4 else bk
                rows = slice(32 * b, 32 * b + 32)
                for h in range(HEADS):
                    o, q = h % 2, h // 2
                    beta = factor[rows, 0, h * HD:(h + 1) * HD]
                    kappa = factor[rows, 1, h * HD:(h + 1) * HD]
                    value = xs[rows, 2 * RW + h * HD:2 * RW + (h + 1) * HD]
                    tp = (32 * b, o * HD)
                    pe.matmul(ps[half(o), GB[b], q * HD:(q + 1) * HD], X[rows, 4 * o + q, 0:HD], beta,
                              start=True, stop=True, tile_position=tp)
                    pe.matmul(ps[half(o), GB[b], 256 + q * HD:256 + (q + 1) * HD], beta, X[rows, 4 * o + q, HD:P],
                              start=True, stop=False, tile_position=tp)
                    last = pe.matmul(ps[half(o), GB[b], 256 + q * HD:256 + (q + 1) * HD], kappa, value,
                                     start=False, stop=True, tile_position=tp)
                last.then_inc(gh_out.sem, 1)

            def state_product(n):
                for q in range(PAIRS):
                    last = pe.matmul(ps[:, 2 + n % 2, q * P:(q + 1) * P], G[:, n % 4, q, :],
                                     m["S"](m["column"](n))[:, q, :],
                                     start=True, stop=True)
                last.then_inc(st_out.sem, 1)

            for n in range(4):
                slots.upto(18 + n)
                transition(n)
            pe.wait_ge(rp_ready.sem, rp_ready.due(t, 1))
            pe.wait_ge(y0_ready.sem, y0_ready.due(t, 1))
            y_bank = m["y_bank"]
            for n in range(m["maps"]):
                slots.upto(22 + n)
                b, odd = n % 4, n >= 4
                rows = slice(32 * b, 32 * b + 32)
                pe.wait_ge(g_ready.sem, g_ready.due(t, n + 1))
                pe.wait_ge(h_ready.sem, h_ready.due(t, n + 1))
                if sample:
                    if n == 0:
                        pe.wait_ge(s_loaded.sem, 32 * SAMPLES)
                    if n >= 2:
                        pe.wait_ge(s_ready.sem, s_ready.due(t, n - 1))
                elif n:
                    pe.wait_ge(s_ready.sem, s_ready.due(t, n))
                for q in range(PAIRS):
                    pe.matmul(ps[rows, y_bank, q * P:(q + 1) * P], (m["rpT_odd"] if odd else rpT)[:, q, rows],
                              m["S"](m["column"](n))[:, q, :], start=not sample or (q == 0 and not odd), stop=not sample or odd,
                              skip_group_check=sample)
                state_product(n)
                if n + 4 < m["maps"]:
                    transition(n + 4)
            slots.upto(28)
            pe.wait_ge(kv_in.sem, kv_in.due(t, 16))
            if sample:
                pe.wait_ge(kv_in2.sem, 16 * 2 * SAMPLES)
            pe.wait_ge(s_ready.sem, s_ready.due(t, m["maps"]))
            for j in range(4):
                pe.transpose(ps[:, 1, j * P:(j + 1) * P], p_cur[:, Q0 + j * P:Q0 + (j + 1) * P], ident[:, :])
            for n in range(nk):
                last = pe.transpose(ps[:, m["kt_bank"] + n // 4, (n % 4) * P:(n % 4 + 1) * P],
                                    m["kv"][:, n, 0:P], ident[:, :])
            last.then_inc(qkT_out.sem, 1)

            def scores(h):
                g = h // 4
                if h >= 2:
                    pe.wait_ge(max_ready.sem, max_ready.due(t, h - 1))
                out = m["sc_bank"][h % 2]
                if sample:
                    for j in range(4):
                        pe.matmul(ps[32 * j:32 * j + 32, out, 0:2 * P], qT[half(g), h % 4, 32 * j:32 * j + 32],
                                  m["keyT"][half(g), 2 * j * P:(2 * j + 2) * P], start=True, stop=True,
                                  tile_position=(g * HD, 32 * j))
                    last = pe.matmul(ps[:, out, 2 * P:3 * P], qT[half(g), h % 4, :],
                                     m["keyT"][half(g), SAMPLES * P:], start=True, stop=True)
                else:
                    last = pe.matmul(ps[:, out, 0:width], qT[half(g), h % 4, :], m["keyT"][half(g), :],
                                     start=True, stop=True)
                last.then_inc(sc_out.sem, 1)

            pe.wait_ge(qkT_ready.sem, qkT_ready.due(t, 1))
            scores(0)
            pe.wait_ge(y_done.sem, y_done.due(t, 1))
            for h in range(HEADS):
                g, d = h // 4, h % 2
                if h + 1 < HEADS:
                    scores(h + 1)
                slots.upto(29 + h)
                pe.wait_ge(pr_ready.sem, pr_ready.due(t, h + 1))
                if h >= 2:
                    pe.wait_ge(prT_ready.sem, prT_ready.due(t, h - 1))
                for n in range(width // P):
                    last = pe.transpose(ps[:, m["prT_bank"][d], n * P:(n + 1) * P],
                                        m["sc"][d][:, n * P:(n + 1) * P], ident[:, :])
                last.then_inc(prT_out.sem, 1)
                pe.wait_ge(prT_ready.sem, prT_ready.due(t, h + 1))
                out, values = slice(h * HD, (h + 1) * HD), slice(P + g * HD, P + (g + 1) * HD)
                if sample:
                    for j in range(4):
                        rows = slice(32 * j, 32 * j + 32)
                        for n, block in enumerate((2 * j, 2 * j + 1, SAMPLES)):
                            last = pe.matmul(ps[rows, m["o_bank"], out],
                                             m["prT"][d][:, n * P + 32 * j:n * P + 32 * j + 32],
                                             m["kv"][:, block, values], start=n == 0, stop=n == 2,
                                             tile_position=(0, 32 * j))
                else:
                    for n in range(nk):
                        last = pe.matmul(ps[:, m["o_bank"], out], m["prT"][d][:, n * P:(n + 1) * P],
                                         m["kv"][:, n, values], start=n == 0, stop=n == nk - 1)
                last.then_inc(o_out.sem, 1)

        def w_block(n):
            return A["w_out"][n * P:(n + 1) * P, :] if n < KC else A["w_q"][n - KC]

        def route_sync(sp, t, xrow):
            sp.wait_ge(y_done.sem, y_done.due(t, 1))
            sp.dma_start(x2[:, :], A["x"][bass.ds(xrow, P), :]).then_inc(x_in.sem, 16)
            sp.dma_start(gain, row(A["norm_ffn"]).to_broadcast([P, D])).then_inc(gain_in.sem, 16)
            for n in range(24):
                if n >= WRING:
                    sp.wait_ge(w_used.sem, w_used.due(t, n - WRING + 1))
                sp.dma_start(wring[n % WRING], w_block(n)).then_inc(w_loaded[n % WRING].sem, 16)

        def route_scalar(act, t, slots):
            blocks = lambda ap: ap.rearrange("p (a n) -> p a n", n=P)
            slots.upto(39)
            act.wait_ge(mT_out.sem, mT_out.due(t, 1))
            act.activation(aT, blocks(banks(0, 2)), ACT.Copy).then_inc(mT_ready.sem, 1)
            slots.upto(42)
            act.wait_ge(ssq_ready.sem, ssq_ready.due(t, 1))
            act.activation(stat[:, 1:2], stat[:, 1:2], ACT.Sqrt).then_inc(std_ready.sem, 1)
            slots.upto(43)
            act.wait_ge(tT_out.sem, tT_out.due(t, 1))
            act.activation(aT, blocks(banks(0, 2)), ACT.Copy).then_inc(tT_ready.sem, 1)
            for g in range(4):
                slots.upto(44 + g)
                act.wait_ge(q_out.sem, q_out.due(t, g + 1))
                act.activation(s12[:, 4 * g:4 * g + 4, :], blocks(bank(2 + g)), ACT.Copy).then_inc(q_ready.sem, 1)
            slots.upto(48)
            for g in range(4):
                act.wait_ge(sco_out.sem, sco_out.due(t, g + 1))
                act.activation(s12[:, 4 * g:4 * g + 4, :], blocks(bank(g)), ACT.Copy).then_inc(sco_ready.sem, 1)
            slots.upto(60)
            act.wait_ge(smax_in.sem, smax_in.due(t, 1))
            act.activation(gate[:, :, :], gate[:, :, :], ACT.Exp).then_inc(sexp.sem, 1)
            act.wait_ge(sexp.sem, sexp.due(t, 1))

        def route_tensor(pe, t, slots):
            def weights(n):
                pe.wait_ge(w_loaded[n % WRING].sem, w_loaded[n % WRING].due(t, 16 * (n // WRING + 1)))
                return wring[n % WRING]

            slots.upto(39)
            pe.wait_ge(cat_ready.sem, cat_ready.due(t, 1))
            for k in range(KC):
                last = pe.transpose(ps[:, k // 4, (k % 4) * P:(k % 4 + 1) * P], cat[:, k * P:(k + 1) * P], ident[:, :])
            last.then_inc(mT_out.sem, 1)
            slots.upto(40)
            pe.wait_ge(mT_ready.sem, mT_ready.due(t, 1))
            for k in range(KC):
                if k == 4:
                    slots.upto(41)
                w = weights(k)
                for n in range(2):
                    last = pe.matmul(bank(2 + n), aT[:, k, :], w[:, n * 512:(n + 1) * 512],
                                     start=k == 0, stop=k == KC - 1)
                last.then_inc(w_used.sem, 1)
            pe.wait_ge(w_used.sem, w_used.due(t, KC))
            pe.sem_inc(wo_out.sem, 1)
            slots.upto(43)
            pe.wait_ge(tn_ready.sem, tn_ready.due(t, 1))
            for k in range(KC):
                last = pe.transpose(ps[:, k // 4, (k % 4) * P:(k % 4 + 1) * P], tn[:, k * P:(k + 1) * P], ident[:, :])
            last.then_inc(tT_out.sem, 1)
            slots.upto(44)
            pe.wait_ge(tT_ready.sem, tT_ready.due(t, 1))
            for g in range(4):
                slots.upto(44 + g)
                for j in range(4):
                    w = weights(KC + 4 * g + j).rearrange("p (k n) -> p k n", n=P)
                    for k in range(KC):
                        last = pe.matmul(ps[:, 2 + g, j * P:(j + 1) * P], w[:, k, :], aT[:, k, :],
                                         start=k == 0, stop=k == KC - 1)
                    last.then_inc(w_used.sem, 1)
                pe.wait_ge(w_used.sem, w_used.due(t, KC + 4 * g + 4))
                pe.sem_inc(q_out.sem, 1)
            slots.upto(48)
            for g in range(4):
                pe.wait_ge(q_ready.sem, q_ready.due(t, g + 1))
                for j in range(4):
                    last = pe.matmul(ps[:, g, j * P:(j + 1) * P], s12[:, 4 * g + j, :], keysT[:, j % 2, :],
                                     start=True, stop=True)
                last.then_inc(sco_out.sem, 1)

        def route_vector(dve, t, slots):
            link = Link(dve, route_link, t)
            slots.upto(42)
            dve.wait_ge(x_in.sem, x_in.due(t, 16))
            dve.wait_ge(gain_in.sem, gain_in.due(t, 16))
            dve.wait_ge(wo_out.sem, wo_out.due(t, 1))
            link(dve.tensor_tensor(x2[:, :], x2[:, :], banks(2, 2), ALU.add))
            link(dve.tensor_tensor_reduce(out=tn[:, :], in0=x2[:, :], in1=x2[:, :], scale=1.0, scalar=0.0,
                                          op0=ALU.mult, op1=ALU.add, accum_out=stat[:, 0:1]))
            dve.tensor_scalar(stat[:, 1:2], stat[:, 0:1], 1.0 / D, RMS_EPS, ALU.mult, ALU.add)\
               .then_inc(ssq_ready.sem, 1)
            dve.wait_ge(std_ready.sem, std_ready.due(t, 1))
            link(dve.reciprocal(stat[:, 1:2], stat[:, 1:2]))
            dve.scalar_tensor_tensor(out=tn[:, :], in0=x2[:, :], scalar=stat[:, 1:2], in1=gain,
                                     op0=ALU.mult, op1=ALU.mult).then_inc(tn_ready.sem, 1)
            slots.upto(49)
            dve.wait_ge(sco_ready.sem, sco_ready.due(t, 4)).then_inc(passed.sem, 1)
            for h in range(16):
                last = dve.max(v16[:, h, 0:8], s12[:, h, :])
            link.hold(last, passed)
            slots.upto(50)
            for h in range(16):
                dve.max_index(i16[:, h, 0:8], v16[:, h, 0:8], s12[:, h, :])
            slots.upto(51)
            for h in range(16):
                last = dve.match_replace(big[:, h, :], v16[:, h, 0:8], s12[:, h, :], NEG)
            link.hold(last, passed)
            slots.upto(52)
            for h in range(16):
                last = dve.max(v16[:, h, 8:16], big[:, h, :])
            link.hold(last, passed)
            slots.upto(53)
            for h in range(16):
                last = dve.max_index(i16[:, h, 8:16], v16[:, h, 8:16], big[:, h, :])
            link(last)
            slots.upto(54)
            link(dve.tensor_copy(f16, i16))
            halves = lambda x: x.rearrange("p (h s) k -> p h s k", s=2)
            v, f = halves(v16), halves(f16)
            link(dve.tensor_scalar(f[:, :, 0, :], f[:, :, 0, :], 128.0, None, ALU.mult))
            for dst, src in ((cand, v), (cidx, f)):
                at = 0
                slots.upto(55 if dst is cand else 56)
                for a, n, w in CAND:
                    out = dst[:, :, at:at + n * w]
                    if n == 1:
                        last = dve.tensor_tensor(out, src[:, :, 1, 0:w],
                                                 src[:, :, 0, a:a + 1].to_broadcast([P, 8, w]), ALU.add)
                    elif w == 1:
                        last = dve.tensor_tensor(out, src[:, :, 0, a:a + n],
                                                 src[:, :, 1, 0:1].to_broadcast([P, 8, n]), ALU.add)
                    else:
                        last = dve.tensor_tensor(out.rearrange("p h (n m) -> p h n m", m=w),
                                                 src[:, :, 1, 0:w].unsqueeze(2).to_broadcast([P, 8, n, w]),
                                                 src[:, :, 0, a:a + n].unsqueeze(3).to_broadcast([P, 8, n, w]),
                                                 ALU.add)
                    at += n * w
            link.hold(last, passed)
            slots.upto(57)
            for h in range(8):
                last = dve.max(best[:, h, 0:8], cand[:, h, :])
            link.hold(last, passed)
            slots.upto(58)
            for h in range(8):
                dve.max_index(pos[:, h, 0:8], best[:, h, 0:8], cand[:, h, :])
            for h in range(8):
                last = dve.match_replace(candb[:, h, :], best[:, h, 0:8], cand[:, h, :], NEG)
            link.hold(last, passed)
            slots.upto(59)
            for h in range(8):
                last = dve.max(best[:, h, 8:16], candb[:, h, :])
            link.hold(last, passed)
            for h in range(8):
                last = dve.max_index(pos[:, h, 8:16], best[:, h, 8:16], candb[:, h, :])
            link(last)
            dve.tensor_tensor(gate[:, :, :], best[:, :, :], best[:, :, 0:1].to_broadcast([P, 8, TOPK]),
                              ALU.subtract).then_inc(smax_in.sem, 1)
            link(dve.tensor_copy(posf, pos))
            for h in range(8):
                slots.upto(60 + h)
                link(dve.tensor_tensor(hot, iota[:, :].unsqueeze(1).to_broadcast([P, TOPK, NCAND]),
                                       posf[:, h, :].unsqueeze(2).to_broadcast([P, TOPK, NCAND]), ALU.is_equal))
                link(dve.tensor_tensor(hot, hot, cidx[:, h, :].unsqueeze(1).to_broadcast([P, TOPK, NCAND]), ALU.mult))
                link(dve.tensor_reduce(expf[:, h, :], hot, AX.X, ALU.add))
            link(dve.tensor_copy(expert[:, :], expf.rearrange("p h k -> p (h k)")))
            dve.wait_ge(sexp.sem, sexp.due(t, 1))
            link(dve.tensor_reduce(gsum[:, 0, :], gate[:, :, :], AX.X, ALU.add))
            link(dve.reciprocal(gsum[:, 1, :], gsum[:, 0, :]))
            link(dve.tensor_tensor(gate[:, :, :], gate[:, :, :],
                                   gsum[:, 1, :].unsqueeze(2).to_broadcast([P, 8, TOPK]), ALU.mult))
            link.close()

        none = Experts()

        with ExitStack() as own:
            def sb1(name, shape):
                return own.enter_context(nc.sbuf_tensor("st_" + name, shape, F32))

            NK = SAMPLES + 1
            keyT_s = sb1("keyT", [P, NK * P])
            states = sb1("states", [P, SAMPLES, PAIRS, P])
            sc_s, prT_s = (sb1(n, [P, 2, 3 * P]) for n in ("scores", "probsT"))
            m = {
                "sample": True, "nk": NK, "width": 3 * P, "maps": SAMPLES, "applied": 4,
                "column": lambda n: 2 * (n % 4) + n // 4,
                "kv": sb1("kv", [P, NK, 256]), "amask": sb1("amask", [P, 3 * P]), "keyT": keyT_s[:, :],
                "sc": [sc_s[:, n, :] for n in range(2)], "prT": [prT_s[:, n, :] for n in range(2)],
                "bk_odd": sb1("bk_odd", [P, 2, RW]), "rpT_odd": sb1("rpT_odd", [P, PAIRS, P]),
                "rowm": sb1("rowm", [P, 2]), "colm": sb1("colm", [P, 2, P]), "S": lambda b: states[:, b, :, :],
                "kt_bank": 3, "sc_bank": [5, 2], "prT_bank": [3, 4], "o_bank": 1, "y_bank": 6,
            }
            block = own.enter_context(nc.Block())

            @block.sync
            def _(sp):
                sp.dma_start(m["rowm"][:, :], A["rowm"]).then_inc(consts.sem, 16)
                sp.dma_start(m["colm"][:, :, :], A["colm"]).then_inc(consts.sem, 16)
                mix_sync(sp, 0, m, SEQ)
                copies = ((A["shift_prompt"], proj[P + SEQ - 1:P + SEQ, 0:P_RWKV]),
                          (A["k_prompt"], proj[SEQ:P + SEQ, K0:V0]),
                          (A["v_prompt"], proj[SEQ:P + SEQ, V0:P_TOTAL]),
                          (A["shift_sample"], proj[P + SEQ + STEPS - 1:P + TOKENS:STEPS, 0:P_RWKV]),
                          (A["k_sample"][:, P - STEPS:, :], proj[P + SEQ:, K0:V0].rearrange("(b s) c -> b s c", s=STEPS)),
                          (A["v_sample"][:, P - STEPS:, :], proj[P + SEQ:, V0:].rearrange("(b s) c -> b s c", s=STEPS)),
                          (A["k_sample"][:, 0:P - STEPS, :], A["cache_k"][:, STEPS:, :]),
                          (A["v_sample"][:, 0:P - STEPS, :], A["cache_v"][:, STEPS:, :]))
                for dst, src in copies:
                    sp.dma_start(dst, src).then_inc(copied.sem, 16)
                sp.wait_ge(s_ready.sem, SAMPLES)
                for b in range(SAMPLES):
                    for o in range(2):
                        sp.dma_start(A["wkvT_sample"][b, o], m["S"](b)[o * HD:(o + 1) * HD, :, o * HD:(o + 1) * HD])\
                          .then_inc(s_stored.sem, 16)
                route_sync(sp, 0, SEQ)
                sp.wait_ge(s_stored.sem, 32 * SAMPLES)
                sp.wait_ge(copied.sem, 16 * len(copies))

            @block.scalar
            def _(act):
                mix_scalar(act, 0, m, none)
                route_scalar(act, 0, none)

            @block.vector
            def _(dve):
                dve.memset(loraT[32:64, 2 * P:], 1.0)
                dve.memset(loraT[64:P, 2 * P:], 1.0).then_inc(ones_ready.sem, 1)
                dve.memset(states[:, :, :, :], 0.0).then_inc(s_zeroed.sem, 1)
                dve.wait_ge(consts.sem, 32)
                mix_vector(dve, 0, m, none)
                route_vector(dve, 0, none)

            @block.tensor
            def _(pe):
                pe.wait_ge(ones_ready.sem, 1)
                mix_tensor(pe, 0, m, none)
                route_tensor(pe, 0, none)

        with ExitStack() as own:
            def sb2(name, shape, dt=F32):
                return own.enter_context(nc.sbuf_tensor("ex_" + name, shape, dt))

            two = lambda buf, at: [part(buf, at + n * 2 * P, (2 * P,)) for n in range(2)]
            m = {
                "sample": False, "nk": 2, "width": 2 * P, "maps": 4, "applied": 5,
                "column": lambda n: n, "S": lambda b: S[:, :, :],
                "kv": sb2("kv", [P, 2, 256]), "amask": sb2("amask", [P, 2 * P]), "keyT": part(work2, 0, (2 * P,)),
                "sc": two(k2, 0), "prT": two(sb2("probsT", [P, 4 * P]), 0),
                "kt_bank": 4, "sc_bank": [5, 2], "prT_bank": [3, 4], "o_bank": 1, "y_bank": 0,
            }
            x2c = sb2("x2c", [P, D])
            tnc = sb2("tnc", [P, D])
            y_out = sb2("y_out", [P, D])
            expert_c = sb2("expert_c", [P, SLOTS], U32)
            gate_c = sb2("gate_c", [P, SLOTS])
            coef = sb2("coef", [P, SLOTS])
            diag = sb2("diag", [P, DIAGS, P])
            down = sb2("down_rows", [P, DOWN_RING, D])
            up = sb2("up_rows", [P, UP_RING, D])

            def experts_gpsimd(pool, t):
                def gather(dst, table, s, arrived):
                    pool.indirect_dma_start(dst, None, table, bass.IndirectOffsetOnAxis(expert_c[:, s:s + 1], 0))\
                        .then_inc(arrived.sem, 16)

                pool.wait_ge(handed.sem, handed.due(t, 1)).then_inc(row_free.sem, 1)
                for s in range(SLOTS + UP_LAG):
                    if s == HALF:
                        pool.wait_ge(handed.sem, handed.due(t, 2)).then_inc(row_free.sem, 1)
                    if s < SLOTS:
                        old = s - DOWN_RING if s >= DOWN_RING else max(range(s, SLOTS, DOWN_RING)) - SLOTS
                        pool.wait_ge(dotted.sem, dotted.due(t, old + 1 + DOWN_RING)).then_inc(row_free.sem, 1)
                        gather(down[:, s % DOWN_RING, :], A["down"], s, down_in[s % DOWN_RING])
                    v = s - UP_LAG
                    if v >= 0:
                        old = v - UP_RING if v >= UP_RING else max(range(v, SLOTS, UP_RING))
                        used, on, credit = (dve_used, ON_VECTOR, 1) if old in ON_VECTOR else (pe_used, ON_PE, DIAGS)
                        count = on.index(old) + 1 + credit - (len(on) if v < UP_RING else 0)
                        assert count > 0
                        pool.wait_ge(used.sem, used.due(t, count)).then_inc(row_free.sem, 1)
                        gather(up[:, v % UP_RING, :], A["up"], v, up_in[v % UP_RING])

            def experts_scalar(act, t):
                def coefficients(slots):
                    for s in slots:
                        act.wait_ge(dotted.sem, dotted.due(t, s + 1 + DOWN_RING))
                        act.activation(coef[:, s:s + 1], coef[:, s:s + 1], ACT.Gelu).then_inc(gelued.sem, 1)
                    for s in slots:
                        act.wait_ge(gelued.sem, gelued.due(t, s + 1))
                        act.activation(coef[:, s:s + 1], coef[:, s:s + 1], ACT.Copy, scale=gate_c[:, s:s + 1])\
                           .then_inc(coefs.sem, 1)
                    for s in slots:
                        if s in ON_PE:
                            n = ON_PE.index(s)
                            act.wait_ge(coefs.sem, coefs.due(t, s + 1))
                            act.wait_ge(pe_used.sem, pe_used.due(t, n + 1))
                            act.activation(diag[:, n % DIAGS, :], ident[:, :], ACT.Copy, scale=coef[:, s:s + 1])\
                               .then_inc(diags.sem, 1)

                def last():
                    act.wait_ge(ssq2_ready.sem, ssq2_ready.due(t, 1))
                    act.activation(stat[:, 3:4], stat[:, 3:4], ACT.Sqrt).then_inc(std2_ready.sem, 1)
                    act.wait_ge(y_ready.sem, y_ready.due(t, 1))
                    act.dma_start(A["y"][bass.ds(t * P, P), :], y_out[:, :]).then_inc(y_stored.sem, 16)

                return Experts((coefficients, 1), last=last)

            def experts_tensor(pe, t):
                def add(slots):
                    for s in slots:
                        if s in ON_PE:
                            n, r = ON_PE.index(s), s % UP_RING
                            pe.wait_ge(up_in[r].sem, up_in[r].due(t, 16 * (s // UP_RING + 1)))
                            pe.wait_ge(diags.sem, diags.due(t, n + 1))
                            for c in range(2):
                                last = pe.matmul(bank(6 + c), diag[:, n % DIAGS, :], up[:, r, c * 512:(c + 1) * 512],
                                                 start=n == 0, stop=n == len(ON_PE) - 1)
                            last.then_inc(pe_used.sem, 1)

                return Experts((add, 2), last=lambda: None)

            def hand_over(dve, t, slots=None):
                dve.tensor_copy(expert_c[:, 0:HALF], expert[:, 0:HALF]).then_inc(handed.sem, 1)
                if slots:
                    slots.upto(MARKS)
                    for n in up_in:
                        dve.wait_ge(n.sem, n.due(t, 0))
                dve.tensor_copy(expert_c[:, HALF:], expert[:, HALF:]).then_inc(handed.sem, 1)

            def experts_vector(dve, t):
                dve.tensor_copy(gate_c[:, :], gate[:, :, :].rearrange("p h k -> p (h k)"))
                dve.tensor_copy(tnc[:, :], tn[:, :])
                dve.tensor_copy(x2c[:, :], x2[:, :]).then_inc(end_link.sem, 1)
                dve.wait_ge(end_link.sem, end_link.due(t, 1))

                def dots(slots):
                    for s in slots:
                        r = s % DOWN_RING
                        dve.wait_ge(down_in[r].sem, down_in[r].due(t, 16 * (s // DOWN_RING + 1)))
                        dve.tensor_tensor_reduce(out=down[:, r, :], in0=down[:, r, :], in1=tnc[:, :],
                                                 scale=1.0, scalar=0.0, op0=ALU.mult, op1=ALU.add,
                                                 accum_out=coef[:, s:s + 1]).then_inc(dotted.sem, 1)

                def add(slots):
                    for s in slots:
                        if s in ON_VECTOR:
                            n, r = ON_VECTOR.index(s), s % UP_RING
                            dve.wait_ge(up_in[r].sem, up_in[r].due(t, 16 * (s // UP_RING + 1)))
                            dve.wait_ge(coefs.sem, coefs.due(t, s + 1))
                            dve.wait_ge(dve_used.sem, dve_used.due(t, n + 1))
                            dve.scalar_tensor_tensor(out=x2c[:, :], in0=up[:, r, :], scalar=coef[:, s:s + 1],
                                                     in1=x2c[:, :], op0=ALU.mult, op1=ALU.add)\
                               .then_inc(dve_used.sem, 1)

                def last():
                    link = Link(dve, end_link, t)
                    link.n = 1
                    dve.wait_ge(dve_used.sem, dve_used.due(t, len(ON_VECTOR) + 1))
                    dve.wait_ge(pe_used.sem, pe_used.due(t, len(ON_PE) + DIAGS))
                    link(dve.tensor_tensor(x2c[:, :], x2c[:, :], banks(6, 2), ALU.add))
                    link(dve.tensor_tensor_reduce(out=tnc[:, :], in0=x2c[:, :], in1=x2c[:, :], scale=1.0, scalar=0.0,
                                                  op0=ALU.mult, op1=ALU.add, accum_out=stat[:, 2:3]))
                    dve.tensor_scalar(stat[:, 3:4], stat[:, 2:3], 1.0 / D, RMS_EPS, ALU.mult, ALU.add)\
                       .then_inc(ssq2_ready.sem, 1)
                    dve.wait_ge(std2_ready.sem, std2_ready.due(t, 1))
                    link(dve.reciprocal(stat[:, 3:4], stat[:, 3:4]))
                    dve.wait_ge(y_stored.sem, y_stored.due(t, 16))
                    link(dve.scalar_tensor_tensor(out=y_out[:, :], in0=x2c[:, :], scalar=stat[:, 3:4], in1=gain_f[:, :],
                                                  op0=ALU.mult, op1=ALU.mult))
                    dve.sem_inc(y_ready.sem, 1)
                    link.close()

                return Experts((dots, 0), (add, 2), last=last)

            block = own.enter_context(nc.Block())
            T = PROMPT_TILES

            @block.sync
            def _(sp):
                sp.sem_inc(y_stored.sem, 16)
                sp.dma_start(rc[:, :], A["rc"][0]).then_inc(late_consts.sem, 16)
                sp.wait_ge(late_consts.sem, 16)
                sp.sem_inc(tile_end.sem, 1)
                with sp.Fori(0, T) as t:
                    mix_sync(sp, t + 1, m, t * P)
                    route_sync(sp, t + 1, t * P)
                    sp.wait_ge(w_used.sem, w_used.due(t + 1, 24))
                    sp.sem_inc(tile_end.sem, 1)
                for o in range(2):
                    sp.dma_start(A["wkvT_prompt"][o], S[o * HD:(o + 1) * HD, :, o * HD:(o + 1) * HD])\
                      .then_inc(s_stored.sem, 16)
                sp.wait_ge(y_stored.sem, 16 * (T + 2))
                sp.wait_ge(s_stored.sem, 32 * (SAMPLES + 1))

            @block.gpsimd
            def _(pool):
                with pool.Fori(0, T + 1) as t:
                    experts_gpsimd(pool, t)

            @block.scalar
            def _(act):
                act.sem_inc(tile_end.sem, 1)
                with act.Fori(0, T) as t:
                    slots = experts_scalar(act, t)
                    mix_scalar(act, t + 1, m, slots)
                    route_scalar(act, t + 1, slots)
                    act.sem_inc(tile_end.sem, 1)
                    slots.finish()
                experts_scalar(act, T).finish()

            @block.vector
            def _(dve):
                dve.memset(S[:, :, :], 0.0)
                dve.sem_inc(dve_used.sem, 1)
                dve.sem_inc(dotted.sem, DOWN_RING)
                dve.sem_inc(tile_end.sem, 1)
                hand_over(dve, 0)
                with dve.Fori(0, T) as t:
                    slots = experts_vector(dve, t)
                    dve.wait_ge(tile_end.sem, tile_end.due(t + 1, 0))
                    mix_vector(dve, t + 1, m, slots)
                    route_vector(dve, t + 1, slots)
                    dve.sem_inc(tile_end.sem, 1)
                    hand_over(dve, t + 1, slots)
                    slots.finish()
                experts_vector(dve, T).finish()

            @block.tensor
            def _(pe):
                pe.sem_inc(pe_used.sem, DIAGS)
                pe.sem_inc(tile_end.sem, 1)
                with pe.Fori(0, T) as t:
                    slots = experts_tensor(pe, t)
                    mix_tensor(pe, t + 1, m, slots)
                    route_tensor(pe, t + 1, slots)
                    pe.wait_ge(sco_out.sem, sco_out.due(t + 1, 4))
                    pe.sem_inc(tile_end.sem, 1)
                    slots.finish()
                experts_tensor(pe, T).finish()



def build(nc, A):
    A["proj"] = nc.dram_tensor("proj_rows", (P + TOKENS, P_TOTAL), F32, kind="Internal").ap()
    with ExitStack() as ctx:
        C = constants(nc, ctx)
        project(nc, A, C)
        mix_and_route(nc, A, C)


def shape_constants():
    i = np.arange(P)
    tok, col = i[:, None], i[None, :]
    rc = np.zeros((2, P, RC_COLS), np.float32)
    decay = np.float32(-math.exp(-0.5))
    for v, c in enumerate((32, STEPS)):
        same = tok // c == col // c
        rc[v, :, TRI_I:TRI_I + P] = decay * (same & (tok <= col))
        rc[v, :, TRI_X:TRI_X + P] = decay * (same & (tok < col))
        rc[v, :, TRI_S:TRI_S + P] = decay * (same & (tok > col))
        rc[v, :, IND:IND + P // c] = decay * (tok // c == np.arange(P // c)[None, :])
        rc[v, :, MASK2:MASK2 + P] = same & (tok < col)
        rc[v, :, MASK2 + P:MASK2 + 2 * P] = same & (tok <= col)
        rc[v, :, MASKN:MASKN + P] = same & (tok > col)
    rowm = np.stack([(i // STEPS) % 2 == 0, (i // STEPS) % 2 == 1], 1).astype(np.float32)
    colm = np.broadcast_to(rowm.T[None], (P, 2, P)).astype(np.float32)
    key = np.arange(2 * P)[None, :] - P
    mp = np.zeros((PROMPT_TILES, P, 2 * P), np.float32)
    for t in range(PROMPT_TILES):
        qc, kc = (t * P + tok) // 64, (t * P + key) // 64
        mp[t] = np.where((kc >= qc - 2) & (kc <= qc) & (kc >= 0), 0, NEG)
    even = np.broadcast_to((tok // STEPS) % 2 == 0, (P, P))
    ms = np.where(np.concatenate([even, ~even, col // STEPS == tok // STEPS], 1), 0, NEG).astype(np.float32)
    return {
        "ident": np.eye(P, dtype=np.float32),
        "ident2": np.concatenate([np.eye(HD, dtype=np.float32)] * 2, 0),
        "rc": rc, "rowm": rowm, "colm": np.ascontiguousarray(colm),
        "mask_prompt": mp.reshape(-1, 2 * P), "mask_sample": ms,
        "iota": np.arange(NCAND, dtype=np.float32),
    }


OUTPUTS = {
    "y": (TOKENS, D), "shift_prompt": (1, P_RWKV), "wkvT_prompt": (2, HD, PAIRS, HD),
    "k_prompt": (P, 128), "v_prompt": (P, 128), "shift_sample": (SAMPLES, P_RWKV),
    "wkvT_sample": (SAMPLES, 2, HD, PAIRS, HD), "k_sample": (SAMPLES, P, 128), "v_sample": (SAMPLES, P, 128),
}


def kernel(**inputs):
    import concourse.bacc as bacc
    from concourse.bass_utils import run_bass_kernel_spmd

    a = {name: np.asarray(x) for name, x in inputs.items()}
    wkv = a["state_rwkv_wkv"][0].reshape(SAMPLES, PAIRS, 2, HD, HD)
    w_in = a["w_in"][0]
    w_q = w_in[:, Q0:K0].reshape(D, 2, 4, HD).transpose(0, 2, 1, 3).reshape(D, RW)
    w_in = np.concatenate([w_in[:, :Q0], w_q, w_in[:, K0:]], 1)
    arrays = {
        "x": np.concatenate([a["x_prompt"].reshape(-1, D), a["x_sample"].reshape(-1, D)], 0),
        "norm_mix_col": np.ascontiguousarray(a["norm_mix_g"][0].reshape(KC, P).T),
        "w_in": w_in, "w_out": a["w_out"][0], 
        "w_q": np.ascontiguousarray(a["peer_w_q"][0].reshape(KC, P, 16, P).transpose(2, 1, 0, 3)).reshape(16, P, D),
        "mu": a["rwkv_mu"][0], "w0": a["rwkv_w0"][0], "a0": a["rwkv_a0"][0],
        "w2": a["rwkv_w2"][0], "a2": a["rwkv_a2"][0], "g2": a["rwkv_g2"][0],
        "k_k": a["rwkv_k_k"][0], "k_a": a["rwkv_k_a"][0], "r_k": a["rwkv_r_k"][0].reshape(-1),
        "ln_w": a["rwkv_ln_w"][0], "ln_b": a["rwkv_ln_b"][0], "out_g": a["attn_out_g"][0],
        "sinks": a["attn_sinks"][0], "norm_ffn": a["norm_ffn_g"][0], "norm_final": a["norm_final_g"],
        "state_shift": a["state_rwkv_shift"][0].reshape(SAMPLES, P_RWKV),
        "state_wkvT": np.ascontiguousarray(wkv.transpose(0, 2, 4, 1, 3)),
        "cache_k": a["cache_swa_k"][0].reshape(SAMPLES, P, 128),
        "cache_v": a["cache_swa_v"][0].reshape(SAMPLES, P, 128),
        "key1T": np.ascontiguousarray(a["peer_key1"][0].T), "key2T": np.ascontiguousarray(a["peer_key2"][0].T),
        "down": a["peer_down"][0], "up": a["peer_up"][0],
    }
    arrays.update(shape_constants())
    nc = bacc.Bacc("TRN2", target_bir_lowering=False, num_devices=1)
    A = {name: nc.dram_tensor(name, x.shape, F32, kind="ExternalInput").ap() for name, x in arrays.items()}
    A.update({name: nc.dram_tensor(name, shape, F32, kind="ExternalOutput").ap() for name, shape in OUTPUTS.items()})
    build(nc, A)
    r = run_bass_kernel_spmd(nc, [arrays], core_ids=[0]).results[0]
    wkv_p = r["wkvT_prompt"].transpose(2, 0, 3, 1).reshape(1, 1, HEADS, HD, HD)
    wkv_s = r["wkvT_sample"].transpose(0, 3, 1, 4, 2).reshape(1, SAMPLES, HEADS, HD, HD)
    return (r["y"][P:].reshape(1, SEQ, D), r["y"][:P].reshape(SAMPLES, STEPS, D),
            r["shift_prompt"].reshape(1, 1, 1, P_RWKV), np.ascontiguousarray(wkv_p),
            r["k_prompt"].reshape(1, 1, P, 2, HD), r["v_prompt"].reshape(1, 1, P, 2, HD),
            r["shift_sample"].reshape(1, SAMPLES, 1, P_RWKV), np.ascontiguousarray(wkv_s),
            r["k_sample"].reshape(1, SAMPLES, P, 2, HD), r["v_sample"].reshape(1, SAMPLES, P, 2, HD))
```
